# Optimizing a Trainium2 kernel written in Bass

```python
import math
import jax, jax.numpy as jnp
from jax import lax
import numpy as np

D_MODEL = 1024
BATCH = 1
SEQ = 512
DEPTH = 1
DEC_BATCH = 8
DEC_SEQ = 16
PAST_LEN = 512

CHUNK = 64
Q_BLOCK = 128
GDN_HEADS = 4
GDN_DK = 128
GDN_DV = 128
CONV_W = 4
DIFF_HEADS = 4
DIFF_DK = 64
DIFF_DV = 128
ROT_DIM = DIFF_DK // 4
ROPE_THETA = 500000.0
D_FF = 2816
EPS = 1e-6

GDN_QK = GDN_HEADS * GDN_DK
GDN_V = GDN_HEADS * GDN_DV
CONV_CH = 2 * GDN_QK + GDN_V
DIFF_QK = DIFF_HEADS * 2 * DIFF_DK
DIFF_V = DIFF_HEADS * DIFF_DV
MIX_WIDTH = GDN_V + DIFF_V
IN_SPLITS = [CONV_CH,
             CONV_CH + GDN_HEADS,
             CONV_CH + 2 * GDN_HEADS,
             CONV_CH + 2 * GDN_HEADS + GDN_V,
             CONV_CH + 2 * GDN_HEADS + GDN_V + DIFF_QK,
             CONV_CH + 2 * GDN_HEADS + GDN_V + 2 * DIFF_QK]
IN_COLS = IN_SPLITS[-1] + DIFF_V

kernel_name = 'hymba_gdn_diffattn_macaron_stream_step'

def rms_norm(x, g):
    xf = x.astype(jnp.float32)
    y = xf * lax.rsqrt(jnp.mean(xf * xf, axis=-1, keepdims=True) + EPS)
    return (y * g.astype(jnp.float32)).astype(x.dtype)

def l2_norm(x):
    xf = x.astype(jnp.float32)
    return xf * lax.rsqrt(jnp.sum(xf * xf, axis=-1, keepdims=True) + EPS)

def swiglu(x, w_gu, w_down):
    gate, up = jnp.split(x @ w_gu, 2, axis=-1)
    return (jax.nn.silu(gate) * up) @ w_down

def causal_conv(x, hist, w):
    L = x.shape[1]
    xp = jnp.concatenate([hist.astype(x.dtype), x], axis=1)
    y = xp[:, 0:L] * w[0]
    for i in range(1, CONV_W):
        y = y + xp[:, i:i + L] * w[i]
    return jax.nn.silu(y), xp[:, -(CONV_W - 1):]

def rope_partial(x, pos):
    half = ROT_DIM // 2
    inv = jnp.float32(ROPE_THETA) ** (-jnp.arange(half, dtype=jnp.float32) * 2.0 / ROT_DIM)
    ang = pos.astype(jnp.float32)[:, None] * inv[None, :]
    cos = jnp.cos(ang)[None, :, None, None, :]
    sin = jnp.sin(ang)[None, :, None, None, :]
    xr = x[..., :ROT_DIM].astype(jnp.float32)
    x1, x2 = xr[..., :half], xr[..., half:]
    rot = jnp.concatenate([x1 * cos - x2 * sin, x2 * cos + x1 * sin], axis=-1).astype(x.dtype)
    return jnp.concatenate([rot, x[..., ROT_DIM:]], axis=-1)

def gated_delta_rule(q, k, v, g, beta, s0, chunk):
    B, L, H, DK = q.shape
    DV = v.shape[-1]
    n = L // chunk

    def blk(t):
        return jnp.moveaxis(t.reshape((B, n, chunk) + t.shape[2:]), 3, 2)

    qc, kc, vc, gc, bc = blk(q), blk(k), blk(v), blk(g), blk(beta)
    G = jnp.cumsum(gc, axis=-1)
    idx = jnp.arange(chunk)
    incl = idx[:, None] >= idx[None, :]
    strict = idx[:, None] > idx[None, :]
    dec = jnp.exp(jnp.where(incl, G[..., :, None] - G[..., None, :], -jnp.inf))
    kk = jnp.einsum('bnhck,bnhsk->bnhcs', kc, kc)
    A = jnp.where(strict, bc[..., None] * kk * dec, 0.0) + jnp.eye(chunk, dtype=jnp.float32)
    rhs = jnp.concatenate([vc * bc[..., None], kc * (bc * jnp.exp(G))[..., None]], axis=-1)
    sol = lax.linalg.triangular_solve(A, rhs, left_side=True, lower=True, unit_diagonal=True)
    u0, w = sol[..., :DV], sol[..., DV:]
    qk = jnp.einsum('bnhck,bnhsk->bnhcs', qc, kc) * dec
    q_dec = qc * jnp.exp(G)[..., None]
    k_dec = kc * jnp.exp(G[..., -1:] - G)[..., None]
    g_last = jnp.exp(G[..., -1])

    def step(S, inp):
        u0_i, w_i, qk_i, qd_i, kd_i, gl_i = inp
        u = u0_i - jnp.einsum('bhck,bhkv->bhcv', w_i, S)
        o = jnp.einsum('bhck,bhkv->bhcv', qd_i, S) + jnp.einsum('bhcs,bhsv->bhcv', qk_i, u)
        S = S * gl_i[..., None, None] + jnp.einsum('bhck,bhcv->bhkv', kd_i, u)
        return S, o

    xs = (jnp.moveaxis(u0, 1, 0), jnp.moveaxis(w, 1, 0), jnp.moveaxis(qk, 1, 0),
          jnp.moveaxis(q_dec, 1, 0), jnp.moveaxis(k_dec, 1, 0), jnp.moveaxis(g_last, 1, 0))
    S, o = lax.scan(step, s0, xs)
    o = jnp.moveaxis(jnp.moveaxis(o, 0, 1), 3, 2).reshape(B, L, H, DV)
    return o, S

def gated_deltanet(conv_in, b_raw, a_raw, z, conv_hist, s0, conv_w, a_log, dt_bias, out_norm):
    B, L, _ = conv_in.shape
    c, new_hist = causal_conv(conv_in, conv_hist, conv_w)
    q, k, v = jnp.split(c, [GDN_QK, 2 * GDN_QK], axis=-1)
    q = l2_norm(q.reshape(B, L, GDN_HEADS, GDN_DK)) * (GDN_DK ** -0.5)
    k = l2_norm(k.reshape(B, L, GDN_HEADS, GDN_DK))
    v = v.reshape(B, L, GDN_HEADS, GDN_DV).astype(jnp.float32)
    beta = jax.nn.sigmoid(b_raw.astype(jnp.float32))
    g = -jnp.exp(a_log.astype(jnp.float32)) * jax.nn.softplus(a_raw.astype(jnp.float32) + dt_bias.astype(jnp.float32))
    o, S = gated_delta_rule(q, k, v, g, beta, s0.astype(jnp.float32), min(CHUNK, L))
    o = rms_norm(o, out_norm) * jax.nn.silu(z.reshape(B, L, GDN_HEADS, GDN_DV).astype(jnp.float32))
    return o.reshape(B, L, GDN_V).astype(conv_in.dtype), S.astype(s0.dtype), new_hist

def diff_attention(q, k, v, mask, lam):
    s = jnp.einsum('bqhmd,bshmd->bhmqs', q, k, preferred_element_type=jnp.float32) * (DIFF_DK ** -0.5)
    if mask is not None:
        s = jnp.where(mask, s, -jnp.inf)
    p = jax.nn.softmax(s, axis=-1)
    p = p[:, :, 0] - lam * p[:, :, 1]
    return jnp.einsum('bhqs,bshv->bqhv', p.astype(v.dtype), v)

def diff_attention_prompt(q, k, v, lam):
    B, L = q.shape[:2]
    nb = L // Q_BLOCK
    qb = jnp.moveaxis(q.reshape(B, nb, Q_BLOCK, DIFF_HEADS, 2, DIFF_DK), 1, 0)
    k_chunk = jnp.arange(L) // CHUNK

    def one(args):
        qi, b = args
        q_chunk = (b * Q_BLOCK + jnp.arange(Q_BLOCK)) // CHUNK
        mask = k_chunk[None, :] <= q_chunk[:, None]
        return diff_attention(qi, k, v, mask, lam)

    o = lax.map(one, (qb, jnp.arange(nb)))
    return jnp.moveaxis(o, 0, 1).reshape(B, L, DIFF_HEADS, DIFF_DV)

def encoder_layer(x, pos, k_hist, v_hist, conv_hist, s0, p, lam_init):
    B, L, _ = x.shape
    x = x + 0.5 * swiglu(rms_norm(x, p['ffn1_norm']), p['ffn1_w_gu'], p['ffn1_w_down'])
    h = rms_norm(x, p['mix_norm'])
    proj = h @ p['w_in']
    conv_in, b_raw, a_raw, z, dq, dk, dv = jnp.split(proj, IN_SPLITS, axis=-1)
    if conv_hist is None:
        conv_hist = jnp.zeros((B, CONV_W - 1, CONV_CH), proj.dtype)
        s0 = jnp.zeros((B, GDN_HEADS, GDN_DK, GDN_DV), x.dtype)
    o_gdn, s_new, conv_new = gated_deltanet(conv_in, b_raw, a_raw, z, conv_hist, s0, p['conv_w'],
                                            p['a_log'], p['dt_bias'], p['gdn_out_norm'])
    q = rope_partial(rms_norm(dq.reshape(B, L, DIFF_HEADS, 2, DIFF_DK), p['q_norm']), pos)
    k = rope_partial(rms_norm(dk.reshape(B, L, DIFF_HEADS, 2, DIFF_DK), p['k_norm']), pos)
    v = dv.reshape(B, L, DIFF_HEADS, DIFF_DV)
    lam_e = jnp.exp(jnp.sum(p['lambda_q'].astype(jnp.float32) * p['lambda_k'].astype(jnp.float32), axis=-1))
    lam = lam_e[0] - lam_e[1] + lam_init
    if k_hist is None:
        o_diff = diff_attention_prompt(q, k, v, lam)
    else:
        k_all = jnp.concatenate([k_hist.astype(k.dtype), k], axis=1)
        v_all = jnp.concatenate([v_hist.astype(v.dtype), v], axis=1)
        o_diff = diff_attention(q, k_all, v_all, None, lam)
    o_diff = rms_norm(o_diff, p['diff_out_norm']) * (1.0 - lam_init)
    mixed = jnp.concatenate([o_gdn, o_diff.reshape(B, L, DIFF_V).astype(o_gdn.dtype)], axis=-1)
    x = x + mixed @ p['w_out']
    x = x + 0.5 * swiglu(rms_norm(x, p['ffn2_norm']), p['ffn2_w_gu'], p['ffn2_w_down'])
    return x, k, v, s_new, conv_new

def setup_inputs(seed: int = 0) -> dict:
    key = jax.random.key(seed)
    ks = jax.random.split(key, 32)
    nrm = lambda i, shape, s: jax.random.normal(ks[i], shape, jnp.float32) * s
    dt = jnp.exp(jax.random.uniform(ks[9], (DEPTH, GDN_HEADS), jnp.float32, math.log(1e-3), math.log(1e-1)))
    return {
        'x_prompt': nrm(0, (BATCH, SEQ, D_MODEL), 1.0),
        'x_sample': nrm(1, (DEC_BATCH, DEC_SEQ, D_MODEL), 1.0),
        'cache_k': nrm(2, (DEPTH, DEC_BATCH, PAST_LEN, DIFF_HEADS, 2, DIFF_DK), 1.0),
        'cache_v': nrm(3, (DEPTH, DEC_BATCH, PAST_LEN, DIFF_HEADS, DIFF_DV), 1.0),
        'state_gdn': nrm(4, (DEPTH, DEC_BATCH, GDN_HEADS, GDN_DK, GDN_DV), 1.0),
        'state_conv': nrm(5, (DEPTH, DEC_BATCH, CONV_W - 1, CONV_CH), 1.0),
        'ffn1_norm': 1.0 + nrm(6, (DEPTH, D_MODEL), 0.02),
        'ffn1_w_gu': nrm(7, (DEPTH, D_MODEL, 2 * D_FF), D_MODEL ** -0.5),
        'ffn1_w_down': nrm(8, (DEPTH, D_FF, D_MODEL), D_FF ** -0.5),
        'mix_norm': 1.0 + nrm(10, (DEPTH, D_MODEL), 0.02),
        'w_in': nrm(11, (DEPTH, D_MODEL, IN_COLS), D_MODEL ** -0.5),
        'conv_w': nrm(12, (DEPTH, CONV_W, CONV_CH), CONV_W ** -0.5),
        'a_log': jnp.log(jax.random.uniform(ks[13], (DEPTH, GDN_HEADS), jnp.float32, 1.0, 16.0)),
        'dt_bias': dt + jnp.log(-jnp.expm1(-dt)),
        'gdn_out_norm': 1.0 + nrm(14, (DEPTH, GDN_DV), 0.02),
        'q_norm': 1.0 + nrm(15, (DEPTH, DIFF_DK), 0.02),
        'k_norm': 1.0 + nrm(16, (DEPTH, DIFF_DK), 0.02),
        'lambda_q': nrm(17, (DEPTH, 2, DIFF_DK), 0.1),
        'lambda_k': nrm(18, (DEPTH, 2, DIFF_DK), 0.1),
        'diff_out_norm': 1.0 + nrm(19, (DEPTH, DIFF_DV), 0.02),
        'w_out': nrm(20, (DEPTH, MIX_WIDTH, D_MODEL), MIX_WIDTH ** -0.5),
        'ffn2_norm': 1.0 + nrm(21, (DEPTH, D_MODEL), 0.02),
        'ffn2_w_gu': nrm(22, (DEPTH, D_MODEL, 2 * D_FF), D_MODEL ** -0.5),
        'ffn2_w_down': nrm(23, (DEPTH, D_FF, D_MODEL), D_FF ** -0.5),
    }

def reference(x_prompt, x_sample, cache_k, cache_v, state_gdn, state_conv,
              ffn1_norm, ffn1_w_gu, ffn1_w_down, mix_norm, w_in, conv_w, a_log, dt_bias,
              gdn_out_norm, q_norm, k_norm, lambda_q, lambda_k, diff_out_norm, w_out,
              ffn2_norm, ffn2_w_gu, ffn2_w_down):
    pos_p = jnp.arange(x_prompt.shape[1])
    pos_s = cache_k.shape[2] + jnp.arange(x_sample.shape[1])
    hp, hs = x_prompt, x_sample
    kp_l, vp_l, sp_l, cp_l, ks_l, vs_l, ss_l, cs_l = [], [], [], [], [], [], [], []
    for l in range(DEPTH):
        lam_init = 0.8 - 0.6 * math.exp(-0.3 * l)
        p = dict(ffn1_norm=ffn1_norm[l], ffn1_w_gu=ffn1_w_gu[l], ffn1_w_down=ffn1_w_down[l],
                 mix_norm=mix_norm[l], w_in=w_in[l], conv_w=conv_w[l], a_log=a_log[l],
                 dt_bias=dt_bias[l], gdn_out_norm=gdn_out_norm[l], q_norm=q_norm[l], k_norm=k_norm[l],
                 lambda_q=lambda_q[l], lambda_k=lambda_k[l], diff_out_norm=diff_out_norm[l],
                 w_out=w_out[l], ffn2_norm=ffn2_norm[l], ffn2_w_gu=ffn2_w_gu[l], ffn2_w_down=ffn2_w_down[l])
        hp, kp, vp, sp, cp = encoder_layer(hp, pos_p, None, None, None, None, p, lam_init)
        hs, ks_, vs_, ss_, cs_ = encoder_layer(hs, pos_s, cache_k[l], cache_v[l], state_conv[l], state_gdn[l], p, lam_init)
        kp_l.append(kp); vp_l.append(vp); sp_l.append(sp); cp_l.append(cp)
        ks_l.append(ks_); vs_l.append(vs_); ss_l.append(ss_); cs_l.append(cs_)
    return (hp, hs,
            jnp.stack(kp_l), jnp.stack(vp_l), jnp.stack(sp_l), jnp.stack(cp_l),
            jnp.stack(ks_l), jnp.stack(vs_l), jnp.stack(ss_l), jnp.stack(cs_l))


_drawn_inputs = setup_inputs


def setup_inputs(seed=0):
    import zlib

    import numpy as np

    out = dict(_drawn_inputs(seed))
    spreads = {}
    factors = {'ffn1_norm': 4.52,
     'gdn_out_norm': 8.0,
     'q_norm': 6.048,
     'lambda_q': 2.824,
     'lambda_k': 3.833,
     'diff_out_norm': 6.214,
     'ffn2_norm': 8.0}
    for name, (base, spread) in spreads.items():
        noise = np.random.default_rng([zlib.crc32(name.encode()), seed]).standard_normal(out[name].shape)
        drawn = base * np.exp(spread * noise) if base else spread * noise
        out[name] = __import__('jax').numpy.asarray(drawn.astype(out[name].dtype))
    for name, factor in factors.items():
        out[name] = (out[name] * factor).astype(out[name].dtype)
    return out
```

```python
import math
from contextlib import ExitStack

import numpy as np

import concourse.bass as bass
from concourse import mybir

F32 = mybir.dt.float32
F32R = mybir.dt.float32r
ALU = mybir.AluOpType
ACT = mybir.ActivationFunctionType
AX = mybir.AxisListType

P = 128
D = 1024
KT = D // P
PROMPT = 512
STREAMS, STEP = 8, 16
TOK = PROMPT + STREAMS * STEP
TT = TOK // P
FF = 2816
FT = FF // P
HALF = TOK // 2
EPS = 1e-6
BANK = 512

ARENA = 16640
ARENA_END = 229368


IN_COLS = 3592
HEADS = 4
DK = 64
MAPS = 2
CONV_T = 12
BA_COL, Z_COL = 1536, 1544
PAST = 512
LAM_INIT = 0.8 - 0.6 * math.exp(0.0)
NEG = -1e30
LEVELS = [1, 2, 4, 8, 16, 32, 64]


def const_layout():
    widths = [("ident", P), ("ones", P), ("cum_p", P), ("cum_s", P), ("blk_s", P)]
    widths += [(f"lvl{n}", P) for n in LEVELS]
    widths += [("sel0", P), ("sel1", P), ("rowmask", STREAMS), ("map0", 1), ("map1", 1), ("early_neg", P)]
    at, out = 0, {}
    for name, w in widths:
        out[name] = (at, w)
        at += w
    return out, at


CONST, CONST_COLS = const_layout()


def constants():
    c = np.zeros((P, CONST_COLS), np.float32)

    def put(name, a):
        at, w = CONST[name]
        c[:, at:at + w] = a

    i = np.arange(P)
    row, col = i[:, None], i[None, :]
    put("ident", row == col)
    put("ones", 1.0)
    same = row // STEP == col // STEP
    put("cum_p", row <= col)
    put("cum_s", (row <= col) & same)
    put("blk_s", same)
    for n in LEVELS:
        put(f"lvl{n}", (row // (2 * n) == col // (2 * n)) & (row // n % 2 == 0) & (col // n % 2 == 1))
    h, m, q = row // 32, row % 32 // STEP, row % STEP
    for par in range(2):
        put(f"sel{par}", col == 32 * h + STEP * par + q)
    put("rowmask", row // STEP == np.arange(STREAMS)[None, :])
    put("map0", m == 0)
    put("map1", -(m == 1).astype(np.float32))
    pos = np.concatenate([np.arange(PROMPT), PAST + np.arange(STREAMS * STEP) % STEP]).astype(np.float32)
    inv = np.float32(500000.0) ** (-np.arange(8, dtype=np.float32) * np.float32(2.0) / np.float32(16.0))
    ang = (pos[:, None] * inv[None, :]).astype(np.float32).reshape(TT, P, 8).transpose(1, 0, 2)
    put("early_neg", np.where(col < 64, NEG, 0.0))
    return c, np.concatenate([np.cos(ang).reshape(P, -1), np.sin(ang).reshape(P, -1)], 1)


class Region:

    def __init__(self, nc, start, end):
        self.nc, self.at, self.end = nc, start, end

    def put(self, name, shape, dtype=F32):
        size = 4 * int(np.prod(shape[1:]))
        size = (size + 31) // 32 * 32
        assert self.at + size <= self.end, (name, self.at + size - self.end)
        t = self.nc.alloc_sbuf_tensor_at(name, shape, dtype, offset=self.at)
        self.at += size
        return t


def raw(t):
    return t.bitcast(F32)


def build(nc, io):
    ctx = ExitStack()
    sem = lambda name: ctx.enter_context(nc.semaphore(name))
    with ctx:
        keep = Region(nc, ARENA, ARENA_END)
        x_tok = keep.put("x_tok", [P, TT, D])
        h_at = keep.at
        hT_hi = keep.put("hT_hi", [P, KT, TOK], F32R)
        hT_lo = keep.put("hT_lo", [P, KT, TOK], F32R)
        h_end = keep.at
        gain_at = keep.at
        gain = keep.put("gain", [P, D])
        x_norm = keep.put("x_norm", [P, 2, D])
        sq_junk = keep.put("sq_junk", [P, D])
        scratch_end = keep.at
        stats = keep.put("stats", [P, 4, TT])
        consts = keep.put("consts", [P, CONST_COLS])

        def const(name):
            at, w = CONST[name]
            return consts[:, at:at + w]

        ident = const("ident")
        F0 = keep.at

        ffn_mem = Region(nc, F0, ARENA_END)
        aT = ffn_mem.put("aT", [P, FT, TOK])
        ring_at = ffn_mem.at
        raw_gu = ffn_mem.put("raw_gu", [P, 2, 2, KT, P])
        gu_hi = ffn_mem.put("gu_hi", [P, 2, 2, KT, P], F32R)
        gu_lo = ffn_mem.put("gu_lo", [P, 2, 2, KT, P], F32R)
        silu_gate = ffn_mem.put("silu_gate", [P, 2, TOK])
        ring_end = ffn_mem.at
        CH = [(0, 2), (2, 6), (6, 14), (14, 22)]
        wd = [[None] * 4, [None] * 4]
        wd[0][0] = ffn_mem.put("wd00", [P, 2, BANK])
        wd[0][1] = ffn_mem.put("wd01", [P, 4, BANK])
        over_h = Region(nc, h_at, h_end)
        wd[0][2] = over_h.put("wd02", [P, 8, BANK])
        wd[0][3] = over_h.put("wd03", [P, 8, BANK])
        wd[1][1] = over_h.put("wd11", [P, 4, BANK])
        over_ring = Region(nc, ring_at, ring_end)
        wd[1][2] = over_ring.put("wd12", [P, 8, BANK])
        wd[1][3] = over_ring.put("wd13", [P, 8, BANK])
        a_hi = over_ring.put("a_hi", [P, 2, TOK], F32R)
        a_lo = over_ring.put("a_lo", [P, 2, TOK], F32R)
        wd_hi = over_ring.put("wd_hi", [P, 2, BANK], F32R)
        wd_lo = over_ring.put("wd_lo", [P, 2, BANK], F32R)
        wd[1][0] = nc.alloc_sbuf_tensor_at("wd10", [P, 2, BANK], F32, offset=over_ring.at) \
            if over_ring.at + 4096 <= ring_end else x_norm[:, 0, :].rearrange("p (a b) -> p a b", a=2)

        psum_all = ctx.enter_context(nc.psum_tensor("psum_all", [P, 8, BANK], F32))
        psum = [psum_all[:, i, :] for i in range(8)]

        s_const = sem("const_loaded")
        s_x = sem("x_loaded")
        s_gain = [sem(f"gain_loaded{i}") for i in range(3)]
        s_y = sem("y_stored")

        class Count:

            def __init__(self, of, base):
                self.sem, self.base = of, base

            def __call__(self, n):
                return self.sem, self.base + n

        norm_sems = {n: sem(f"norm_{w}") for n, w in dict(
            sq="mean_square",
            var="inverse",
            rstd="root",
            xn="scaled",
            tr="transposed",
            hi="hi",
            lo="lo").items()}
        NORM_STEPS = dict(sq=TT, var=2, rstd=1, xn=TT, tr=2 * TT, hi=2 * TT, lo=2 * TT)

        class Norm:

            def __init__(self, r):
                rounds = r - (r == 3)
                self.sq, self.var, self.rstd, self.xn = (
                    Count(norm_sems[n], NORM_STEPS[n] * rounds) for n in ("sq", "var", "rstd", "xn"))
                self.tr, self.hi, self.lo = (
                    Count(norm_sems[n], NORM_STEPS[n] * r) for n in ("tr", "hi", "lo"))

        ffn_sems = {n: sem(f"ffn_{w}") for n, w in dict(
            hi="gate_up_hi", lo="gate_up_lo",
            mm="gate_up_product",
            silu="silu",
            a="hidden",
            dhi="down_hi", dlo="down_lo",
            dmm="down_step",
            out="down_product",
            res="residual").items()}
        FFN_STEPS = dict(hi=2 * FT, lo=2 * FT, mm=2 * FT, silu=2 * FT, a=2 * FT, dhi=4 * FT,
                         dlo=4 * FT, dmm=2 * (FT - 1), out=2 * TT, res=2 * TT)
        gu_loaded = [sem(f"ffn_gate_up_loaded{i}") for i in range(2)]
        down_loaded = [[sem(f"ffn_down_loaded{h}{c}") for c in range(4)] for h in range(2)]

        class Ffn:

            def __init__(self, r, norm):
                self.n = norm
                self.w = [Count(q, 16 * FT * r) for q in gu_loaded]
                self.wd = [[Count(q, 16 * r) for q in qs] for qs in down_loaded]
                (self.hi, self.lo, self.mm, self.silu, self.a, self.dhi, self.dlo, self.dmm,
                 self.out, self.res) = (Count(ffn_sems[n], FFN_STEPS[n] * r) for n in
                                        "hi lo mm silu a dhi dlo dmm out res".split())

        f1, f2 = Ffn(0, Norm(0)), Ffn(1, Norm(3))

        def norm_act(act, s, x_ready):
            for t in range(TT):
                x_ready(act, t)
                if t:
                    act.wait_ge(*s.sq(t))
                nc.scalar.activation(sq_junk[:], x_tok[:, t, :], ACT.Square,
                                     accum_out=stats[:, 0, t:t + 1]).then_inc(s.sq.sem, 1)
            act.wait_ge(*s.var(2))
            nc.scalar.activation(stats[:, 2, :], stats[:, 1, :], ACT.Sqrt).then_inc(s.rstd.sem, 1)
            split_act(act, s)

        def split_act(act, s):
            for n in range(2 * TT):
                t, half = n // 2, n % 2
                act.wait_ge(*s.tr(n + 1))
                nc.scalar.activation(
                    hT_hi[:, 4 * half:4 * half + 4, t * P:(t + 1) * P],
                    psum[n % 4].rearrange("p (k c) -> p k c", k=4), ACT.Copy).then_inc(s.hi.sem, 1)

        def norm_dve(dve, s):
            dve.wait_ge(*s.sq(TT))
            nc.vector.tensor_scalar(stats[:, 3, :], stats[:, 0, :], 1.0 / D, EPS, ALU.mult,
                                    ALU.add).then_inc(s.var.sem, 1)
            dve.wait_ge(*s.var(1))
            nc.vector.reciprocal(stats[:, 1, :], stats[:, 3, :]).then_inc(s.var.sem, 1)
            dve.wait_ge(*s.rstd(1))

            def scale(t):
                if t >= 2:
                    dve.wait_ge(*s.tr(2 * (t - 1)))
                nc.vector.scalar_tensor_tensor(x_norm[:, t % 2, :], x_tok[:, t, :],
                                               stats[:, 2, t:t + 1], gain[:], ALU.mult,
                                               ALU.mult).then_inc(s.xn.sem, 1)

            scale(0)
            for t in range(TT):
                if t + 1 < TT:
                    scale(t + 1)
                split_dve(dve, s, t)

        def split_dve(dve, s, t):
            if True:
                for half in range(2):
                    n = 2 * t + half
                    dve.wait_ge(*s.hi(n + 1))
                    cols = (slice(None), slice(4 * half, 4 * half + 4), slice(t * P, (t + 1) * P))
                    nc.vector.tensor_tensor(
                        hT_lo[cols], psum[n % 4].rearrange("p (k c) -> p k c", k=4),
                        raw(hT_hi[cols]), ALU.subtract).then_inc(s.lo.sem, 1)

        def norm_pe(pe, s, src=lambda t, c: x_norm[:, t % 2, c:c + P], ready=None):
            for n in range(2 * TT):
                t, half = n // 2, n % 2
                if ready is not None:
                    ready(pe, t, half)
                elif half == 0:
                    pe.wait_ge(*s.xn(t + 1))
                if n >= 4:
                    pe.wait_ge(*s.lo(n - 3))
                for k in range(4):
                    c = (4 * half + k) * P
                    last = nc.tensor.transpose(psum[n % 4][:, k * P:(k + 1) * P],
                                               src(t, c), ident)
                last.then_inc(s.tr.sem, 1)

        def bank_pair(which, slot):
            b = 4 * slot + 2 * which
            return psum[b], psum[b + 1]

        def ffn_sync(sp, s, w_gu, w_down, before=None):
            gu = w_gu.rearrange("(k p) c -> p k c", p=P)
            if before is not None:
                sp.wait_ge(before, 2 * TT)

            def load(j, slot):
                for which in range(2):
                    sp.dma_start(raw_gu[:, slot, which],
                                 gu[:, :, bass.ds(which * FF + j * P, P)]).then_inc(s.w[slot].sem, 16)

            load(0, 0)
            load(1, 1)
            dn = w_down.rearrange("(k p) c -> p k c", p=P)

            def load_down(half, c):
                a, b = CH[c]
                sp.dma_start(wd[half][c][:, :, :], dn[:, a:b, half * BANK:(half + 1) * BANK])\
                    .then_inc(s.wd[half][c].sem, 16)

            with sp.Fori(1, FT // 2) as pair:
                j = 2 * pair
                for slot in range(2):
                    sp.wait_ge(*s.lo(2 * (j + slot) - 2))
                    load(j + slot, slot)
            load_down(0, 0)
            load_down(0, 1)
            sp.wait_ge(*s.mm(2 * FT))
            load_down(0, 2)
            load_down(0, 3)
            load_down(1, 0)
            load_down(1, 1)
            load_down(1, 2)
            load_down(1, 3)

        def ffn_act(act, s):
            def split(j, slot):
                if slot == 0:
                    pass
                act.wait_ge(*s.w[slot](16 * (j - slot) + 32))
                for which in range(2):
                    nc.scalar.activation(gu_hi[:, slot, which], raw_gu[:, slot, which],
                                         ACT.Copy).then_inc(s.hi.sem, 1)

            def silu(j, slot):
                for n in range(1):
                    g = bank_pair(0, slot)
                act.wait_ge(*s.mm(2 * j + 1))
                for part in range(2):
                    nc.scalar.activation(silu_gate[:, slot, part * HALF:(part + 1) * HALF],
                                         g[part][:, 0:HALF], ACT.Silu).then_inc(s.silu.sem, 1)

            split(0, 0)
            split(1, 1)
            silu(0, 0)
            with act.Fori(1, FT // 2) as pair:
                j = 2 * pair
                act.wait_ge(*s.mm(2 * j - 2))
                split(j, 0)
                act.wait_ge(*s.a(2 * j - 2))
                silu(j - 1, 1)
                act.wait_ge(*s.mm(2 * j))
                split(j + 1, 1)
                act.wait_ge(*s.a(2 * j - 2))
                silu(j, 0)
            act.wait_ge(*s.a(2 * (FT - 2)))
            silu(FT - 1, 1)

            def down_split(half, c, j, slot):
                a, _ = CH[c]
                nc.scalar.activation(a_hi[:, slot, :], aT[:, j, :], ACT.Copy).then_inc(s.dhi.sem, 1)
                nc.scalar.activation(wd_hi[:, slot, :], wd[half][c][:, j - a, :], ACT.Copy)\
                    .then_inc(s.dhi.sem, 1)

            for half in range(2):
                for c, (a, b) in enumerate(CH):
                    act.wait_ge(*s.wd[half][c](16))
                    if c == 0:
                        for slot in range(2):
                            if half == 0:
                                act.wait_ge(*s.mm(2 * FT))
                                act.wait_ge(*s.a(2 * FT))
                            elif slot == 0:
                                act.wait_ge(*s.dmm(FT - 1))
                            else:
                                act.wait_ge(*s.out(TT))
                            down_split(half, 0, slot, slot)
                        continue
                    with act.Fori(a // 2, b // 2) as pair:
                        j = 2 * pair
                        for slot in range(2):
                            act.wait_ge(*s.dmm(half * (FT - 1) + j + slot - 1))
                            down_split(half, c, j + slot, slot)

        def ffn_dve(dve, s):
            def split(j, slot):
                for which in range(2):
                    dve.wait_ge(*s.hi(2 * j + which + 1))
                    nc.vector.tensor_tensor(gu_lo[:, slot, which], raw_gu[:, slot, which],
                                            raw(gu_hi[:, slot, which]), ALU.subtract)\
                        .then_inc(s.lo.sem, 1)

            def hidden(j, slot):
                dve.wait_ge(*s.mm(2 * j + 2))
                u = bank_pair(1, slot)
                for part in range(2):
                    dve.wait_ge(*s.silu(2 * j + part + 1))
                    nc.vector.tensor_tensor(aT[:, j, part * HALF:(part + 1) * HALF],
                                            silu_gate[:, slot, part * HALF:(part + 1) * HALF],
                                            u[part][:, 0:HALF], ALU.mult).then_inc(s.a.sem, 1)

            split(0, 0)
            split(1, 1)
            hidden(0, 0)
            with dve.Fori(1, FT // 2) as pair:
                j = 2 * pair
                split(j, 0)
                hidden(j - 1, 1)
                split(j + 1, 1)
                hidden(j, 0)
            hidden(FT - 1, 1)

            def down_split(half, c, j, slot):
                a, _ = CH[c]
                n = 2 * (half * FT + j)
                dve.wait_ge(*s.dhi(n + 1))
                nc.vector.tensor_tensor(a_lo[:, slot, :], aT[:, j, :], raw(a_hi[:, slot, :]),
                                        ALU.subtract).then_inc(s.dlo.sem, 1)
                dve.wait_ge(*s.dhi(n + 2))
                nc.vector.tensor_tensor(wd_lo[:, slot, :], wd[half][c][:, j - a, :],
                                        raw(wd_hi[:, slot, :]), ALU.subtract).then_inc(s.dlo.sem, 1)

            for half in range(2):
                for c, (a, b) in enumerate(CH):
                    with dve.Fori(a // 2, b // 2) as pair:
                        j = 2 * pair
                        for slot in range(2):
                            down_split(half, c, j + slot, slot)
                    if half == 1 and c == 0:
                        for t in range(TT):
                            residual(dve, s, 0, t)
            for t in range(TT):
                residual(dve, s, 1, t)

        def residual(dve, s, half, t):
            dve.wait_ge(*s.out(half * TT + t + 1))
            cols = x_tok[:, t, half * BANK:(half + 1) * BANK]
            nc.vector.scalar_tensor_tensor(cols, psum[(half * TT + t) % 8], 0.5, cols,
                                           ALU.mult, ALU.add).then_inc(s.res.sem, 1)

        def three(out, lhs_hi, lhs_lo, rhs_hi, rhs_lo, start, stop):
            nc.tensor.matmul(out, lhs_hi, rhs_hi, start=start, stop=False, skip_group_check=True)
            nc.tensor.matmul(out, lhs_hi, rhs_lo, start=False, stop=False, skip_group_check=True)
            return nc.tensor.matmul(out, lhs_lo, rhs_hi, start=False, stop=stop,
                                    skip_group_check=True)

        def ffn_pe(pe, s):
            def gate_up(j, slot):
                for which in range(2):
                    for k in range(KT):
                        for part in range(2):
                            tok = slice(part * HALF, (part + 1) * HALF)
                            last = three(bank_pair(which, slot)[part][:, 0:HALF],
                                         gu_hi[:, slot, which, k, :], gu_lo[:, slot, which, k, :],
                                         hT_hi[:, k, tok], hT_lo[:, k, tok], k == 0, k == KT - 1)
                    last.then_inc(s.mm.sem, 1)

            pe.wait_ge(*s.n.lo(2 * TT))
            for slot in range(2):
                pe.wait_ge(*s.lo(2 * slot + 2))
                gate_up(slot, slot)
            with pe.Fori(1, FT // 2) as pair:
                j = 2 * pair
                for slot in range(2):
                    pe.wait_ge(*s.lo(2 * (j + slot) + 2))
                    pe.wait_ge(*s.a(2 * (j + slot) - 2))
                    gate_up(j + slot, slot)

            def down(half, j, slot, start, stop):
                pe.wait_ge(*s.dlo(2 * (half * FT + j) + 2))
                for t in range(TT):
                    if start and half == 1 and (TT + t) % 8 < TT:
                        pe.wait_ge(*s.res((TT + t) % 8 + 1))
                    tok = slice(t * P, (t + 1) * P)
                    last = three(psum[(half * TT + t) % 8], a_hi[:, slot, tok],
                                 a_lo[:, slot, tok], wd_hi[:, slot, :], wd_lo[:, slot, :],
                                 start, stop)
                    if stop:
                        last.then_inc(s.out.sem, 1)
                return last

            pe.wait_ge(*s.a(2 * FT))
            for half in range(2):
                for slot in range(2):
                    down(half, slot, slot, slot == 0, False).then_inc(s.dmm.sem, 1)
                with pe.Fori(1, FT // 2 - 1) as pair:
                    j = 2 * pair
                    for slot in range(2):
                        down(half, j + slot, slot, False, False).then_inc(s.dmm.sem, 1)
                down(half, FT - 2, 0, False, False).then_inc(s.dmm.sem, 1)
                down(half, FT - 1, 1, False, True)

        small = Region(nc, gain_at, scratch_end)
        xp = small.put("xp", [P, 2, 668])
        sq_rows = [nc.alloc_sbuf_tensor_at(f"sq_rows{i}", [P, BANK], F32, offset=gain_at + 2048 * i)
                   for i in range(2)]
        rope_tmp = small.put("rope_tmp", [P, 4, TT * 64])
        rot = small.put("rot", [P, 2, TT, 8])
        gdn_gain = small.put("gdn_gain", [P, P])
        diff_gain = small.put("diff_gain", [P, P])
        qk_gain = small.put("qk_gain", [P, 2, DK])
        lam_in = small.put("lam_in", [P, 2, 2, DK])
        head_par = small.put("head_par", [P, 2, HEADS])
        gates = small.put("gates", [P, 20, TT, HEADS])
        ba = small.put("ba", [P, TT, 8])
        lam = small.put("lam", [P, 8])
        qk_ss = small.put("qk_ss", [P, 2, 3, TT * 8])
        soft = small.put("soft", [P, 16])

        mixm = Region(nc, F0, ARENA_END)
        z = mixm.put("z", [P, TT, BANK])
        q_tok = mixm.put("q_tok", [P, TT, BANK])
        k_at = mixm.at
        k_tok = mixm.put("k_tok", [P, TT, BANK])
        v_at = mixm.at
        v_tok = mixm.put("v_tok", [P, TT, BANK])
        tok_at = mixm.at
        tok = mixm.put("tok", [P, TT, CONV_T, P])
        c_at = mixm.at
        cT = mixm.put("cT", [P, CONV_T, TOK])
        c_end = d_at = mixm.at
        raw_cv = mixm.put("raw_cv", [P, 2, KT, P])
        cv_hi = mixm.put("cv_hi", [P, 2, KT, P], F32R)
        cv_lo = mixm.put("cv_lo", [P, 2, KT, P], F32R)
        d_end = mixm.at
        kb_mem = Region(nc, k_at, v_at)
        hist = kb_mem.put("hist", [P, CONV_T, 28])
        tail = kb_mem.put("tail", [P, CONV_T, 27])
        vb_mem = Region(nc, v_at, tok_at)
        conv_out = vb_mem.put("conv_out", [27, CONV_T * P])
        raw_ba = vb_mem.put("raw_ba", [P, KT, 8])
        ba_hi = vb_mem.put("ba_hi", [P, KT, 8], F32R)
        ba_lo = vb_mem.put("ba_lo", [P, KT, 8], F32R)
        conv_rows = Region(nc, tok_at, c_at).put("conv_rows", [28, CONV_T * P])
        dm = Region(nc, d_at, d_end)
        raw_b = dm.put("raw_b", [P, 2, 4, BANK])
        b_hi = dm.put("b_hi", [P, 2, BANK], F32R)
        b_lo = dm.put("b_lo", [P, 2, BANK], F32R)

        g1 = Region(nc, ARENA, h_at)
        H4 = [P, HEADS, P]
        kbg, kd, qd, knT, kbT, qnT, qdT, LT, QKT = (
            g1.put(n, H4) for n in "kbg kd qd knT kbT qnT qdT LT QKT".split())
        g2 = Region(nc, c_at, c_end)
        Tm, Rm, Xm, nwT, u_sb, S_p = (g2.put(n, H4) for n in "Tm Rm Xm nwT u_sb S_p".split())
        ct_at = g2.at
        CT = [g2.put(f"CT{i}", H4) for i in range(2)]
        u_exp = nc.alloc_sbuf_tensor_at("u_exp", [P, STREAMS, P], F32, offset=ct_at)
        ge_at = g2.at
        gbc, ET = g2.put("gbc", H4), g2.put("ET", H4)
        qd_exp = nc.alloc_sbuf_tensor_at("qd_exp", [P, STREAMS, P], F32, offset=ge_at)
        S_s = g2.put("S_s", [P, STREAMS, P])
        w_exp = g2.put("w_exp", [P, STREAMS, P])
        o_sq = nc.alloc_sbuf_tensor_at("o_sq", [P, TT, BANK], F32, offset=ARENA)

        a1 = Region(nc, h_at, h_end)
        qT = a1.put("qT", [P, HEADS, PROMPT])
        kTn = a1.put("kTn", [P, HEADS, TOK])
        q_bd = a1.put("q_bd", [P, STREAMS, HEADS, 32])
        KTc = a1.put("KTc", [P, HEADS, PAST])
        pc = a1.put("pc", [P, BANK])
        a2 = Region(nc, d_at, d_end)
        K_c = [a2.put("K_c0", [P, 4, BANK]),
               nc.alloc_sbuf_tensor_at("K_c1", [P, 4, BANK], F32, offset=k_at)]
        V_c = a2.put("V_c", [P, 4, BANK])
        V_n = a2.put("V_n", [STEP, BANK])
        p_at = a2.at
        pr = a2.put("pr", [P, 2, BANK])
        ps = nc.alloc_sbuf_tensor_at("ps", [P, PAST + STEP], F32, offset=p_at)
        Cm = nc.alloc_sbuf_tensor_at("Cm", [P, P], F32, offset=p_at + 3072)
        pT = a1.put("pT", [P, BANK])
        pTn = a2.put("pTn", [STEP, P])
        od_sq = nc.alloc_sbuf_tensor_at("od_sq", [P, TT, BANK], F32, offset=h_at)
        wout = Region(nc, tok_at, c_at)
        raw_o = wout.put("raw_o", [P, KT, BANK])
        o_hi = wout.put("o_hi", [P, 2, BANK], F32R)
        o_lo = wout.put("o_lo", [P, 2, BANK], F32R)
        wout2 = Region(nc, c_at, c_end)
        raw_o1 = wout2.put("raw_o1", [P, KT, BANK])

        mn, on = Norm(1), Norm(2)
        N = {n: sem(n) for n in """
            x_spilled x_back params_loaded conv_rows_loaded hist_transposed hist_ready pad_zero
            conv_hi conv_lo conv_product conv_padded conv_sum conv_silu tail_transposed tail_rows
            tail_stored ba_loaded ba_hi ba_lo ba_product ba_copied
            group_hi group_lo group_step group_evac row_squares row_sums kv_stored
            lam_chain qk_chain act_qk qk_done lam_exp
            tok_tr tok_copied tok_sq tok_sums gate_chain gate_act g_product cs_ready rk_root
            scaled pooled tr_scaled act_T kbT_ready diff decay_exp decay kk masked ct r0 t0 t0c x_mm
            x_copied level_mm level_upd w_mm nw u_mm u_copied o_mm o_copied S_ready S_stored
            ss_loaded ss_stored exp_ready zero_exp u4_mm ue_ready o4_mm oc4 ss_ready gls
            og_chain og_act og_done
            qbd_zero qkT_mm qkT_copied sc_mm nmax probs pcomb p_tr p_copied pv_mm pv_copied att_chain
            kt_mm kt_copied ssc_mm s_nmax s_probs s_comb sp_mm sp_copied spv_mm 
            od_chain od_act od_done wo_hi wo_lo wo_step wo_res 
            """.split()}
        s_cvw = [sem(f"conv_loaded{i}") for i in range(2)]
        s_gw = [sem(f"group_loaded{i}") for i in range(2)]
        s_K = [sem(f"k_cache_loaded{i}") for i in range(2)]
        s_V = sem("v_cache_loaded")

        x_mid = nc.dram_tensor("x_mid", [TOK, D], F32, kind="Internal").ap()
        w_in = io["w_in"][0].rearrange("(k p) c -> p k c", p=P)
        w_out = io["w_out"][0].rearrange("(k p) c -> p k c", p=P)
        V = nc.vector

        def link(eng, s, n, ins):
            ins.then_inc(N[s], 1)
            eng.wait_ge(N[s], n)

        def bc(ap, n):
            return ap.unsqueeze(2).broadcast_to([ap.shape[0], ap.shape[1], n])

        def over(ap, n):
            return ap.unsqueeze(1).broadcast_to([ap.shape[0], n, ap.shape[1]])

        def conv_sync(sp):
            rows = conv_rows[:]
            sp.wait_ge(*f1.res(2 * TT))
            sp.dma_start(rows[0:24, :], io["state_conv"][0].rearrange("b w c -> (b w) c"))\
                .then_inc(N["conv_rows_loaded"], 16)
            sp.dma_start(rows[24:28, :], io["conv_w"][0]).then_inc(N["conv_rows_loaded"], 16)

            def load(j, slot):
                sp.dma_start(raw_cv[:, slot], w_in[:, :, bass.ds(j * P, P)]).then_inc(s_cvw[slot], 16)

            load(0, 0)
            load(1, 1)
            sp.dma_start(raw_ba[:], w_in[:, :, BA_COL:BA_COL + 8]).then_inc(N["ba_loaded"], 16)
            sp.wait_ge(*mn.lo(2 * TT))
            for dst, src in ((gdn_gain[:], io["gdn_out_norm"].to_broadcast([P, P])),
                             (diff_gain[:], io["diff_out_norm"].to_broadcast([P, P])),
                             (qk_gain[:, 0, :], io["q_norm"].to_broadcast([P, DK])),
                             (qk_gain[:, 1, :], io["k_norm"].to_broadcast([P, DK])),
                             (lam_in[:, 0], io["lambda_q"].to_broadcast([P, 2, DK])),
                             (lam_in[:, 1], io["lambda_k"].to_broadcast([P, 2, DK])),
                             (head_par[:, 0, :], io["a_log"].to_broadcast([P, HEADS])),
                             (head_par[:, 1, :], io["dt_bias"].to_broadcast([P, HEADS])),
                             (rot[:], io["rotary"].rearrange("p (a t f) -> p a t f", a=2, t=TT))):
                sp.dma_start(dst, src).then_inc(N["params_loaded"], 16)
            sp.dma_start(x_mid[0:PROMPT, :].rearrange("(t p) c -> p t c", p=P), x_tok[:, 0:4, :])\
                .then_inc(N["x_spilled"], 16)
            sp.dma_start(x_mid[PROMPT:TOK, :], x_tok[:, 4, :]).then_inc(N["x_spilled"], 16)
            with sp.Fori(1, CONV_T // 2) as pair:
                j = 2 * pair
                for slot in range(2):
                    sp.wait_ge(N["conv_lo"], j + slot - 1)
                    load(j + slot, slot)
            for hg in range(8):
                g, kh = hg // 2, hg % 2
                if hg < 2:
                    sp.wait_ge(N["conv_lo"], CONV_T)
                    sp.wait_ge(N["conv_product"], CONV_T)
                else:
                    sp.wait_ge(N["group_lo"], 4 * (hg - 1))
                sp.dma_start(raw_b[:, hg % 2],
                             w_in[:, 4 * kh:4 * kh + 4, Z_COL + BANK * g:Z_COL + BANK * (g + 1)])\
                    .then_inc(s_gw[hg % 2], 16)

        def conv_act(act):
            def split(j, slot):
                act.wait_ge(s_cvw[slot], 8 * (j - slot) + 16)
                nc.scalar.activation(cv_hi[:, slot], raw_cv[:, slot], ACT.Copy)\
                    .then_inc(N["conv_hi"], 1)

            def pad(j, slot):
                act.wait_ge(N["conv_product"], j + 1)
                a, b = psum[2 * slot], psum[2 * slot + 1]
                x = xp[:, slot, :]
                for dst, src in ((x[:, 3:3 + HALF], a[:, 0:HALF]),
                                 (x[:, 3 + HALF:3 + PROMPT], b[:, 0:PROMPT - HALF]),
                                 (streams(x)[:, :, 3:19],
                                  b[:, PROMPT - HALF:HALF].rearrange("p (b s) -> p b s", s=STEP))):
                    nc.scalar.activation(dst, src, ACT.Copy).then_inc(N["conv_padded"], 1)

            def silu(j):
                act.wait_ge(N["conv_sum"], 11 * j + 11)
                nc.scalar.activation(cT[:, j, :], cT[:, j, :], ACT.Silu).then_inc(N["conv_silu"], 1)

            split(0, 0)
            split(1, 1)
            act.wait_ge(N["pad_zero"], 1)
            pad(0, 0)
            with act.Fori(1, CONV_T // 2) as pair:
                j = 2 * pair
                act.wait_ge(N["conv_product"], j - 1)
                split(j, 0)
                act.wait_ge(N["conv_sum"], 11 * j - 21)
                pad(j - 1, 1)
                silu(j - 2)
                act.wait_ge(N["conv_product"], j)
                split(j + 1, 1)
                act.wait_ge(N["conv_sum"], 11 * j - 11)
                pad(j, 0)
                silu(j - 1)
            act.wait_ge(N["conv_sum"], 11 * (CONV_T - 2))
            pad(CONV_T - 1, 1)
            silu(CONV_T - 2)
            silu(CONV_T - 1)
            act.wait_ge(N["ba_loaded"], 16)
            nc.scalar.activation(ba_hi[:], raw_ba[:], ACT.Copy).then_inc(N["ba_hi"], 1)

        def streams(x):
            return x[:, 515:667].rearrange("p (b s) -> p b s", s=19)

        def conv_dve(dve):
            V.memset(xp[:, :, 0:3], 0.0).then_inc(N["pad_zero"], 1)
            dve.wait_ge(N["hist_transposed"], 1)
            V.tensor_copy(hist[:], psum[7][:, 0:336].rearrange("p (c w) -> p c w", w=28))\
                .then_inc(N["hist_ready"], 1)
            dve.wait_ge(N["hist_ready"], 1)

            def split(j, slot):
                dve.wait_ge(N["conv_hi"], j + 1)
                V.tensor_tensor(cv_lo[:, slot], raw_cv[:, slot], raw(cv_hi[:, slot]), ALU.subtract)\
                    .then_inc(N["conv_lo"], 1)

            def conv(j, slot):
                x, s, n = xp[:, slot, :], N["conv_sum"], 11 * j
                V.tensor_copy(streams(x)[:, :, 0:3],
                              hist[:, j, 0:24].rearrange("p (b w) -> p b w", w=3)).then_inc(s, 1)
                dve.wait_ge(N["conv_padded"], 3 * j + 3)
                V.tensor_copy(tail[:, j, 0:3], x[:, PROMPT:PROMPT + 3]).then_inc(s, 1)
                V.tensor_copy(tail[:, j, 3:27].rearrange("p (b w) -> p b w", w=3),
                              streams(x)[:, :, 16:19]).then_inc(s, 1)
                yp = cT[:, j, 0:PROMPT]
                yq = cT[:, j, PROMPT:TOK].rearrange("p (b s) -> p b s", s=STEP)
                for i in range(4):
                    w = hist[:, j, 24 + i:25 + i]
                    if i == 0:
                        dve.wait_ge(s, n + 1)
                        V.tensor_scalar(yp, x[:, 0:PROMPT], w, None, ALU.mult).then_inc(s, 1)
                        V.tensor_scalar(yq, streams(x)[:, :, 0:16], w, None, ALU.mult).then_inc(s, 1)
                    else:
                        dve.wait_ge(s, n + 2 + 2 * i)
                        V.scalar_tensor_tensor(yp, x[:, i:i + PROMPT], w, yp, ALU.mult,
                                               ALU.add).then_inc(s, 1)
                        dve.wait_ge(s, n + 3 + 2 * i)
                        V.scalar_tensor_tensor(yq, streams(x)[:, :, i:i + 16], w, yq, ALU.mult,
                                               ALU.add).then_inc(s, 1)

            split(0, 0)
            split(1, 1)
            conv(0, 0)
            with dve.Fori(1, CONV_T // 2) as pair:
                j = 2 * pair
                split(j, 0)
                dve.wait_ge(N["conv_sum"], 11 * j - 11)
                conv(j - 1, 1)
                split(j + 1, 1)
                dve.wait_ge(N["conv_sum"], 11 * j)
                conv(j, 0)
            dve.wait_ge(N["conv_sum"], 11 * (CONV_T - 1))
            conv(CONV_T - 1, 1)
            dve.wait_ge(N["ba_hi"], 1)
            V.tensor_tensor(ba_lo[:], raw_ba[:], raw(ba_hi[:]), ALU.subtract).then_inc(N["ba_lo"], 1)
            for i in range(3):
                dve.wait_ge(N["tail_transposed"], i + 1)
                V.tensor_copy(conv_out[:, i * BANK:(i + 1) * BANK], psum[5 + i][0:27, :])\
                    .then_inc(N["tail_rows"], 1)

        def conv_pe(pe):
            pe.wait_ge(N["conv_rows_loaded"], 32)
            for c in range(CONV_T):
                last = nc.tensor.transpose(psum[7][:, 28 * c:28 * c + 28],
                                           conv_rows[:, c * P:(c + 1) * P], ident[0:28, 0:28])
            last.then_inc(N["hist_transposed"], 1)

            def product(j, slot):
                for k in range(KT):
                    for part in range(2):
                        t = slice(part * HALF, (part + 1) * HALF)
                        last = three(psum[2 * slot + part][:, 0:HALF], cv_hi[:, slot, k, :],
                                     cv_lo[:, slot, k, :], hT_hi[:, k, t], hT_lo[:, k, t],
                                     k == 0, k == KT - 1)
                last.then_inc(N["conv_product"], 1)

            pe.wait_ge(*mn.lo(2 * TT))
            for slot in range(2):
                pe.wait_ge(N["conv_lo"], slot + 1)
                product(slot, slot)
            with pe.Fori(1, CONV_T // 2) as pair:
                for slot in range(2):
                    j = 2 * pair + slot
                    pe.wait_ge(N["conv_lo"], j + 1)
                    pe.wait_ge(N["conv_padded"], 3 * j - 3)
                    product(j, slot)
            pe.wait_ge(N["ba_lo"], 1)
            pe.wait_ge(N["conv_padded"], 3 * CONV_T)
            for t in range(TT):
                for k in range(KT):
                    c = slice(t * P, (t + 1) * P)
                    last = three(psum[0][:, 8 * t:8 * t + 8], hT_hi[:, k, c], hT_lo[:, k, c],
                                 ba_hi[:, k, :], ba_lo[:, k, :], k == 0, k == KT - 1)
            last.then_inc(N["ba_product"], 1)
            pe.wait_ge(N["conv_sum"], 11 * CONV_T)
            for i in range(3):
                for c in range(4):
                    last = nc.tensor.transpose(psum[5 + i][0:27, c * P:(c + 1) * P],
                                               tail[:, 4 * i + c, :], ident)
                last.then_inc(N["tail_transposed"], 1)

        EVACS = [(0, 1), (2, 3, 4)] + [()] * (KT - 2)

        def group_act(act):
            for g in range(4):
                for k in range(KT):
                    n = g * KT + k
                    act.wait_ge(s_gw[n // 4 % 2], 16 * (n // 8 + 1))
                    if n == 0:
                        act.wait_ge(N["conv_product"], CONV_T)
                    elif n >= 2:
                        act.wait_ge(N["group_step"], n - 1)
                    nc.scalar.activation(b_hi[:, n % 2], raw_b[:, n // 4 % 2, n % 4], ACT.Copy)\
                        .then_inc(N["group_hi"], 1)
                    for t in EVACS[k] if g else ():
                        evac(act, g - 1, t)
            for t in range(TT):
                evac(act, 3, t)

        def evac(act, g, t):
            act.wait_ge(N["group_step"], (g + 1) * KT)
            if g == 2 and t == 0:
                act.wait_ge(N["tail_transposed"], 3)
            if g == 3 and t == 0:
                act.wait_ge(N["tail_stored"], 32)
            dst = (z, q_tok, k_tok, v_tok)[g][:, t, :]
            nc.scalar.activation(dst, psum[t], ACT.Silu if g == 0 else ACT.Copy)\
                .then_inc(N["group_evac"], 1)
            if g in (1, 2):
                m = (g - 1) * TT + t
                act.wait_ge(N["group_evac"], g * TT + t + 1)
                if m < 2:
                    act.wait_ge(N["conv_sum"], 11 * CONV_T)
                else:
                    act.wait_ge(N["row_sums"], m - 1)
                nc.scalar.activation(sq_rows[m % 2][:], dst, ACT.Square)\
                    .then_inc(N["row_squares"], 1)

        def group_dve(dve):
            def sums(g, t):
                m = (g - 1) * TT + t
                dve.wait_ge(N["row_squares"], m + 1)
                V.tensor_reduce(qk_ss[:, g - 1, 0, 8 * t:8 * t + 8],
                                sq_rows[m % 2][:].rearrange("p (c d) -> p c d", d=DK), AX.X,
                                ALU.add).then_inc(N["row_sums"], 1)

            for g in range(4):
                for k in range(KT):
                    n = g * KT + k
                    dve.wait_ge(N["group_hi"], n + 1)
                    V.tensor_tensor(b_lo[:, n % 2], raw_b[:, n // 4 % 2, n % 4],
                                    raw(b_hi[:, n % 2]), ALU.subtract).then_inc(N["group_lo"], 1)
                    for t in EVACS[k] if g in (2, 3) else ():
                        sums(g - 1, t)

        def group_pe(pe):
            for g in range(4):
                for k in range(KT):
                    n = g * KT + k
                    pe.wait_ge(N["group_lo"], n + 1)
                    for t in range(TT):
                        if k == 0:
                            if g:
                                pe.wait_ge(N["group_evac"], (g - 1) * TT + t + 1)
                            elif t == 0:
                                pe.wait_ge(N["conv_padded"], 3 * CONV_T)
                                pe.wait_ge(N["ba_copied"], 1)
                        c = slice(t * P, (t + 1) * P)
                        last = three(psum[t], hT_hi[:, k, c], hT_lo[:, k, c], b_hi[:, n % 2],
                                     b_lo[:, n % 2], k == 0, k == KT - 1)
                    last.then_inc(N["group_step"], 1)

        def qk_dve(dve):
            dve.wait_ge(N["params_loaded"], 16 * 9)
            prod = lam_in[:, 0]
            link(dve, "lam_chain", 1, V.tensor_tensor(prod, lam_in[:, 0], lam_in[:, 1], ALU.mult))
            V.tensor_reduce(lam[:, 0:2], prod, AX.X, ALU.add).then_inc(N["lam_chain"], 1)
            dve.wait_ge(N["lam_exp"], 1)
            link(dve, "lam_chain", 3, V.tensor_tensor(lam[:, 4:5], lam[:, 2:3], lam[:, 3:4],
                                                      ALU.subtract))
            link(dve, "lam_chain", 4, V.tensor_scalar(lam[:, 5:6], lam[:, 4:5], LAM_INIT, None,
                                                      ALU.add))
            link(dve, "lam_chain", 5, V.scalar_tensor_tensor(
                lam[:, 6:7], const("map1"), lam[:, 5:6], const("map0"), ALU.mult, ALU.add))
            link(dve, "lam_chain", 6, V.tensor_scalar(lam[:, 7:8], lam[:, 5:6], -1.0, None, ALU.mult))
            n = 0
            for w, x in enumerate((q_tok, k_tok)):
                dve.wait_ge(N["row_sums"], TT * (w + 1))
                dve.wait_ge(N["group_evac"], TT * (w + 2))
                link(dve, "qk_chain", n + 1, V.tensor_scalar(qk_ss[:, w, 1, :], qk_ss[:, w, 0, :],
                                                             1.0 / DK, EPS, ALU.mult, ALU.add))
                V.reciprocal(qk_ss[:, w, 2, :], qk_ss[:, w, 1, :]).then_inc(N["qk_chain"], 1)
                dve.wait_ge(N["act_qk"], w + 1)
                rows = x[:].rearrange("p t (c d) -> p (t c) d", d=DK)
                link(dve, "qk_chain", n + 3, V.tensor_tensor(rows, rows, bc(qk_ss[:, w, 0, :], DK),
                                                             ALU.mult))
                link(dve, "qk_chain", n + 4, V.tensor_tensor(rows, rows,
                                                             over(qk_gain[:, w, :], TT * 8), ALU.mult))
                v4 = x[:].rearrange("p t (c d) -> p t c d", d=DK)
                x1, x2 = v4[:, :, :, 0:8], v4[:, :, :, 8:16]
                tmp = [rope_tmp[:, i, :].rearrange("p (t c d) -> p t c d", c=8, d=8)
                       for i in range(4)]
                cos, sin = (rot[:, i].unsqueeze(2).broadcast_to([P, TT, 8, 8]) for i in range(2))
                for i, (a, f) in enumerate(((x1, cos), (x2, sin), (x2, cos), (x1, sin))):
                    V.tensor_tensor(tmp[i], a, f, ALU.mult).then_inc(N["qk_chain"], 1)
                dve.wait_ge(N["qk_chain"], n + 8)
                V.tensor_tensor(x1, tmp[0], tmp[1], ALU.subtract).then_inc(N["qk_done"], 1)
                V.tensor_tensor(x2, tmp[2], tmp[3], ALU.add).then_inc(N["qk_done"], 1)
                dve.wait_ge(N["qk_done"], 2 * w + 2)
                n += 8

        def qk_act(act):
            act.wait_ge(N["lam_chain"], 2)
            nc.scalar.activation(lam[:, 2:4], lam[:, 0:2], ACT.Exp).then_inc(N["lam_exp"], 1)
            for w in range(2):
                act.wait_ge(N["qk_chain"], 8 * w + 2)
                nc.scalar.activation(qk_ss[:, w, 0, :], qk_ss[:, w, 2, :], ACT.Sqrt)\
                    .then_inc(N["act_qk"], 1)

        (G_BETA, G_G, G_CUM, G_TOT, G_EC, G_ER, G_ET, G_RQ, G_RK, G_KB, G_KBG, G_KD, G_QD, G_A,
         G_B, G_C, G_D, G_SSQ, G_SSK, G_E) = range(20)
        gt = lambda i: gates[:, i]
        GB = [5, 6, 7]

        def tok_pe(pe):
            pe.wait_ge(N["conv_silu"], CONV_T)
            pe.wait_ge(N["tail_rows"], 3)
            for n in range(3 * TT):
                t, w = n // 3, n % 3
                if n >= 3:
                    pe.wait_ge(N["tok_copied"], n - 2)
                for h in range(HEADS):
                    last = nc.tensor.transpose(psum[GB[w]][:, h * P:(h + 1) * P],
                                               cT[:, 4 * w + h, t * P:(t + 1) * P], ident)
                last.then_inc(N["tok_tr"], 1)

        def tok_dve(dve):
            for n in range(3 * TT):
                t, w = n // 3, n % 3
                dve.wait_ge(N["tok_tr"], n + 1)
                V.tensor_copy(tok[:, t, 4 * w:4 * w + 4, :],
                              psum[GB[w]].rearrange("p (h d) -> p h d", d=P))\
                    .then_inc(N["tok_copied"], 1)
                if n >= 3 and w < 2:
                    tok_sum(dve, 2 * (t - 1) + w)
            tok_sum(dve, 2 * TT - 2)
            tok_sum(dve, 2 * TT - 1)

        def tok_sum(dve, m):
            t, w = m // 2, m % 2
            dve.wait_ge(N["tok_sq"], m + 1)
            V.tensor_reduce(gates[:, G_SSQ + w, t, :],
                            sq_rows[w][:].rearrange("p (h d) -> p h d", d=P), AX.X, ALU.add)\
                .then_inc(N["tok_sums"], 1)

        def tok_act(act):
            act.wait_ge(N["row_sums"], 2 * TT)
            for m in range(2 * TT):
                t, w = m // 2, m % 2
                act.wait_ge(N["tok_copied"], 3 * t + w + 1)
                if m >= 2:
                    act.wait_ge(N["tok_sums"], m - 1)
                nc.scalar.activation(sq_rows[w][:].rearrange("p (h d) -> p h d", d=P),
                                     tok[:, t, 4 * w:4 * w + 4, :], ACT.Square)\
                    .then_inc(N["tok_sq"], 1)

        def gate_dve(dve):
            c = [0]

            def l(ins):
                c[0] += 1
                link(dve, "gate_chain", c[0], ins)

            beta_in, a_in = ba[:, :, 0:4], ba[:, :, 4:8]
            dt = over(head_par[:, 1, :], TT)
            l(V.tensor_tensor(gt(G_A), a_in, dt, ALU.add))
            l(V.tensor_scalar(gt(G_B), gt(G_A), -1.0, None, ALU.mult))
            l(V.tensor_tensor(gt(G_B), gt(G_A), gt(G_B), ALU.min))
            dve.wait_ge(N["gate_act"], 3)
            l(V.tensor_scalar(gt(G_C), gt(G_C), 1.0, None, ALU.add))
            l(V.reciprocal(gt(G_BETA), gt(G_C)))
            l(V.tensor_scalar(gt(G_A), gt(G_A), 0.0, None, ALU.max))
            l(V.tensor_tensor(gt(G_A), gt(G_A), gt(G_D), ALU.add))
            l(V.scalar_tensor_tensor(gt(G_G), gt(G_A), -1.0, over(head_par[:, 0, :], TT), ALU.mult,
                                     ALU.mult))
            dve.wait_ge(N["g_product"], 1)
            l(V.tensor_copy(gt(G_CUM), psum[6][:, 0:20].rearrange("p (t h) -> p t h", h=4)))
            l(V.tensor_copy(gt(G_TOT), psum[6][:, 32:52].rearrange("p (t h) -> p t h", h=4)))
            l(V.tensor_tensor(gt(G_E), gt(G_TOT), gt(G_CUM), ALU.subtract))
            ss = gates[:, G_SSQ:G_SSQ + 2]
            l(V.tensor_scalar(gates[:, G_A:G_A + 2], ss, EPS, None, ALU.add))
            l(V.reciprocal(gates[:, G_C:G_C + 2], gates[:, G_A:G_A + 2]))
            dve.wait_ge(N["gate_act"], 7)
            l(V.tensor_scalar(gt(G_RQ), gt(G_RQ), float(P) ** -0.5, None, ALU.mult))
            l(V.tensor_tensor(gt(G_KB), gt(G_RK), gt(G_BETA), ALU.mult))
            l(V.tensor_tensor(gt(G_KBG), gt(G_KB), gt(G_EC), ALU.mult))
            l(V.tensor_tensor(gt(G_KD), gt(G_RK), gt(G_ER), ALU.mult))
            V.tensor_tensor(gt(G_QD), gt(G_RQ), gt(G_EC), ALU.mult).then_inc(N["cs_ready"], 1)
            dve.wait_ge(N["cs_ready"], 1)

        def gate_act(act):
            act.wait_ge(N["gate_chain"], 3)
            nc.scalar.activation(gt(G_C), ba[:, :, 0:4], ACT.Exp, scale=-1.0)\
                .then_inc(N["gate_act"], 1)
            nc.scalar.activation(head_par[:, 0, :], head_par[:, 0, :], ACT.Exp)\
                .then_inc(N["gate_act"], 1)
            nc.scalar.activation(gt(G_D), gt(G_B), ACT.Exp).then_inc(N["rk_root"], 1)
            act.wait_ge(N["rk_root"], 1)
            nc.scalar.activation(gt(G_D), gt(G_D), ACT.Ln, bias=1.0).then_inc(N["gate_act"], 1)
            act.wait_ge(N["gate_chain"], 11)
            for dst, src in ((G_EC, G_CUM), (G_ER, G_E), (G_ET, G_TOT)):
                nc.scalar.activation(gt(dst), gt(src), ACT.Exp).then_inc(N["gate_act"], 1)
            act.wait_ge(N["gate_chain"], 13)
            nc.scalar.activation(gates[:, G_RQ:G_RQ + 2], gates[:, G_C:G_C + 2], ACT.Sqrt)\
                .then_inc(N["gate_act"], 1)

        def gate_pe(pe):
            pe.wait_ge(N["gate_chain"], 8)
            pe.wait_ge(N["tok_copied"], 3 * TT)
            g = gt(G_G)
            nc.tensor.matmul(psum[6][:, 0:16], const("cum_p"), g[:, 0:4, :], start=True, stop=True)
            nc.tensor.matmul(psum[6][:, 16:20], const("cum_s"), g[:, 4, :], start=True, stop=True)
            nc.tensor.matmul(psum[6][:, 32:48], const("ones"), g[:, 0:4, :], start=True, stop=True)
            nc.tensor.matmul(psum[6][:, 48:52], const("blk_s"), g[:, 4, :], start=True, stop=True)\
                .then_inc(N["g_product"], 1)

        LV = [7, 7, 7, 7, 4]
        CTB = [sum(LV[:t]) for t in range(TT + 1)]
        UPB = [sum(2 * (v - 1) - 1 for v in LV[:t]) for t in range(TT + 1)]
        XB = [sum(v - 1 for v in LV[:t]) for t in range(TT + 1)]
        b4 = lambda bank: psum[bank].rearrange("p (h d) -> p h d", d=P)
        hc = lambda h: slice(h * P, (h + 1) * P)

        def gdn_dve(dve, t):
            q4, k4 = tok[:, t, 0:4, :], tok[:, t, 4:8, :]
            f = lambda i: bc(gates[:, i, t, :], P)
            if t:
                dve.wait_ge(N["o_mm"], 2 * t)
            V.tensor_tensor(Xm[:], k4, f(G_RK), ALU.mult).then_inc(N["scaled"], 1)
            V.tensor_tensor(CT[1][:], k4, f(G_KB), ALU.mult).then_inc(N["scaled"], 1)
            V.tensor_tensor(CT[0][:], q4, f(G_RQ), ALU.mult).then_inc(N["scaled"], 1)
            V.tensor_tensor(qd[:], q4, f(G_QD), ALU.mult).then_inc(N["scaled"], 1)
            V.tensor_copy(gbc[:], f(G_G)).then_inc(N["scaled"], 1)
            dve.wait_ge(N["tr_scaled"], 5 * t + 2)
            V.tensor_copy(kbT[:], b4(6)).then_inc(N["kbT_ready"], 1)
            dve.wait_ge(N["tr_scaled"], 5 * t + 5)
            V.tensor_tensor(ET[:], b4(6), f(G_CUM), ALU.subtract).then_inc(N["diff"], 1)
            dve.wait_ge(N["diff"], 2 * t + 1)
            V.tensor_scalar(ET[:], ET[:], 0.0, None, ALU.min).then_inc(N["diff"], 1)
            dve.wait_ge(N["decay_exp"], t + 1)
            V.tensor_tensor(ET[:], ET[:], over(const("cum_s" if t == 4 else "cum_p"), HEADS),
                            ALU.mult).then_inc(N["decay"], 1)
            dve.wait_ge(N["decay"], t + 1)
            dve.wait_ge(N["kk"], 2 * t + 1)
            V.tensor_tensor(LT[:], b4(7), ET[:], ALU.mult).then_inc(N["masked"], 1)
            dve.wait_ge(N["kk"], 2 * t + 2)
            V.tensor_tensor(QKT[:], b4(5), ET[:], ALU.mult).then_inc(N["masked"], 1)
            dve.wait_ge(N["ct"], CTB[t] + 1)
            V.tensor_tensor(Rm[:], over(ident, HEADS), CT[0][:], ALU.subtract).then_inc(N["r0"], 1)
            n = LV[t] - 1
            for l in range(1, n + 1):
                dve.wait_ge(N["level_mm"], XB[t] + l)
                if l == 1:
                    dve.wait_ge(N["t0c"], t + 1)
                    dve.wait_ge(N["r0"], t + 1)
                else:
                    dve.wait_ge(N["level_upd"], UPB[t] + 2 * (l - 1))
                if l < n:
                    V.tensor_tensor(Tm[:], Tm[:], b4(5), ALU.subtract).then_inc(N["level_upd"], 1)
                V.tensor_tensor(Rm[:], Rm[:], b4(6), ALU.subtract).then_inc(N["level_upd"], 1)

        def gdn_state_dve(dve, t):
            dve.wait_ge(N["u_mm"], t + 1)
            V.tensor_copy(u_sb[:], b4(5)).then_inc(N["u_copied"], 1)
            dve.wait_ge(N["o_mm"], 2 * t + 2)
            dve.wait_ge(N["S_ready"], 4 * t + 1)
            for h in range(HEADS):
                V.scalar_tensor_tensor(S_p[:, h, :], S_p[:, h, :], gates[:, G_ET, t, h:h + 1],
                                       psum[7][:, hc(h)], ALU.mult, ALU.add)\
                    .then_inc(N["S_ready"], 1)

        def gdn_act(act, t):
            act.wait_ge(N["tr_scaled"], 5 * t + 1)
            nc.scalar.activation(knT[:], b4(5), ACT.Copy).then_inc(N["act_T"], 1)
            act.wait_ge(N["tr_scaled"], 5 * t + 3)
            nc.scalar.activation(qnT[:], b4(7), ACT.Copy).then_inc(N["act_T"], 1)
            act.wait_ge(N["tr_scaled"], 5 * t + 4)
            nc.scalar.activation(qdT[:], b4(5), ACT.Copy).then_inc(N["act_T"], 1)
            act.wait_ge(N["diff"], 2 * t + 2)
            if t == 4:
                nc.scalar.activation(gls[:], b4(6)[:, :, STEP - 1::STEP], ACT.Exp)\
                    .then_inc(N["gls"], 1)
            nc.scalar.activation(ET[:], ET[:], ACT.Exp).then_inc(N["decay_exp"], 1)
            act.wait_ge(N["t0"], t + 1)
            nc.scalar.activation(Tm[:], b4(6), ACT.Copy).then_inc(N["t0c"], 1)
            for l in range(1, LV[t]):
                act.wait_ge(N["x_mm"], XB[t] + l)
                nc.scalar.activation(Xm[:], b4(7), ACT.Copy).then_inc(N["x_copied"], 1)
            act.wait_ge(N["w_mm"], t + 1)
            nc.scalar.activation(nwT[:], b4(7), ACT.Copy, scale=-1.0).then_inc(N["nw"], 1)
            if t < 4:
                act.wait_ge(N["o_mm"], 2 * t + 1)
                nc.scalar.activation(tok[:, t, 0:4, :], b4(6), ACT.Copy).then_inc(N["o_copied"], 1)

        def gdn_pool(pool, t):
            k4, v4 = tok[:, t, 4:8, :], tok[:, t, 8:12, :]
            f = lambda i: bc(gates[:, i, t, :], P)
            if t == 0:
                pool.wait_ge(N["cs_ready"], 1)
            else:
                pool.wait_ge(N["o_mm"], 2 * t)
            nc.gpsimd.tensor_tensor(kbg[:], k4, f(G_KBG), ALU.mult).then_inc(N["pooled"], 1)
            nc.gpsimd.tensor_tensor(v4, v4, f(G_BETA), ALU.mult).then_inc(N["pooled"], 1)
            nc.gpsimd.tensor_tensor(kd[:], k4, f(G_KD), ALU.mult).then_inc(N["pooled"], 1)
            pool.wait_ge(N["masked"], 2 * t + 1)
            for i in range(LV[t]):
                if i == 2:
                    pool.wait_ge(N["r0"], t + 1)
                if i >= 3:
                    pool.wait_ge(N["x_mm"], XB[t] + i - 2)
                nc.gpsimd.tensor_tensor(CT[i % 2][:], LT[:], over(const(f"lvl{LEVELS[i]}"), HEADS),
                                        ALU.mult).then_inc(N["ct"], 1)

        def gdn_pe(pe, t):
            for i, (src, bank) in enumerate(((Xm, 5), (CT[1], 6), (CT[0], 7))):
                pe.wait_ge(N["scaled"], 5 * t + i + 1)
                if i == 1 and t:
                    pe.wait_ge(N["o_copied"], t)
                if i == 2 and t:
                    pe.wait_ge(N["S_ready"], 4 * t + 1)
                for h in range(HEADS):
                    last = nc.tensor.transpose(psum[bank][:, hc(h)], src[:, h, :], ident)
                last.then_inc(N["tr_scaled"], 1)
            pe.wait_ge(N["scaled"], 5 * t + 4)
            pe.wait_ge(N["act_T"], 3 * t + 1)
            for h in range(HEADS):
                last = nc.tensor.transpose(psum[5][:, hc(h)], qd[:, h, :], ident)
            last.then_inc(N["tr_scaled"], 1)
            pe.wait_ge(N["scaled"], 5 * t + 5)
            pe.wait_ge(N["kbT_ready"], t + 1)
            for h in range(HEADS):
                last = nc.tensor.matmul(psum[6][:, hc(h)], gbc[:, h, :],
                                        const("cum_s" if t == 4 else "cum_p"), start=True, stop=True)
            last.then_inc(N["tr_scaled"], 1)
            pe.wait_ge(N["act_T"], 3 * t + 2)
            for h in range(HEADS):
                last = nc.tensor.matmul(psum[7][:, hc(h)], knT[:, h, :], kbT[:, h, :], start=True,
                                        stop=True)
            last.then_inc(N["kk"], 1)
            pe.wait_ge(N["act_T"], 3 * t + 3)
            for h in range(HEADS):
                last = nc.tensor.matmul(psum[5][:, hc(h)], knT[:, h, :], qnT[:, h, :], start=True,
                                        stop=True)
            last.then_inc(N["kk"], 1)
            pe.wait_ge(N["r0"], t + 1)
            if t == 4:
                pe.wait_ge(N["gls"], 1)
            for h in range(HEADS):
                last = nc.tensor.transpose(psum[6][:, hc(h)], Rm[:, h, :], ident)
            last.then_inc(N["t0"], 1)
            n = LV[t] - 1
            for l in range(1, n + 1):
                pe.wait_ge(N["ct"], CTB[t] + l + 1)
                if l == 1:
                    pe.wait_ge(N["t0c"], t + 1)
                else:
                    pe.wait_ge(N["level_upd"], UPB[t] + 2 * (l - 1))
                for h in range(HEADS):
                    last = nc.tensor.matmul(psum[7][:, hc(h)], CT[l % 2][:, h, :], Tm[:, h, :],
                                            start=True, stop=True)
                last.then_inc(N["x_mm"], 1)
                pe.wait_ge(N["x_copied"], XB[t] + l)
                if l < n:
                    for h in range(HEADS):
                        nc.tensor.matmul(psum[5][:, hc(h)], Rm[:, h, :], Xm[:, h, :], start=True,
                                         stop=True)
                for h in range(HEADS):
                    last = nc.tensor.matmul(psum[6][:, hc(h)], Xm[:, h, :], Rm[:, h, :], start=True,
                                            stop=True)
                last.then_inc(N["level_mm"], 1)
            pe.wait_ge(N["level_upd"], UPB[t + 1])
            pe.wait_ge(N["pooled"], 3 * t + 1)
            for h in range(HEADS):
                last = nc.tensor.matmul(psum[7][:, hc(h)], kbg[:, h, :], Rm[:, h, :], start=True,
                                        stop=True)
            last.then_inc(N["w_mm"], 1)
            pe.wait_ge(N["nw"], t + 1)
            pe.wait_ge(N["pooled"], 3 * t + 3)

        def gdn_state_pe(pe, t):
            pe.wait_ge(N["S_ready"], 4 * t + 1)
            if t:
                pe.wait_ge(N["S_ready"], 4 * t + 1)
            for h in range(HEADS):
                nc.tensor.matmul(psum[5][:, hc(h)], Rm[:, h, :], tok[:, t, 8 + h, :], start=True,
                                 stop=False)
                last = nc.tensor.matmul(psum[5][:, hc(h)], nwT[:, h, :], S_p[:, h, :], start=False,
                                        stop=True)
            last.then_inc(N["u_mm"], 1)
            pe.wait_ge(N["u_copied"], t + 1)
            for h in range(HEADS):
                nc.tensor.matmul(psum[6][:, hc(h)], qdT[:, h, :], S_p[:, h, :], start=True,
                                 stop=False)
                last = nc.tensor.matmul(psum[6][:, hc(h)], QKT[:, h, :], u_sb[:, h, :], start=False,
                                        stop=True)
            last.then_inc(N["o_mm"], 1)
            for h in range(HEADS):
                last = nc.tensor.matmul(psum[7][:, hc(h)], kd[:, h, :], u_sb[:, h, :], start=True,
                                        stop=True)
            last.then_inc(N["o_mm"], 1)

        def diag(t):
            flat = t[:].rearrange("p b c -> p (b c)")
            full = bass.AP(tensor=flat.tensor, offset=flat.offset,
                           ap=[flat.ap[0], [P + STEP, STREAMS], [1, STEP]])
            return full

        def streams_sync(sp):
            st = io["state_gdn"][0]
            for h in range(HEADS):
                if h:
                    sp.wait_ge(N["ss_stored"], 16 * h)
                sp.dma_start(S_s[:], st[:, h].rearrange("b k v -> k b v")).then_inc(N["ss_loaded"], 16)
                sp.wait_ge(N["ss_ready"], 3 * h + 3)
                sp.dma_start(io["gdn_sample"][0][:, h].rearrange("b k v -> k b v"), S_s[:])\
                    .then_inc(N["ss_stored"], 16)

        def streams_pe(pe):
            t = 4
            for h in range(HEADS):
                pe.wait_ge(N["exp_ready"], 2 * h + 2)
                pe.wait_ge(N["ss_loaded"], 16 * (h + 1))
                if h:
                    pe.wait_ge(N["ss_ready"], 3 * h)
                nc.tensor.matmul(psum[5][:, hc(h)], Rm[:, h, :], tok[:, t, 8 + h, :], start=True,
                                 stop=False)
                for b in range(STREAMS):
                    last = nc.tensor.matmul(psum[5][:, hc(h)], w_exp[:, b, :], S_s[:, b, :],
                                            start=False, stop=b == STREAMS - 1)
                last.then_inc(N["u4_mm"], 1)
                pe.wait_ge(N["ue_ready"], 2 * h + 2)
                if h:
                    pe.wait_ge(N["oc4"], h)
                for b in range(STREAMS):
                    nc.tensor.matmul(psum[6][:, hc(h)], qd_exp[:, b, :], S_s[:, b, :], start=b == 0,
                                     stop=False)
                nc.tensor.matmul(psum[6][:, hc(h)], QKT[:, h, :], u_sb[:, h, :], start=False,
                                 stop=True)
                for half in range(2):
                    last = nc.tensor.matmul(psum[7 - 2 * half], kd[:, h, :],
                                            u_exp[:, 4 * half:4 * half + 4, :], start=True, stop=True)
                last.then_inc(N["o4_mm"], 1)

        def streams_act(act):
            for h in range(HEADS):
                act.wait_ge(N["o4_mm"], h + 1)
                nc.scalar.activation(tok[:, 4, h, :], psum[6][:, hc(h)], ACT.Copy)\
                    .then_inc(N["oc4"], 1)

        def streams_dve(dve):
            dve.wait_ge(N["level_upd"], UPB[5])
            V.memset(w_exp[:], 0.0).then_inc(N["zero_exp"], 1)
            V.memset(qd_exp[:], 0.0).then_inc(N["zero_exp"], 1)
            dve.wait_ge(N["zero_exp"], 2)
            dve.wait_ge(N["nw"], 5)
            for h in range(HEADS):
                if h:
                    dve.wait_ge(N["o4_mm"], h)
                V.tensor_copy(diag(w_exp), nwT[:, h, :].rearrange("p (b s) -> p b s", s=STEP))\
                    .then_inc(N["exp_ready"], 1)
                V.tensor_copy(diag(qd_exp), qdT[:, h, :].rearrange("p (b s) -> p b s", s=STEP))\
                    .then_inc(N["exp_ready"], 1)
                dve.wait_ge(N["u4_mm"], h + 1)
                V.tensor_copy(u_sb[:, h, :], psum[5][:, hc(h)]).then_inc(N["ue_ready"], 1)
                dve.wait_ge(N["ue_ready"], 2 * h + 1)
                V.tensor_tensor(u_exp[:], over(u_sb[:, h, :], STREAMS), bc(const("rowmask"), P),
                                ALU.mult).then_inc(N["ue_ready"], 1)
                dve.wait_ge(N["o4_mm"], h + 1)
                V.tensor_tensor(S_s[:], S_s[:], bc(gls[:, h, :], P), ALU.mult)\
                    .then_inc(N["ss_ready"], 1)
                dve.wait_ge(N["ss_ready"], 3 * h + 1)
                for half in range(2):
                    part = S_s[:, 4 * half:4 * half + 4, :]
                    V.tensor_tensor(part, part, b4(7 - 2 * half), ALU.add)\
                        .then_inc(N["ss_ready"], 1)

        def gdn_out_dve(dve):
            o4 = tok[:, :, 0:4, :]
            dve.wait_ge(N["og_act"], TT)
            ssum = gates[:, G_A].rearrange("p t h -> p (t h)")
            link(dve, "og_chain", 1, V.tensor_reduce(
                ssum, o_sq[:].rearrange("p t (h d) -> p (t h) d", d=P), AX.X, ALU.add))
            link(dve, "og_chain", 2, V.tensor_scalar(gt(G_B), gt(G_A), 1.0 / P, EPS, ALU.mult,
                                                     ALU.add))
            V.reciprocal(gt(G_C), gt(G_B)).then_inc(N["og_chain"], 1)
            dve.wait_ge(N["og_act"], TT + 1)
            for t in range(TT):
                n = 3 + 2 * t
                o = tok[:, t, 0:4, :]
                link(dve, "og_chain", n + 1, V.tensor_tensor(o, o, bc(gates[:, G_D, t, :], P),
                                                             ALU.mult))
                link(dve, "og_chain", n + 2, V.tensor_tensor(o, o, over(gdn_gain[:], HEADS),
                                                             ALU.mult))
                zt = z[:, t, :].rearrange("p (h d) -> p h d", d=P)
                V.tensor_tensor(zt, zt, o, ALU.mult).then_inc(N["og_done"], 1)

        def gdn_out_act(act):
            act.wait_ge(N["o_copied"], 4)
            act.wait_ge(N["ss_ready"], 12)
            act.wait_ge(N["oc4"], 4)
            for t in range(TT):
                nc.scalar.activation(o_sq[:, t, :].rearrange("p (h d) -> p h d", d=P),
                                     tok[:, t, 0:4, :], ACT.Square).then_inc(N["og_act"], 1)
            act.wait_ge(N["og_chain"], 3)
            nc.scalar.activation(gt(G_D), gt(G_C), ACT.Sqrt).then_inc(N["og_act"], 1)

        def qkT_pe(pe):
            pe.wait_ge(N["group_evac"], 4 * TT)
            pe.wait_ge(N["qk_done"], 4)
            for n in range(2 * TT):
                w, t = n // TT, n % TT
                if n >= 4:
                    pe.wait_ge(N["qkT_copied"], QKC[n - 3])
                for h in range(HEADS):
                    last = nc.tensor.transpose(psum[n % 4][:, hc(h)],
                                               (q_tok, k_tok)[w][:, t, hc(h)], ident)
                last.then_inc(N["qkT_mm"], 1)

        QKC = [0, 1, 2, 3, 4, 6, 7, 8, 9, 10, 11]

        def qkT_act(act):
            act.wait_ge(N["qbd_zero"], 1)
            for n in range(2 * TT):
                w, t = n // TT, n % TT
                act.wait_ge(N["qkT_mm"], n + 1)
                if w == 0 and t == 4:
                    for m in range(MAPS):
                        rows = slice(DK * m, DK * m + DK)
                        nc.scalar.activation(
                            q_bd[rows, :, :, STEP * m:STEP * m + STEP].rearrange(
                                "p b h s -> p h b s"),
                            b4(n % 4)[rows].rearrange("p h (b s) -> p h b s", s=STEP), ACT.Copy)\
                            .then_inc(N["qkT_copied"], 1)
                else:
                    dst = (qT, kTn)[w][:, :, t * P:(t + 1) * P]
                    nc.scalar.activation(dst, b4(n % 4), ACT.Copy).then_inc(N["qkT_copied"], 1)

        UNITS = [(qt, h) for qt in range(4) for h in range(HEADS)]

        def att_pe(pe):
            def scores(u):
                qt, h = UNITS[u]
                n = P * (qt + 1)
                if u:
                    pe.wait_ge(N["probs"], 2 * u)
                for m in range(MAPS):
                    rows = slice(DK * m, DK * m + DK)
                    nc.tensor.matmul(psum[m][:, 0:n], qT[rows, h, qt * P:(qt + 1) * P],
                                     kTn[rows, h, 0:n], start=True, stop=False,
                                     skip_group_check=True)
                    last = nc.tensor.matmul(psum[m][:, n - P:n], const("early_neg")[0:1, :],
                                            const("lvl64")[0:1, :], start=False, stop=True,
                                            skip_group_check=True)
                last.then_inc(N["sc_mm"], 1)

            def transposes(u):
                qt, h = UNITS[u]
                pe.wait_ge(N["pcomb"], u + 1)
                if u:
                    pe.wait_ge(N["p_copied"], u)
                for k in range(qt + 1):
                    last = nc.tensor.transpose(psum[2][:, hc(k)], pc[:, hc(k)], ident)
                last.then_inc(N["p_tr"], 1)

            def values(u):
                qt, h = UNITS[u]
                pe.wait_ge(N["p_copied"], u + 1)
                if u:
                    pe.wait_ge(N["pv_copied"], u)
                for k in range(qt + 1):
                    last = nc.tensor.matmul(psum[3][:, 0:P], pT[:, hc(k)], v_tok[:, k, hc(h)],
                                            start=k == 0, stop=k == qt)
                last.then_inc(N["pv_mm"], 1)

            pe.wait_ge(N["qkT_copied"], 11)
            scores(0)
            for u in range(len(UNITS)):
                if u + 1 < len(UNITS):
                    scores(u + 1)
                if u:
                    values(u - 1)
                transposes(u)
            values(len(UNITS) - 1)

        def att_dve(dve):
            for u, (qt, h) in enumerate(UNITS):
                n = P * (qt + 1)
                dve.wait_ge(N["sc_mm"], u + 1)
                c = 4 * u
                both = psum_all[:, 0:2, 0:n]
                link(dve, "att_chain", c + 1, V.tensor_reduce(soft[:, 0:2], both, AX.X, ALU.max))
                V.tensor_scalar(soft[:, 2:4], soft[:, 0:2], -(DK ** -0.5), None, ALU.mult)\
                    .then_inc(N["nmax"], 1)
                dve.wait_ge(N["probs"], 2 * u + 2)
                link(dve, "att_chain", c + 2, V.reciprocal(soft[:, 6:8], soft[:, 4:6]))
                link(dve, "att_chain", c + 3, V.tensor_tensor(soft[:, 8:9], soft[:, 7:8],
                                                              lam[:, 7:8], ALU.mult))
                link(dve, "att_chain", c + 4, V.tensor_scalar(pr[:, 1, 0:n], pr[:, 1, 0:n],
                                                              soft[:, 8:9], None, ALU.mult))
                if u:
                    dve.wait_ge(N["p_tr"], u)
                V.scalar_tensor_tensor(pc[:, 0:n], pr[:, 0, 0:n], soft[:, 6:7], pr[:, 1, 0:n],
                                       ALU.mult, ALU.add).then_inc(N["pcomb"], 1)
                dve.wait_ge(N["pcomb"], u + 1)

        def att_act(act):
            def copies(u):
                qt, h = UNITS[u]
                n = P * (qt + 1)
                act.wait_ge(N["p_tr"], u + 1)
                if u:
                    act.wait_ge(N["pv_mm"], u)
                nc.scalar.activation(pT[:, 0:n], psum[2][:, 0:n], ACT.Copy)\
                    .then_inc(N["p_copied"], 1)
                act.wait_ge(N["pv_mm"], u + 1)
                nc.scalar.activation(q_tok[:, qt, hc(h)], psum[3][:, 0:P], ACT.Copy)\
                    .then_inc(N["pv_copied"], 1)

            for u, (qt, h) in enumerate(UNITS):
                n = P * (qt + 1)
                act.wait_ge(N["nmax"], u + 1)
                if u:
                    act.wait_ge(N["pcomb"], u)
                for m in range(MAPS):
                    nc.scalar.activation(pr[:, m, 0:n], psum[m][:, 0:n], ACT.Exp,
                                         bias=soft[:, 2 + m:3 + m], scale=DK ** -0.5,
                                         accum_out=soft[:, 4 + m:5 + m]).then_inc(N["probs"], 1)
                if u:
                    copies(u - 1)
            copies(len(UNITS) - 1)

        def cache_sync(sp):
            ck = io["cache_k"][0].rearrange("b (k p) h m d -> b p k (h m d)", p=P)
            cv = io["cache_v"][0].rearrange("b (k p) h d -> b p k (h d)", p=P)
            sp.wait_ge(N["group_step"], 4 * KT)
            sp.wait_ge(N["qkT_mm"], 2 * TT)
            sp.wait_ge(N["kv_stored"], 64)
            for b in range(STREAMS):
                if b >= 2:
                    sp.wait_ge(N["kt_mm"], 4 * (b - 1))
                sp.dma_start(K_c[b % 2][:], ck[b]).then_inc(s_K[b % 2], 16)
                if b:
                    sp.wait_ge(N["spv_mm"], b)
                sp.dma_start(V_c[:], cv[b]).then_inc(s_V, 16)
                sp.dma_start(V_n[:], v_tok[STEP * b:STEP * b + STEP, 4, :]).then_inc(s_V, 16)

        def cache_pe(pe):
            def keys(b):
                pe.wait_ge(s_K[b % 2], 16 * (b // 2 + 1))
                for h in range(HEADS):
                    n = 4 * b + h
                    if n >= 2:
                        pe.wait_ge(N["kt_copied"], n - 1)
                    for k in range(4):
                        last = nc.tensor.transpose(psum[2 + n % 2][:, hc(k)], K_c[b % 2][:, k, hc(h)],
                                                   ident)
                    last.then_inc(N["kt_mm"], 1)

            def scores(b):
                pe.wait_ge(N["kt_copied"], 4 * b + 4)
                if b:
                    pe.wait_ge(N["sp_copied"], 2 * b)
                for h in range(HEADS):
                    rows = slice(32 * h, 32 * h + 32)
                    nc.tensor.matmul(psum[0][rows, :], q_bd[:, b, h, :], KTc[:, h, :], start=True,
                                     stop=True, tile_position=(0, 32 * h))
                    last = nc.tensor.matmul(psum[1][rows, 0:STEP], q_bd[:, b, h, :],
                                            kTn[:, h, PROMPT + STEP * b:PROMPT + STEP * b + STEP],
                                            start=True, stop=True, tile_position=(0, 32 * h))
                last.then_inc(N["ssc_mm"], 1)

            def turn(b):
                pe.wait_ge(N["s_comb"], b + 1)
                for k in range(4):
                    nc.tensor.matmul(psum[0][:, hc(k)], ps[:, hc(k)], Cm[:], start=True, stop=True)
                nc.tensor.matmul(psum[1][0:STEP, 0:P], ps[:, PAST:PAST + STEP], Cm[:], start=True,
                                 stop=True).then_inc(N["sp_mm"], 1)

            def values(b):
                pe.wait_ge(N["sp_copied"], 2 * b + 2)
                pe.wait_ge(s_V, 32 * (b + 1))
                rows = slice(32 * (b // 2), 32 * (b // 2) + 32)
                for h in range(HEADS):
                    out = psum[4][rows, hc(h)]
                    for k in range(4):
                        nc.tensor.matmul(out, pT[:, P * k + 32 * h:P * k + 32 * h + 32],
                                         V_c[:, k, hc(h)], start=b % 2 == 0 and h == 0 and k == 0,
                                         stop=False, skip_group_check=True,
                                         tile_position=(0, 32 * (b // 2)))
                    last = nc.tensor.matmul(out, pTn[:, 32 * h:32 * h + 32], V_n[:, hc(h)],
                                            start=False, stop=True, skip_group_check=True,
                                            tile_position=(0, 32 * (b // 2)))
                last.then_inc(N["spv_mm"], 1)

            pe.wait_ge(N["pv_copied"], 16)
            keys(0)
            scores(0)
            for b in range(STREAMS):
                if b + 1 < STREAMS:
                    keys(b + 1)
                turn(b)
                values(b)
                if b + 1 < STREAMS:
                    scores(b + 1)

        def cache_act(act):
            def keys(b):
                for h in (0, 2):
                    act.wait_ge(N["kt_mm"], 4 * b + h + 1)
                    if h == 0 and b:
                        act.wait_ge(N["ssc_mm"], b)
                    act.wait_ge(N["kt_copied"], 4 * b + h)
                    nc.scalar.activation(KTc[:, h, :], psum[2 + h % 2], ACT.Copy)\
                        .then_inc(N["kt_copied"], 1)

            keys(0)
            for b in range(STREAMS):
                act.wait_ge(N["s_nmax"], b + 1)
                if b:
                    act.wait_ge(N["sp_mm"], b)
                nc.scalar.activation(ps[:], psum_flat[:, 0:PAST + STEP], ACT.Exp, bias=soft[:, 10:11],
                                     scale=DK ** -0.5, accum_out=soft[:, 11:12])\
                    .then_inc(N["s_probs"], 1)
                if b + 1 < STREAMS:
                    keys(b + 1)
                act.wait_ge(N["sp_mm"], b + 1)
                if b:
                    act.wait_ge(N["spv_mm"], b)
                nc.scalar.activation(pT[:], psum[0], ACT.Copy).then_inc(N["sp_copied"], 1)
                nc.scalar.activation(pTn[:], psum[1][0:STEP, 0:P], ACT.Copy)\
                    .then_inc(N["sp_copied"], 1)
            act.wait_ge(N["spv_mm"], STREAMS)
            nc.scalar.activation(q_tok[:, 4, :], psum[4], ACT.Copy).then_inc(N["pv_copied"], 1)

        def cache_dve(dve):
            def keys(b):
                for h in (1, 3):
                    dve.wait_ge(N["kt_mm"], 4 * b + h + 1)
                    if b:
                        dve.wait_ge(N["ssc_mm"], b)
                    dve.wait_ge(N["kt_copied"], 4 * b + h)
                    V.tensor_copy(KTc[:, h, :], psum[2 + h % 2]).then_inc(N["kt_copied"], 1)

            keys(0)
            c = 4 * len(UNITS)
            for b in range(STREAMS):
                dve.wait_ge(N["ssc_mm"], b + 1)
                link(dve, "att_chain", c + 3 * b + 1,
                     V.tensor_reduce(soft[:, 9:10], psum_flat[:, 0:PAST + STEP], AX.X, ALU.max))
                V.tensor_scalar(soft[:, 10:11], soft[:, 9:10], -(DK ** -0.5), None, ALU.mult)\
                    .then_inc(N["s_nmax"], 1)
                if b + 1 < STREAMS:
                    keys(b + 1)
                dve.wait_ge(N["s_probs"], b + 1)
                link(dve, "att_chain", c + 3 * b + 2, V.reciprocal(soft[:, 12:13], soft[:, 11:12]))
                link(dve, "att_chain", c + 3 * b + 3,
                     V.tensor_tensor(soft[:, 13:14], soft[:, 12:13], lam[:, 6:7], ALU.mult))
                V.tensor_scalar(Cm[:], const(f"sel{b % 2}"), soft[:, 13:14], None, ALU.mult)\
                    .then_inc(N["s_comb"], 1)

        def diff_out_act(act):
            act.wait_ge(N["pv_copied"], 17)
            act.wait_ge(N["spv_mm"], STREAMS)
            for t in range(TT):
                nc.scalar.activation(od_sq[:, t, :], q_tok[:, t, :], ACT.Square)\
                    .then_inc(N["od_act"], 1)
            act.wait_ge(N["od_chain"], 3)
            nc.scalar.activation(gt(G_SSQ), gt(G_SSK), ACT.Sqrt).then_inc(N["od_act"], 1)

        def diff_out_dve(dve):
            dve.wait_ge(N["od_act"], TT)
            link(dve, "od_chain", 1, V.tensor_reduce(
                gates[:, G_RQ].rearrange("p t h -> p (t h)"),
                od_sq[:].rearrange("p t (h d) -> p (t h) d", d=P), AX.X, ALU.add))
            link(dve, "od_chain", 2, V.tensor_scalar(gt(G_RK), gt(G_RQ), 1.0 / P, EPS, ALU.mult,
                                                     ALU.add))
            V.reciprocal(gt(G_SSK), gt(G_RK)).then_inc(N["od_chain"], 1)
            dve.wait_ge(N["od_act"], TT + 1)
            link(dve, "od_chain", 4, V.tensor_scalar(gt(G_E), gt(G_SSQ), 1.0 - LAM_INIT, None,
                                                     ALU.mult))
            for t in range(TT):
                o = q_tok[:, t, :].rearrange("p (h d) -> p h d", d=P)
                link(dve, "od_chain", 5 + t, V.tensor_tensor(o, o, bc(gates[:, G_E, t, :], P),
                                                             ALU.mult))
                V.tensor_tensor(o, o, over(diff_gain[:], HEADS), ALU.mult).then_inc(N["od_done"], 1)

        def wout_sync(sp):
            sp.wait_ge(N["og_done"], TT)
            sp.wait_ge(N["S_stored"], 16)
            sp.wait_ge(N["ss_stored"], 16 * HEADS)
            for half, dst in enumerate((raw_o, raw_o1)):
                sp.dma_start(dst[:], w_out[:, :, half * BANK:(half + 1) * BANK])\
                    .then_inc(s_wo[half], 16)
            sp.dma_start(x_tok[:, 0:4, :], x_mid[0:PROMPT, :].rearrange("(t p) c -> p t c", p=P))\
                .then_inc(N["x_back"], 16)
            sp.dma_start(x_tok[:, 4, :], x_mid[PROMPT:TOK, :]).then_inc(N["x_back"], 16)
            sp.wait_ge(N["od_done"], TT)
            sp.dma_start(gain[:], io["ffn2_norm"].to_broadcast([P, D])).then_inc(s_gain[2], 16)

        def wout_act(act):
            for n in range(2 * KT):
                half, k = n // KT, n % KT
                act.wait_ge(s_wo[half], 16)
                if n >= 2:
                    act.wait_ge(N["wo_step"], n - 1)
                nc.scalar.activation(o_hi[:, n % 2], (raw_o, raw_o1)[half][:, k, :], ACT.Copy)\
                    .then_inc(N["wo_hi"], 1)

        def wout_dve(dve):
            for n in range(2 * KT):
                half, k = n // KT, n % KT
                dve.wait_ge(N["wo_hi"], n + 1)
                V.tensor_tensor(o_lo[:, n % 2], (raw_o, raw_o1)[half][:, k, :], raw(o_hi[:, n % 2]),
                                ALU.subtract).then_inc(N["wo_lo"], 1)
                if n == KT + 1:
                    dve.wait_ge(N["x_back"], 32)
                    for t in range(TT):
                        wout_residual(dve, 0, t)
            for t in range(TT):
                wout_residual(dve, 1, t)

        def wout_residual(dve, half, t):
            dve.wait_ge(N["wo_step"], (half + 1) * KT)
            cols = x_tok[:, t, half * BANK:(half + 1) * BANK]
            V.tensor_tensor(cols, psum[(half * TT + t) % 8], cols, ALU.add).then_inc(N["wo_res"], 1)

        def wout_pe(pe):
            pe.wait_ge(*on.lo(2 * TT))
            for n in range(2 * KT):
                half, k = n // KT, n % KT
                pe.wait_ge(N["wo_lo"], n + 1)
                for t in range(TT):
                    c = slice(t * P, (t + 1) * P)
                    if k == 0 and half == 1 and (TT + t) % 8 < TT:
                        pe.wait_ge(N["wo_res"], (TT + t) % 8 + 1)
                    last = three(psum[(half * TT + t) % 8], hT_hi[:, k, c], hT_lo[:, k, c],
                                 o_hi[:, n % 2], o_lo[:, n % 2], k == 0, k == KT - 1)
                last.then_inc(N["wo_step"], 1)

        s_wo = [sem(f"w_out_loaded{i}") for i in range(2)]
        psum_flat = psum_all[:].rearrange("p b c -> p (b c)")
        gls = small.put("stream_decay", [P, HEADS, STREAMS])

        block = ctx.enter_context(nc.Block())

        @block.sync
        def _(sp):
            sp.dma_start(x_tok[:, 0:4, :], io["x_prompt"][0].rearrange("(t p) c -> p t c", p=P))\
                .then_inc(s_x, 16)
            sp.dma_start(x_tok[:, 4, :], io["x_sample"].rearrange("b s c -> (b s) c"))\
                .then_inc(s_x, 16)
            sp.dma_start(consts[:], io["consts"]).then_inc(s_const, 16)
            sp.dma_start(gain[:], io["ffn1_norm"].to_broadcast([P, D])).then_inc(s_gain[0], 16)
            ffn_sync(sp, f1, io["ffn1_w_gu"][0], io["ffn1_w_down"][0])
            sp.wait_ge(*f1.dlo(4 + 0))
            sp.wait_ge(*f1.mm(2 * FT))
            sp.dma_start(gain[:], io["mix_norm"].to_broadcast([P, D])).then_inc(s_gain[1], 16)
            conv_sync(sp)
            cache_sync(sp)
            streams_sync(sp)
            wout_sync(sp)
            ffn_sync(sp, f2, io["ffn2_w_gu"][0], io["ffn2_w_down"][0], N["wo_res"])
            sp.wait_ge(*f2.res(2 * TT))
            sp.dma_start(io["y_prompt"][0].rearrange("(t p) c -> p t c", p=P), x_tok[:, 0:4, :])\
                .then_inc(s_y, 16)
            sp.dma_start(io["y_sample"].rearrange("b s c -> (b s) c"), x_tok[:, 4, :])\
                .then_inc(s_y, 16)
            sp.wait_ge(s_y, 32)

        @block.gpsimd
        def _(pool):
            pool.wait_ge(N["tail_rows"], 3)
            pool.dma_start(io["conv_prompt"][0, 0], conv_out[0:3, :]).then_inc(N["tail_stored"], 16)
            pool.dma_start(io["conv_sample"][0].rearrange("b w c -> (b w) c"), conv_out[3:27, :])\
                .then_inc(N["tail_stored"], 16)
            pool.wait_ge(N["group_step"], 4 * KT)
            nc.gpsimd.memset(q_bd[:], 0.0).then_inc(N["qbd_zero"], 1)
            pool.wait_ge(N["qk_done"], 4)
            pool.wait_ge(N["group_evac"], 4 * TT)
            for name, src in (("k", k_tok), ("v", v_tok)):
                dims = "t h m d" if name == "k" else "t h d"
                flat = "(t p) h m d -> p t (h m d)" if name == "k" else "(t p) h d -> p t (h d)"
                pool.dma_start(io[f"{name}_prompt"][0, 0].rearrange(flat, p=P), src[:, 0:4, :])\
                    .then_inc(N["kv_stored"], 16)
                flat = "b s h m d -> (b s) (h m d)" if name == "k" else "b s h d -> (b s) (h d)"
                pool.dma_start(io[f"{name}_sample"][0].rearrange(flat), src[:, 4, :])\
                    .then_inc(N["kv_stored"], 16)
            pool.wait_ge(N["x_spilled"], 32)
            for t in range(TT):
                gdn_pool(pool, t)
                if t == 3:
                    pool.wait_ge(N["S_ready"], 17)
                    pool.dma_start(io["gdn_prompt"][0, 0].rearrange("h k v -> k h v"), S_p[:])\
                        .then_inc(N["S_stored"], 16)
            pool.wait_ge(N["S_stored"], 16)
            pool.wait_ge(N["ss_stored"], 16 * HEADS)

        @block.scalar
        def _(act):
            norm_act(act, f1.n, lambda e, t: e.wait_ge(s_x, 32) if t == 0 else None)
            ffn_act(act, f1)
            norm_act(act, mn, lambda e, t: e.wait_ge(*f1.res(6 + t)))
            conv_act(act)
            group_act(act)
            qk_act(act)
            tok_act(act)
            gate_act(act)
            qkT_act(act)
            att_act(act)
            cache_act(act)
            for t in range(TT):
                gdn_act(act, t)
            streams_act(act)
            gdn_out_act(act)
            diff_out_act(act)
            split_act(act, on)
            wout_act(act)
            norm_act(act, f2.n, lambda e, t: e.wait_ge(N["wo_res"], 6 + t))
            ffn_act(act, f2)

        @block.vector
        def _(dve):
            dve.wait_ge(s_gain[0], 16)
            norm_dve(dve, f1.n)
            ffn_dve(dve, f1)
            dve.wait_ge(s_gain[1], 16)
            norm_dve(dve, mn)
            dve.wait_ge(*mn.lo(2 * TT))
            conv_dve(dve)
            dve.wait_ge(N["ba_product"], 1)
            V.tensor_copy(ba[:], psum[0][:, 0:40].rearrange("p (t c) -> p t c", c=8))\
                .then_inc(N["ba_copied"], 1)
            group_dve(dve)
            qk_dve(dve)
            tok_dve(dve)
            dve.wait_ge(N["tok_sums"], 2 * TT)
            gate_dve(dve)
            att_dve(dve)
            cache_dve(dve)
            dve.wait_ge(N["x_spilled"], 32)
            V.memset(S_p[:], 0.0).then_inc(N["S_ready"], 1)
            for t in range(TT):
                gdn_dve(dve, t)
                if t < 4:
                    gdn_state_dve(dve, t)
            streams_dve(dve)
            gdn_out_dve(dve)
            diff_out_dve(dve)
            for t in range(TT):
                split_dve(dve, on, t)
            wout_dve(dve)
            dve.wait_ge(s_gain[2], 16)
            norm_dve(dve, f2.n)
            ffn_dve(dve, f2)

        @block.tensor
        def _(pe):
            pe.wait_ge(s_const, 16)
            norm_pe(pe, f1.n)
            ffn_pe(pe, f1)
            norm_pe(pe, mn)
            conv_pe(pe)
            group_pe(pe)
            tok_pe(pe)
            gate_pe(pe)
            qkT_pe(pe)
            att_pe(pe)
            cache_pe(pe)
            for t in range(TT):
                gdn_pe(pe, t)
                if t < 4:
                    gdn_state_pe(pe, t)
            streams_pe(pe)
            norm_pe(pe, on, lambda t, c: (z if c < BANK else q_tok)[:, t, c % BANK:c % BANK + P],
                    lambda e, t, half: e.wait_ge(N["od_done" if half else "og_done"], t + 1))
            wout_pe(pe)
            norm_pe(pe, f2.n)
            ffn_pe(pe, f2)


INPUTS = """x_prompt x_sample cache_k cache_v state_gdn state_conv ffn1_norm ffn1_w_gu ffn1_w_down
    mix_norm w_in conv_w a_log dt_bias gdn_out_norm q_norm k_norm lambda_q lambda_k diff_out_norm
    w_out ffn2_norm ffn2_w_gu ffn2_w_down""".split()
OUTPUTS = {
    "y_prompt": (1, PROMPT, D), "y_sample": (STREAMS, STEP, D),
    "k_prompt": (1, 1, PROMPT, HEADS, MAPS, DK), "v_prompt": (1, 1, PROMPT, HEADS, P),
    "gdn_prompt": (1, 1, HEADS, P, P), "conv_prompt": (1, 1, 3, CONV_T * P),
    "k_sample": (1, STREAMS, STEP, HEADS, MAPS, DK), "v_sample": (1, STREAMS, STEP, HEADS, P),
    "gdn_sample": (1, STREAMS, HEADS, P, P), "conv_sample": (1, STREAMS, 3, CONV_T * P),
}


def kernel(**inputs):
    from concourse import bacc
    from concourse.bass_utils import run_bass_kernel_spmd

    nc = bacc.Bacc("TRN2", target_bir_lowering=False, num_devices=1)
    arrays, io = {}, {}
    consts, rotary = constants()
    for name, a in [(n, inputs[n]) for n in INPUTS] + [("consts", consts), ("rotary", rotary)]:
        a = np.ascontiguousarray(a)
        arrays[name] = a
        io[name] = nc.dram_tensor(name, a.shape, mybir.dt.from_np(a.dtype), kind="ExternalInput").ap()
    for name, shape in OUTPUTS.items():
        io[name] = nc.dram_tensor(name, shape, F32, kind="ExternalOutput").ap()
    build(nc, io)
    r = run_bass_kernel_spmd(nc, [arrays], core_ids=[0])
    return tuple(r.results[0][name] for name in OUTPUTS)
```

```python
import math
from contextlib import ExitStack

import numpy as np

import concourse.bass as bass
from concourse import mybir

F32 = mybir.dt.float32
F32R = mybir.dt.float32r
ALU = mybir.AluOpType
ACT = mybir.ActivationFunctionType
AX = mybir.AxisListType

P = 128
D = 1024
KT = D // P
PROMPT = 512
STREAMS, STEP = 8, 16
TOK = PROMPT + STREAMS * STEP
TT = TOK // P
FF = 2816
FT = FF // P
HALF = TOK // 2
EPS = 1e-6
BANK = 512

ARENA = 16640
ARENA_END = 229368


IN_COLS = 3592
HEADS = 4
DK = 64
MAPS = 2
CONV_T = 12
BA_COL, Z_COL = 1536, 1544
PAST = 512
LAM_INIT = 0.8 - 0.6 * math.exp(0.0)
NEG = -1e30
LEVELS = [1, 2, 4, 8, 16, 32, 64]


def const_layout():
    widths = [("ident", P), ("ones", P), ("cum_p", P), ("cum_s", P), ("blk_s", P)]
    widths += [(f"lvl{n}", P) for n in LEVELS]
    widths += [("sel0", P), ("sel1", P), ("rowmask", STREAMS), ("map0", 1), ("map1", 1), ("early_neg", P)]
    at, out = 0, {}
    for name, w in widths:
        out[name] = (at, w)
        at += w
    return out, at


CONST, CONST_COLS = const_layout()


def constants():
    c = np.zeros((P, CONST_COLS), np.float32)

    def put(name, a):
        at, w = CONST[name]
        c[:, at:at + w] = a

    i = np.arange(P)
    row, col = i[:, None], i[None, :]
    put("ident", row == col)
    put("ones", 1.0)
    same = row // STEP == col // STEP
    put("cum_p", row <= col)
    put("cum_s", (row <= col) & same)
    put("blk_s", same)
    for n in LEVELS:
        put(f"lvl{n}", (row // (2 * n) == col // (2 * n)) & (row // n % 2 == 0) & (col // n % 2 == 1))
    h, m, q = row // 32, row % 32 // STEP, row % STEP
    for par in range(2):
        put(f"sel{par}", col == 32 * h + STEP * par + q)
    put("rowmask", row // STEP == np.arange(STREAMS)[None, :])
    put("map0", m == 0)
    put("map1", -(m == 1).astype(np.float32))
    pos = np.concatenate([np.arange(PROMPT), PAST + np.arange(STREAMS * STEP) % STEP]).astype(np.float32)
    inv = np.float32(500000.0) ** (-np.arange(8, dtype=np.float32) * np.float32(2.0) / np.float32(16.0))
    ang = (pos[:, None] * inv[None, :]).astype(np.float32).reshape(TT, P, 8).transpose(1, 0, 2)
    put("early_neg", np.where(col < 64, NEG, 0.0))
    return c, np.concatenate([np.cos(ang).reshape(P, -1), np.sin(ang).reshape(P, -1)], 1)


class Region:

    def __init__(self, nc, start, end):
        self.nc, self.at, self.end = nc, start, end

    def put(self, name, shape, dtype=F32):
        size = 4 * int(np.prod(shape[1:]))
        size = (size + 31) // 32 * 32
        assert self.at + size <= self.end, (name, self.at + size - self.end)
        t = self.nc.alloc_sbuf_tensor_at(name, shape, dtype, offset=self.at)
        self.at += size
        return t


def raw(t):
    return t.bitcast(F32)


def build(nc, io):
    ctx = ExitStack()
    sem = lambda name: ctx.enter_context(nc.semaphore(name))
    with ctx:
        keep = Region(nc, ARENA, ARENA_END)
        x_tok = keep.put("x_tok", [P, TT, D])
        h_at = keep.at
        hT_hi = keep.put("hT_hi", [P, KT, TOK], F32R)
        hT_lo = keep.put("hT_lo", [P, KT, TOK], F32R)
        h_end = keep.at
        gain_at = keep.at
        gain = keep.put("gain", [P, D])
        x_norm = keep.put("x_norm", [P, 2, D])
        sq_junk = keep.put("sq_junk", [P, D])
        scratch_end = keep.at
        stats = keep.put("stats", [P, 4, TT])
        consts = keep.put("consts", [P, CONST_COLS])

        def const(name):
            at, w = CONST[name]
            return consts[:, at:at + w]

        ident = const("ident")
        F0 = keep.at

        ffn_mem = Region(nc, F0, ARENA_END)
        aT = ffn_mem.put("aT", [P, FT, TOK])
        ring_at = ffn_mem.at
        raw_gu = ffn_mem.put("raw_gu", [P, 2, 2, KT, P])
        gu_hi = ffn_mem.put("gu_hi", [P, 2, 2, KT, P], F32R)
        gu_lo = ffn_mem.put("gu_lo", [P, 2, 2, KT, P], F32R)
        silu_gate = ffn_mem.put("silu_gate", [P, 2, TOK])
        ring_end = ffn_mem.at
        CH = [(0, 2), (2, 6), (6, 14), (14, 22)]
        wd = [[None] * 4, [None] * 4]
        wd[0][0] = ffn_mem.put("wd00", [P, 2, BANK])
        wd[0][1] = ffn_mem.put("wd01", [P, 4, BANK])
        over_h = Region(nc, h_at, h_end)
        wd[0][2] = over_h.put("wd02", [P, 8, BANK])
        wd[0][3] = over_h.put("wd03", [P, 8, BANK])
        wd[1][1] = over_h.put("wd11", [P, 4, BANK])
        over_ring = Region(nc, ring_at, ring_end)
        wd[1][2] = over_ring.put("wd12", [P, 8, BANK])
        wd[1][3] = over_ring.put("wd13", [P, 8, BANK])
        a_hi = over_ring.put("a_hi", [P, 2, TOK], F32R)
        a_lo = over_ring.put("a_lo", [P, 2, TOK], F32R)
        wd_hi = over_ring.put("wd_hi", [P, 2, BANK], F32R)
        wd_lo = over_ring.put("wd_lo", [P, 2, BANK], F32R)
        wd[1][0] = nc.alloc_sbuf_tensor_at("wd10", [P, 2, BANK], F32, offset=over_ring.at) \
            if over_ring.at + 4096 <= ring_end else x_norm[:, 0, :].rearrange("p (a b) -> p a b", a=2)

        psum_all = ctx.enter_context(nc.psum_tensor("psum_all", [P, 8, BANK], F32))
        psum = [psum_all[:, i, :] for i in range(8)]

        s_const = sem("const_loaded")
        s_x = sem("x_loaded")
        s_gain = [sem(f"gain_loaded{i}") for i in range(3)]
        s_y = sem("y_stored")

        class Count:

            def __init__(self, of, base):
                self.sem, self.base = of, base

            def __call__(self, n):
                return self.sem, self.base + n

        norm_sems = {n: sem(f"norm_{w}") for n, w in dict(
            sq="mean_square",
            var="inverse",
            rstd="root",
            xn="scaled",
            tr="transposed",
            hi="hi",
            lo="lo").items()}
        NORM_STEPS = dict(sq=TT, var=2, rstd=1, xn=TT, tr=2 * TT, hi=2 * TT, lo=2 * TT)

        class Norm:

            def __init__(self, r):
                rounds = r - (r == 3)
                self.sq, self.var, self.rstd, self.xn = (
                    Count(norm_sems[n], NORM_STEPS[n] * rounds) for n in ("sq", "var", "rstd", "xn"))
                self.tr, self.hi, self.lo = (
                    Count(norm_sems[n], NORM_STEPS[n] * r) for n in ("tr", "hi", "lo"))

        ffn_sems = {n: sem(f"ffn_{w}") for n, w in dict(
            hi="gate_up_hi", lo="gate_up_lo",
            mm="gate_up_product",
            silu="silu",
            a="hidden",
            dhi="down_hi", dlo="down_lo",
            dmm="down_step",
            out="down_product",
            res="residual").items()}
        FFN_STEPS = dict(hi=2 * FT, lo=2 * FT, mm=2 * FT, silu=2 * FT, a=2 * FT, dhi=4 * FT,
                         dlo=4 * FT, dmm=2 * (FT - 1), out=2 * TT, res=2 * TT)
        gu_loaded = [sem(f"ffn_gate_up_loaded{i}") for i in range(2)]
        down_loaded = [[sem(f"ffn_down_loaded{h}{c}") for c in range(4)] for h in range(2)]

        class Ffn:

            def __init__(self, r, norm):
                self.n = norm
                self.w = [Count(q, 16 * FT * r) for q in gu_loaded]
                self.wd = [[Count(q, 16 * r) for q in qs] for qs in down_loaded]
                (self.hi, self.lo, self.mm, self.silu, self.a, self.dhi, self.dlo, self.dmm,
                 self.out, self.res) = (Count(ffn_sems[n], FFN_STEPS[n] * r) for n in
                                        "hi lo mm silu a dhi dlo dmm out res".split())

        f1, f2 = Ffn(0, Norm(0)), Ffn(1, Norm(3))

        def norm_act(act, s, x_ready):
            for t in range(TT):
                x_ready(act, t)
                if t:
                    act.wait_ge(*s.sq(t))
                nc.scalar.activation(sq_junk[:], x_tok[:, t, :], ACT.Square,
                                     accum_out=stats[:, 0, t:t + 1]).then_inc(s.sq.sem, 1)
            act.wait_ge(*s.var(2))
            nc.scalar.activation(stats[:, 2, :], stats[:, 1, :], ACT.Sqrt).then_inc(s.rstd.sem, 1)
            split_act(act, s)

        def split_act(act, s):
            for n in range(2 * TT):
                t, half = n // 2, n % 2
                act.wait_ge(*s.tr(n + 1))
                nc.scalar.activation(
                    hT_hi[:, 4 * half:4 * half + 4, t * P:(t + 1) * P],
                    psum[n % 4].rearrange("p (k c) -> p k c", k=4), ACT.Copy).then_inc(s.hi.sem, 1)

        def norm_dve(dve, s):
            dve.wait_ge(*s.sq(TT))
            nc.vector.tensor_scalar(stats[:, 3, :], stats[:, 0, :], 1.0 / D, EPS, ALU.mult,
                                    ALU.add).then_inc(s.var.sem, 1)
            dve.wait_ge(*s.var(1))
            nc.vector.reciprocal(stats[:, 1, :], stats[:, 3, :]).then_inc(s.var.sem, 1)
            dve.wait_ge(*s.rstd(1))

            def scale(t):
                if t >= 2:
                    dve.wait_ge(*s.tr(2 * (t - 1)))
                nc.vector.scalar_tensor_tensor(x_norm[:, t % 2, :], x_tok[:, t, :],
                                               stats[:, 2, t:t + 1], gain[:], ALU.mult,
                                               ALU.mult).then_inc(s.xn.sem, 1)

            scale(0)
            for t in range(TT):
                if t + 1 < TT:
                    scale(t + 1)
                split_dve(dve, s, t)

        def split_dve(dve, s, t):
            if True:
                for half in range(2):
                    n = 2 * t + half
                    dve.wait_ge(*s.hi(n + 1))
                    cols = (slice(None), slice(4 * half, 4 * half + 4), slice(t * P, (t + 1) * P))
                    nc.vector.tensor_tensor(
                        hT_lo[cols], psum[n % 4].rearrange("p (k c) -> p k c", k=4),
                        raw(hT_hi[cols]), ALU.subtract).then_inc(s.lo.sem, 1)

        def norm_pe(pe, s, src=lambda t, c: x_norm[:, t % 2, c:c + P], ready=None):
            for n in range(2 * TT):
                t, half = n // 2, n % 2
                if ready is not None:
                    ready(pe, t, half)
                elif half == 0:
                    pe.wait_ge(*s.xn(t + 1))
                if n >= 4:
                    pe.wait_ge(*s.lo(n - 3))
                for k in range(4):
                    c = (4 * half + k) * P
                    last = nc.tensor.transpose(psum[n % 4][:, k * P:(k + 1) * P],
                                               src(t, c), ident)
                last.then_inc(s.tr.sem, 1)

        def bank_pair(which, slot):
            b = 4 * slot + 2 * which
            return psum[b], psum[b + 1]

        def ffn_sync(sp, s, w_gu, w_down, before=None):
            gu = w_gu.rearrange("(k p) c -> p k c", p=P)
            if before is not None:
                sp.wait_ge(before, 2 * TT)

            def load(j, slot):
                for which in range(2):
                    sp.dma_start(raw_gu[:, slot, which],
                                 gu[:, :, bass.ds(which * FF + j * P, P)]).then_inc(s.w[slot].sem, 16)

            load(0, 0)
            load(1, 1)
            dn = w_down.rearrange("(k p) c -> p k c", p=P)

            def load_down(half, c):
                a, b = CH[c]
                sp.dma_start(wd[half][c][:, :, :], dn[:, a:b, half * BANK:(half + 1) * BANK])\
                    .then_inc(s.wd[half][c].sem, 16)

            with sp.Fori(1, FT // 2) as pair:
                j = 2 * pair
                for slot in range(2):
                    sp.wait_ge(*s.lo(2 * (j + slot) - 2))
                    load(j + slot, slot)
            load_down(0, 0)
            load_down(0, 1)
            sp.wait_ge(*s.mm(2 * FT))
            load_down(0, 2)
            load_down(0, 3)
            load_down(1, 0)
            load_down(1, 1)
            load_down(1, 2)
            load_down(1, 3)

        def ffn_act(act, s):
            def split(j, slot):
                if slot == 0:
                    pass
                act.wait_ge(*s.w[slot](16 * (j - slot) + 32))
                for which in range(2):
                    nc.scalar.activation(gu_hi[:, slot, which], raw_gu[:, slot, which],
                                         ACT.Copy).then_inc(s.hi.sem, 1)

            def silu(j, slot):
                for n in range(1):
                    g = bank_pair(0, slot)
                act.wait_ge(*s.mm(2 * j + 1))
                for part in range(2):
                    nc.scalar.activation(silu_gate[:, slot, part * HALF:(part + 1) * HALF],
                                         g[part][:, 0:HALF], ACT.Silu).then_inc(s.silu.sem, 1)

            split(0, 0)
            split(1, 1)
            silu(0, 0)
            with act.Fori(1, FT // 2) as pair:
                j = 2 * pair
                act.wait_ge(*s.mm(2 * j - 2))
                split(j, 0)
                act.wait_ge(*s.a(2 * j - 2))
                silu(j - 1, 1)
                act.wait_ge(*s.mm(2 * j))
                split(j + 1, 1)
                act.wait_ge(*s.a(2 * j - 2))
                silu(j, 0)
            act.wait_ge(*s.a(2 * (FT - 2)))
            silu(FT - 1, 1)

            def down_split(half, c, j, slot):
                a, _ = CH[c]
                nc.scalar.activation(a_hi[:, slot, :], aT[:, j, :], ACT.Copy).then_inc(s.dhi.sem, 1)
                nc.scalar.activation(wd_hi[:, slot, :], wd[half][c][:, j - a, :], ACT.Copy)\
                    .then_inc(s.dhi.sem, 1)

            for half in range(2):
                for c, (a, b) in enumerate(CH):
                    act.wait_ge(*s.wd[half][c](16))
                    if c == 0:
                        for slot in range(2):
                            if half == 0:
                                act.wait_ge(*s.mm(2 * FT))
                                act.wait_ge(*s.a(2 * FT))
                            elif slot == 0:
                                act.wait_ge(*s.dmm(FT - 1))
                            else:
                                act.wait_ge(*s.out(TT))
                            down_split(half, 0, slot, slot)
                        continue
                    with act.Fori(a // 2, b // 2) as pair:
                        j = 2 * pair
                        for slot in range(2):
                            act.wait_ge(*s.dmm(half * (FT - 1) + j + slot - 1))
                            down_split(half, c, j + slot, slot)

        def ffn_dve(dve, s):
            def split(j, slot):
                for which in range(2):
                    dve.wait_ge(*s.hi(2 * j + which + 1))
                    nc.vector.tensor_tensor(gu_lo[:, slot, which], raw_gu[:, slot, which],
                                            raw(gu_hi[:, slot, which]), ALU.subtract)\
                        .then_inc(s.lo.sem, 1)

            def hidden(j, slot):
                dve.wait_ge(*s.mm(2 * j + 2))
                u = bank_pair(1, slot)
                for part in range(2):
                    dve.wait_ge(*s.silu(2 * j + part + 1))
                    nc.vector.tensor_tensor(aT[:, j, part * HALF:(part + 1) * HALF],
                                            silu_gate[:, slot, part * HALF:(part + 1) * HALF],
                                            u[part][:, 0:HALF], ALU.mult).then_inc(s.a.sem, 1)

            split(0, 0)
            split(1, 1)
            hidden(0, 0)
            with dve.Fori(1, FT // 2) as pair:
                j = 2 * pair
                split(j, 0)
                hidden(j - 1, 1)
                split(j + 1, 1)
                hidden(j, 0)
            hidden(FT - 1, 1)

            def down_split(half, c, j, slot):
                a, _ = CH[c]
                n = 2 * (half * FT + j)
                dve.wait_ge(*s.dhi(n + 1))
                nc.vector.tensor_tensor(a_lo[:, slot, :], aT[:, j, :], raw(a_hi[:, slot, :]),
                                        ALU.subtract).then_inc(s.dlo.sem, 1)
                dve.wait_ge(*s.dhi(n + 2))
                nc.vector.tensor_tensor(wd_lo[:, slot, :], wd[half][c][:, j - a, :],
                                        raw(wd_hi[:, slot, :]), ALU.subtract).then_inc(s.dlo.sem, 1)

            for half in range(2):
                for c, (a, b) in enumerate(CH):
                    with dve.Fori(a // 2, b // 2) as pair:
                        j = 2 * pair
                        for slot in range(2):
                            down_split(half, c, j + slot, slot)
                    if half == 1 and c == 0:
                        for t in range(TT):
                            residual(dve, s, 0, t)
            for t in range(TT):
                residual(dve, s, 1, t)

        def residual(dve, s, half, t):
            dve.wait_ge(*s.out(half * TT + t + 1))
            cols = x_tok[:, t, half * BANK:(half + 1) * BANK]
            nc.vector.scalar_tensor_tensor(cols, psum[(half * TT + t) % 8], 0.5, cols,
                                           ALU.mult, ALU.add).then_inc(s.res.sem, 1)

        def three(out, lhs_hi, lhs_lo, rhs_hi, rhs_lo, start, stop):
            nc.tensor.matmul(out, lhs_hi, rhs_hi, start=start, stop=False, skip_group_check=True)
            nc.tensor.matmul(out, lhs_hi, rhs_lo, start=False, stop=False, skip_group_check=True)
            return nc.tensor.matmul(out, lhs_lo, rhs_hi, start=False, stop=stop,
                                    skip_group_check=True)

        def ffn_pe(pe, s):
            def gate_up(j, slot):
                for which in range(2):
                    for k in range(KT):
                        for part in range(2):
                            tok = slice(part * HALF, (part + 1) * HALF)
                            last = three(bank_pair(which, slot)[part][:, 0:HALF],
                                         gu_hi[:, slot, which, k, :], gu_lo[:, slot, which, k, :],
                                         hT_hi[:, k, tok], hT_lo[:, k, tok], k == 0, k == KT - 1)
                    last.then_inc(s.mm.sem, 1)

            pe.wait_ge(*s.n.lo(2 * TT))
            for slot in range(2):
                pe.wait_ge(*s.lo(2 * slot + 2))
                gate_up(slot, slot)
            with pe.Fori(1, FT // 2) as pair:
                j = 2 * pair
                for slot in range(2):
                    pe.wait_ge(*s.lo(2 * (j + slot) + 2))
                    pe.wait_ge(*s.a(2 * (j + slot) - 2))
                    gate_up(j + slot, slot)

            def down(half, j, slot, start, stop):
                pe.wait_ge(*s.dlo(2 * (half * FT + j) + 2))
                for t in range(TT):
                    if start and half == 1 and (TT + t) % 8 < TT:
                        pe.wait_ge(*s.res((TT + t) % 8 + 1))
                    tok = slice(t * P, (t + 1) * P)
                    last = three(psum[(half * TT + t) % 8], a_hi[:, slot, tok],
                                 a_lo[:, slot, tok], wd_hi[:, slot, :], wd_lo[:, slot, :],
                                 start, stop)
                    if stop:
                        last.then_inc(s.out.sem, 1)
                return last

            pe.wait_ge(*s.a(2 * FT))
            for half in range(2):
                for slot in range(2):
                    down(half, slot, slot, slot == 0, False).then_inc(s.dmm.sem, 1)
                with pe.Fori(1, FT // 2 - 1) as pair:
                    j = 2 * pair
                    for slot in range(2):
                        down(half, j + slot, slot, False, False).then_inc(s.dmm.sem, 1)
                down(half, FT - 2, 0, False, False).then_inc(s.dmm.sem, 1)
                down(half, FT - 1, 1, False, True)

        small = Region(nc, gain_at, scratch_end)
        xp = small.put("xp", [P, 2, 668])
        sq_rows = [nc.alloc_sbuf_tensor_at(f"sq_rows{i}", [P, BANK], F32, offset=gain_at + 2048 * i)
                   for i in range(2)]
        rope_tmp = small.put("rope_tmp", [P, 4, TT * 64])
        rot = small.put("rot", [P, 2, TT, 8])
        gdn_gain = small.put("gdn_gain", [P, P])
        diff_gain = small.put("diff_gain", [P, P])
        qk_gain = small.put("qk_gain", [P, 2, DK])
        lam_in = small.put("lam_in", [P, 2, 2, DK])
        head_par = small.put("head_par", [P, 2, HEADS])
        gates = small.put("gates", [P, 20, TT, HEADS])
        ba = small.put("ba", [P, TT, 8])
        lam = small.put("lam", [P, 8])
        qk_ss = small.put("qk_ss", [P, 2, 3, TT * 8])
        soft = small.put("soft", [P, 16])

        mixm = Region(nc, F0, ARENA_END)
        z = mixm.put("z", [P, TT, BANK])
        q_tok = mixm.put("q_tok", [P, TT, BANK])
        k_at = mixm.at
        k_tok = mixm.put("k_tok", [P, TT, BANK])
        v_at = mixm.at
        v_tok = mixm.put("v_tok", [P, TT, BANK])
        tok_at = mixm.at
        tok = mixm.put("tok", [P, TT, CONV_T, P])
        c_at = mixm.at
        cT = mixm.put("cT", [P, CONV_T, TOK])
        c_end = d_at = mixm.at
        raw_cv = mixm.put("raw_cv", [P, 2, KT, P])
        cv_hi = mixm.put("cv_hi", [P, 2, KT, P], F32R)
        cv_lo = mixm.put("cv_lo", [P, 2, KT, P], F32R)
        d_end = mixm.at
        kb_mem = Region(nc, k_at, v_at)
        hist = kb_mem.put("hist", [P, CONV_T, 28])
        tail = kb_mem.put("tail", [P, CONV_T, 27])
        vb_mem = Region(nc, v_at, tok_at)
        conv_out = vb_mem.put("conv_out", [27, CONV_T * P])
        baT = vb_mem.put("baT", [8, TOK])
        conv_rows = Region(nc, tok_at, c_at).put("conv_rows", [28, CONV_T * P])
        dm = Region(nc, d_at, d_end)
        raw_b = dm.put("raw_b", [P, 2, 4, BANK])
        b_hi = dm.put("b_hi", [P, 2, BANK], F32R)
        b_lo = dm.put("b_lo", [P, 2, BANK], F32R)

        g1 = Region(nc, ARENA, h_at)
        H4 = [P, HEADS, P]
        qd, knT, kbT, qnT, kbg, kd, qdT, LT, QKT = (
            g1.put(n, H4) for n in "qd knT kbT qnT kbg kd qdT LT QKT".split())
        g2 = Region(nc, c_at, c_end)
        Rm, nwT, u_sb, S_p = (g2.put(n, H4) for n in "Rm nwT u_sb S_p".split())
        tx_at = g2.at
        Tm, Xm = g2.put("Tm", H4), g2.put("Xm", H4)
        ct_at = g2.at
        CT = [g2.put(f"CT{i}", H4) for i in range(2)]
        u_exp = nc.alloc_sbuf_tensor_at("u_exp", [P, STREAMS, P], F32, offset=ct_at)
        ge_at = g2.at
        gbc, ET = g2.put("gbc", H4), g2.put("ET", H4)
        wide = lambda name, at: nc.alloc_sbuf_tensor_at(name, [P, STREAMS, P], F32, offset=at)
        qd_exp = [wide("qd_exp0", ge_at), wide("qd_exp1", tx_at)]
        S_s = [g2.put("S_s0", [P, STREAMS, P]), wide("S_s1", ARENA)]
        w_exp = [g2.put("w_exp0", [P, STREAMS, P]), wide("w_exp1", ARENA + 4096)]
        o_sq = nc.alloc_sbuf_tensor_at("o_sq", [P, TT, BANK], F32, offset=ARENA + 8192)

        a1 = Region(nc, h_at, h_end)
        qT = a1.put("qT", [P, HEADS, PROMPT])
        kTn = a1.put("kTn", [P, HEADS, TOK])
        q_bd = a1.put("q_bd", [P, STREAMS, HEADS, 32])
        KTc = a1.put("KTc", [P, HEADS, PAST])
        pc = a1.put("pc", [P, BANK])
        a2 = Region(nc, d_at, d_end)
        K_c = [a2.put("K_c0", [P, 4, BANK]),
               nc.alloc_sbuf_tensor_at("K_c1", [P, 4, BANK], F32, offset=k_at)]
        V_c = a2.put("V_c", [P, 4, BANK])
        V_n = a2.put("V_n", [STEP, BANK])
        p_at = a2.at
        pr = a2.put("pr", [P, 2, BANK])
        ps = nc.alloc_sbuf_tensor_at("ps", [P, PAST + STEP], F32, offset=p_at)
        Cm = nc.alloc_sbuf_tensor_at("Cm", [P, P], F32, offset=p_at + 3072)
        pT = a1.put("pT", [P, BANK])
        pTn = a2.put("pTn", [STEP, P])
        od_sq = nc.alloc_sbuf_tensor_at("od_sq", [P, TT, BANK], F32, offset=h_at)
        wout = Region(nc, tok_at, c_at)
        raw_o = wout.put("raw_o", [P, KT, BANK])
        o_hi = wout.put("o_hi", [P, 2, BANK], F32R)
        o_lo = wout.put("o_lo", [P, 2, BANK], F32R)
        wout2 = Region(nc, c_at, c_end)
        raw_o1 = wout2.put("raw_o1", [P, KT, BANK])

        mn, on = Norm(1), Norm(2)
        N = {n: sem(n) for n in """
            x_spilled x_back params_loaded conv_rows_loaded hist_transposed hist_ready pad_zero
            conv_hi conv_lo conv_product conv_padded conv_sum conv_silu tail_transposed tail_rows
            tail_stored baT_copied ba_tr ba_copied
            group_hi group_lo group_step group_evac row_squares row_sums kv_stored
            lam_chain qk_chain act_qk qk_done lam_exp
            tok_tr tok_copied tok_sq tok_sums gate_chain gate_act g_product cs_ready rk_root
            scaled pooled tr_scaled act_T kbT_ready diff decay_exp decay kk masked ct r0 t0 t0c x_mm
            x_copied level_mm level_upd w_mm nw u_mm u_copied o_mm o_copied S_ready S_stored
            exp_ready zero_exp u4_mm ue_ready o4_mm oc4 ss_ready gls
            og_chain og_act og_done
            qbd_zero qkT_mm qkT_copied sc_mm nmax probs pcomb p_tr p_copied pv_mm pv_copied att_chain
            kt_mm kt_copied ssc_mm s_nmax s_probs s_comb sp_mm sp_copied spv_mm 
            od_chain od_act od_done wo_hi wo_lo wo_step wo_res 
            """.split()}
        s_cvw = [sem(f"conv_loaded{i}") for i in range(2)]
        s_gw = [sem(f"group_loaded{i}") for i in range(2)]
        s_K = [sem(f"k_cache_loaded{i}") for i in range(2)]
        s_V = sem("v_cache_loaded")
        s_ss_in = [sem(f"stream_state_loaded{i}") for i in range(2)]
        s_ss_out = [sem(f"stream_state_stored{i}") for i in range(2)]

        x_mid = nc.dram_tensor("x_mid", [TOK, D], F32, kind="Internal").ap()
        w_in = io["w_in"][0].rearrange("(k p) c -> p k c", p=P)
        w_out = io["w_out"][0].rearrange("(k p) c -> p k c", p=P)
        V = nc.vector

        def link(eng, s, n, ins):
            ins.then_inc(N[s], 1)
            eng.wait_ge(N[s], n)

        def bc(ap, n):
            return ap.unsqueeze(2).broadcast_to([ap.shape[0], ap.shape[1], n])

        def over(ap, n):
            return ap.unsqueeze(1).broadcast_to([ap.shape[0], n, ap.shape[1]])

        def conv_sync(sp):
            rows = conv_rows[:]
            sp.wait_ge(*f1.res(2 * TT))
            sp.dma_start(rows[0:24, :], io["state_conv"][0].rearrange("b w c -> (b w) c"))\
                .then_inc(N["conv_rows_loaded"], 16)
            sp.dma_start(rows[24:28, :], io["conv_w"][0]).then_inc(N["conv_rows_loaded"], 16)

            def load(j, slot):
                sp.dma_start(raw_cv[:, slot], w_in[:, :, bass.ds(j * P, P)]).then_inc(s_cvw[slot], 16)

            load(0, 0)
            load(1, 1)
            sp.wait_ge(*mn.lo(2 * TT))
            for dst, src in ((gdn_gain[:], io["gdn_out_norm"].to_broadcast([P, P])),
                             (diff_gain[:], io["diff_out_norm"].to_broadcast([P, P])),
                             (qk_gain[:, 0, :], io["q_norm"].to_broadcast([P, DK])),
                             (qk_gain[:, 1, :], io["k_norm"].to_broadcast([P, DK])),
                             (lam_in[:, 0], io["lambda_q"].to_broadcast([P, 2, DK])),
                             (lam_in[:, 1], io["lambda_k"].to_broadcast([P, 2, DK])),
                             (head_par[:, 0, :], io["a_log"].to_broadcast([P, HEADS])),
                             (head_par[:, 1, :], io["dt_bias"].to_broadcast([P, HEADS])),
                             (rot[:], io["rotary"].rearrange("p (a t f) -> p a t f", a=2, t=TT))):
                sp.dma_start(dst, src).then_inc(N["params_loaded"], 16)
            sp.dma_start(x_mid[0:PROMPT, :].rearrange("(t p) c -> p t c", p=P), x_tok[:, 0:4, :])\
                .then_inc(N["x_spilled"], 16)
            sp.dma_start(x_mid[PROMPT:TOK, :], x_tok[:, 4, :]).then_inc(N["x_spilled"], 16)
            with sp.Fori(1, CONV_T // 2) as pair:
                j = 2 * pair
                for slot in range(2):
                    sp.wait_ge(N["conv_lo"], j + slot - 1)
                    load(j + slot, slot)
            sp.wait_ge(N["conv_lo"], CONV_T - 1)
            load(CONV_T, 0)
            for hg in range(8):
                g, kh = GROUPS[hg // 2], hg % 2
                if hg < 2:
                    sp.wait_ge(N["conv_lo"], CONV_T + 1)
                    sp.wait_ge(N["conv_product"], CONV_T + 1)
                else:
                    sp.wait_ge(N["group_lo"], 4 * (hg - 1))
                sp.dma_start(raw_b[:, hg % 2],
                             w_in[:, 4 * kh:4 * kh + 4, Z_COL + BANK * g:Z_COL + BANK * (g + 1)])\
                    .then_inc(s_gw[hg % 2], 16)
            sp.wait_ge(N["qk_done"], 4)
            sp.wait_ge(N["group_evac"], 3 * TT)
            for name, dims, src in (("k", "(h m d)", k_tok), ("v", "(h d)", v_tok)):
                row = dims[1:-1]
                sp.dma_start(io[f"{name}_prompt"][0, 0].rearrange(f"(t p) {row} -> p t {dims}", p=P),
                             src[:, 0:4, :]).then_inc(N["kv_stored"], 16)
                sp.dma_start(io[f"{name}_sample"][0].rearrange(f"b s {row} -> (b s) {dims}"),
                             src[:, 4, :]).then_inc(N["kv_stored"], 16)

        def conv_act(act):
            def split(j, slot):
                act.wait_ge(s_cvw[slot], 8 * (j - slot) + 16)
                nc.scalar.activation(cv_hi[:, slot], raw_cv[:, slot], ACT.Copy)\
                    .then_inc(N["conv_hi"], 1)

            def pad(j, slot):
                act.wait_ge(N["conv_product"], j + 1)
                a, b = psum[2 * slot], psum[2 * slot + 1]
                x = xp[:, slot, :]
                for dst, src in ((x[:, 3:3 + HALF], a[:, 0:HALF]),
                                 (x[:, 3 + HALF:3 + PROMPT], b[:, 0:PROMPT - HALF]),
                                 (streams(x)[:, :, 3:19],
                                  b[:, PROMPT - HALF:HALF].rearrange("p (b s) -> p b s", s=STEP))):
                    nc.scalar.activation(dst, src, ACT.Copy).then_inc(N["conv_padded"], 1)

            def silu(j):
                act.wait_ge(N["conv_sum"], 11 * j + 11)
                nc.scalar.activation(cT[:, j, :], cT[:, j, :], ACT.Silu).then_inc(N["conv_silu"], 1)

            split(0, 0)
            split(1, 1)
            act.wait_ge(N["pad_zero"], 1)
            pad(0, 0)
            with act.Fori(1, CONV_T // 2) as pair:
                j = 2 * pair
                act.wait_ge(N["conv_product"], j - 1)
                split(j, 0)
                act.wait_ge(N["conv_sum"], 11 * j - 21)
                pad(j - 1, 1)
                silu(j - 2)
                act.wait_ge(N["conv_product"], j)
                split(j + 1, 1)
                act.wait_ge(N["conv_sum"], 11 * j - 11)
                pad(j, 0)
                silu(j - 1)
            act.wait_ge(N["conv_product"], CONV_T - 1)
            split(CONV_T, 0)
            act.wait_ge(N["conv_sum"], 11 * (CONV_T - 2))
            pad(CONV_T - 1, 1)
            silu(CONV_T - 2)
            silu(CONV_T - 1)
            act.wait_ge(N["conv_product"], CONV_T + 1)
            for part in range(2):
                nc.scalar.activation(baT[:, part * HALF:(part + 1) * HALF], psum[part][0:8, 0:HALF],
                                     ACT.Copy).then_inc(N["baT_copied"], 1)

        def streams(x):
            return x[:, 515:667].rearrange("p (b s) -> p b s", s=19)

        def conv_dve(dve):
            V.memset(xp[:, :, 0:3], 0.0).then_inc(N["pad_zero"], 1)
            dve.wait_ge(N["hist_transposed"], 1)
            V.tensor_copy(hist[:], psum[7][:, 0:336].rearrange("p (c w) -> p c w", w=28))\
                .then_inc(N["hist_ready"], 1)
            dve.wait_ge(N["hist_ready"], 1)

            def split(j, slot):
                dve.wait_ge(N["conv_hi"], j + 1)
                V.tensor_tensor(cv_lo[:, slot], raw_cv[:, slot], raw(cv_hi[:, slot]), ALU.subtract)\
                    .then_inc(N["conv_lo"], 1)

            def conv(j, slot):
                x, s, n = xp[:, slot, :], N["conv_sum"], 11 * j
                V.tensor_copy(streams(x)[:, :, 0:3],
                              hist[:, j, 0:24].rearrange("p (b w) -> p b w", w=3)).then_inc(s, 1)
                dve.wait_ge(N["conv_padded"], 3 * j + 3)
                V.tensor_copy(tail[:, j, 0:3], x[:, PROMPT:PROMPT + 3]).then_inc(s, 1)
                V.tensor_copy(tail[:, j, 3:27].rearrange("p (b w) -> p b w", w=3),
                              streams(x)[:, :, 16:19]).then_inc(s, 1)
                yp = cT[:, j, 0:PROMPT]
                yq = cT[:, j, PROMPT:TOK].rearrange("p (b s) -> p b s", s=STEP)
                for i in range(4):
                    w = hist[:, j, 24 + i:25 + i]
                    if i == 0:
                        dve.wait_ge(s, n + 1)
                        V.tensor_scalar(yp, x[:, 0:PROMPT], w, None, ALU.mult).then_inc(s, 1)
                        V.tensor_scalar(yq, streams(x)[:, :, 0:16], w, None, ALU.mult).then_inc(s, 1)
                    else:
                        dve.wait_ge(s, n + 2 + 2 * i)
                        V.scalar_tensor_tensor(yp, x[:, i:i + PROMPT], w, yp, ALU.mult,
                                               ALU.add).then_inc(s, 1)
                        dve.wait_ge(s, n + 3 + 2 * i)
                        V.scalar_tensor_tensor(yq, streams(x)[:, :, i:i + 16], w, yq, ALU.mult,
                                               ALU.add).then_inc(s, 1)

            split(0, 0)
            split(1, 1)
            conv(0, 0)
            with dve.Fori(1, CONV_T // 2) as pair:
                j = 2 * pair
                split(j, 0)
                dve.wait_ge(N["conv_sum"], 11 * j - 11)
                conv(j - 1, 1)
                split(j + 1, 1)
                dve.wait_ge(N["conv_sum"], 11 * j)
                conv(j, 0)
            split(CONV_T, 0)
            dve.wait_ge(N["conv_sum"], 11 * (CONV_T - 1))
            conv(CONV_T - 1, 1)
            for i in range(3):
                dve.wait_ge(N["tail_transposed"], i + 1)
                V.tensor_copy(conv_out[:, i * BANK:(i + 1) * BANK], psum[5 + i][0:27, :])\
                    .then_inc(N["tail_rows"], 1)

        def conv_pe(pe):
            pe.wait_ge(N["conv_rows_loaded"], 32)
            for c in range(CONV_T):
                last = nc.tensor.transpose(psum[7][:, 28 * c:28 * c + 28],
                                           conv_rows[:, c * P:(c + 1) * P], ident[0:28, 0:28])
            last.then_inc(N["hist_transposed"], 1)

            def product(j, slot):
                for k in range(KT):
                    for part in range(2):
                        t = slice(part * HALF, (part + 1) * HALF)
                        last = three(psum[2 * slot + part][:, 0:HALF], cv_hi[:, slot, k, :],
                                     cv_lo[:, slot, k, :], hT_hi[:, k, t], hT_lo[:, k, t],
                                     k == 0, k == KT - 1)
                last.then_inc(N["conv_product"], 1)

            pe.wait_ge(*mn.lo(2 * TT))
            for slot in range(2):
                pe.wait_ge(N["conv_lo"], slot + 1)
                product(slot, slot)
            with pe.Fori(1, CONV_T // 2) as pair:
                for slot in range(2):
                    j = 2 * pair + slot
                    pe.wait_ge(N["conv_lo"], j + 1)
                    pe.wait_ge(N["conv_padded"], 3 * j - 3)
                    product(j, slot)
            pe.wait_ge(N["conv_lo"], CONV_T + 1)
            pe.wait_ge(N["conv_padded"], 3 * (CONV_T - 1))
            product(CONV_T, 0)
            pe.wait_ge(N["conv_sum"], 11 * CONV_T)
            for i in range(3):
                for c in range(4):
                    last = nc.tensor.transpose(psum[5 + i][0:27, c * P:(c + 1) * P],
                                               tail[:, 4 * i + c, :], ident)
                last.then_inc(N["tail_transposed"], 1)

        GROUPS = (1, 2, 3, 0)

        def group_act(act):
            def split(n):
                act.wait_ge(s_gw[n // 4 % 2], 16 * (n // 8 + 1))
                if n >= 2:
                    act.wait_ge(N["group_step"], n - 1)
                nc.scalar.activation(b_hi[:, n % 2], raw_b[:, n // 4 % 2, n % 4], ACT.Copy)\
                    .then_inc(N["group_hi"], 1)

            def square(i, t):
                m = i * TT + t
                if m < 2:
                    act.wait_ge(N["conv_sum"], 11 * CONV_T)
                else:
                    act.wait_ge(N["row_sums"], m - 1)
                act.wait_ge(N["group_evac"], m + 1)
                nc.scalar.activation(sq_rows[m % 2][:], (q_tok, k_tok)[i][:, t, :], ACT.Square)\
                    .then_inc(N["row_squares"], 1)

            rope = qk_act(act)
            split(0)
            for n in range(4 * KT):
                i, k = n // KT, n % KT
                if i and k == 0:
                    for t in range(3):
                        evac(act, i - 1, t)
                if n + 1 < 4 * KT:
                    split(n + 1)
                yield
                if i and k == 0:
                    evac(act, i - 1, 3)
                    evac(act, i - 1, 4)
                if i in (1, 2) and 1 <= k <= TT:
                    square(i - 1, k - 1)
                if n >= ROPE_FROM:
                    next(rope, None)
                yield
            for t in range(TT):
                evac(act, 3, t)
            yield

        ROPE_FROM = KT + 6

        def evac(act, i, t):
            act.wait_ge(N["group_step"], (i + 1) * KT)
            if i == 1 and t == 0:
                act.wait_ge(N["tail_transposed"], 3)
            if i == 2 and t == 0:
                act.wait_ge(N["tail_stored"], 32)
            dst = (q_tok, k_tok, v_tok, z)[i][:, t, :]
            nc.scalar.activation(dst, psum[t], ACT.Silu if i == 3 else ACT.Copy)\
                .then_inc(N["group_evac"], 1)

        def group_dve(dve):
            def split(n):
                dve.wait_ge(N["group_hi"], n + 1)
                V.tensor_tensor(b_lo[:, n % 2], raw_b[:, n // 4 % 2, n % 4],
                                raw(b_hi[:, n % 2]), ALU.subtract).then_inc(N["group_lo"], 1)

            rope = qk_dve(dve)
            split(0)
            for n in range(4 * KT):
                i, k = n // KT, n % KT
                if n + 1 < 4 * KT:
                    split(n + 1)
                yield
                if i in (1, 2) and 1 <= k <= TT:
                    m = (i - 1) * TT + k - 1
                    dve.wait_ge(N["row_squares"], m + 1)
                    V.tensor_reduce(qk_ss[:, i - 1, 0, 8 * (k - 1):8 * k],
                                    sq_rows[m % 2][:].rearrange("p (c d) -> p c d", d=DK), AX.X,
                                    ALU.add).then_inc(N["row_sums"], 1)
                if n >= ROPE_FROM:
                    next(rope, None)
                yield
            yield

        def group_pe(pe):
            for n in range(4 * KT):
                i, k = n // KT, n % KT
                pe.wait_ge(N["group_lo"], n + 1)
                for t in range(TT):
                    if t == 3:
                        yield
                    if k == 0 and i:
                        pe.wait_ge(N["group_evac"], (i - 1) * TT + t + 1)
                    if n == 0 and t == 0:
                        pe.wait_ge(N["conv_padded"], 3 * CONV_T)
                        pe.wait_ge(N["baT_copied"], 2)
                    c = slice(t * P, (t + 1) * P)
                    last = three(psum[t], hT_hi[:, k, c], hT_lo[:, k, c], b_hi[:, n % 2],
                                 b_lo[:, n % 2], k == 0, k == KT - 1)
                last.then_inc(N["group_step"], 1)
                yield
            yield

        def qk_dve(dve):
            dve.wait_ge(N["params_loaded"], 16 * 9)
            prod = lam_in[:, 0]
            link(dve, "lam_chain", 1, V.tensor_tensor(prod, lam_in[:, 0], lam_in[:, 1], ALU.mult))
            V.tensor_reduce(lam[:, 0:2], prod, AX.X, ALU.add).then_inc(N["lam_chain"], 1)
            yield
            dve.wait_ge(N["lam_exp"], 1)
            link(dve, "lam_chain", 3, V.tensor_tensor(lam[:, 4:5], lam[:, 2:3], lam[:, 3:4],
                                                      ALU.subtract))
            link(dve, "lam_chain", 4, V.tensor_scalar(lam[:, 5:6], lam[:, 4:5], LAM_INIT, None,
                                                      ALU.add))
            link(dve, "lam_chain", 5, V.scalar_tensor_tensor(
                lam[:, 6:7], const("map1"), lam[:, 5:6], const("map0"), ALU.mult, ALU.add))
            link(dve, "lam_chain", 6, V.tensor_scalar(lam[:, 7:8], lam[:, 5:6], -1.0, None, ALU.mult))
            yield
            for w, x in enumerate((q_tok, k_tok)):
                n = 10 * w
                dve.wait_ge(N["row_sums"], TT * (w + 1))
                dve.wait_ge(N["group_evac"], TT * (w + 1))
                link(dve, "qk_chain", n + 1, V.tensor_scalar(qk_ss[:, w, 1, :], qk_ss[:, w, 0, :],
                                                             1.0 / DK, EPS, ALU.mult, ALU.add))
                V.reciprocal(qk_ss[:, w, 2, :], qk_ss[:, w, 1, :]).then_inc(N["qk_chain"], 1)
                yield
                dve.wait_ge(N["act_qk"], w + 1)
                for p, (a, b) in enumerate(((0, 2), (2, TT))):
                    rows = x[:, a:b, :].rearrange("p t (c d) -> p (t c) d", d=DK)
                    link(dve, "qk_chain", n + 2 * p + 3, V.tensor_tensor(
                        rows, rows, bc(qk_ss[:, w, 0, 8 * a:8 * b], DK), ALU.mult))
                    yield
                    link(dve, "qk_chain", n + 2 * p + 4, V.tensor_tensor(
                        rows, rows, over(qk_gain[:, w, :], (b - a) * 8), ALU.mult))
                    yield
                v4 = x[:].rearrange("p t (c d) -> p t c d", d=DK)
                x1, x2 = v4[:, :, :, 0:8], v4[:, :, :, 8:16]
                tmp = [rope_tmp[:, i, :].rearrange("p (t c d) -> p t c d", c=8, d=8)
                       for i in range(4)]
                cos, sin = (rot[:, i].unsqueeze(2).broadcast_to([P, TT, 8, 8]) for i in range(2))
                for i, (a, f) in enumerate(((x1, cos), (x2, sin), (x2, cos), (x1, sin))):
                    V.tensor_tensor(tmp[i], a, f, ALU.mult).then_inc(N["qk_chain"], 1)
                yield
                dve.wait_ge(N["qk_chain"], n + 10)
                V.tensor_tensor(x1, tmp[0], tmp[1], ALU.subtract).then_inc(N["qk_done"], 1)
                V.tensor_tensor(x2, tmp[2], tmp[3], ALU.add).then_inc(N["qk_done"], 1)
                dve.wait_ge(N["qk_done"], 2 * w + 2)
                yield

        def qk_act(act):
            act.wait_ge(N["lam_chain"], 2)
            nc.scalar.activation(lam[:, 2:4], lam[:, 0:2], ACT.Exp).then_inc(N["lam_exp"], 1)
            yield
            yield
            for w in range(2):
                act.wait_ge(N["qk_chain"], 10 * w + 2)
                nc.scalar.activation(qk_ss[:, w, 0, :], qk_ss[:, w, 2, :], ACT.Sqrt)\
                    .then_inc(N["act_qk"], 1)
                for _ in range(7):
                    yield

        (G_BETA, G_G, G_CUM, G_TOT, G_EC, G_ER, G_ET, G_RQ, G_RK, G_KB, G_KBG, G_KD, G_QD, G_A,
         G_B, G_C, G_D, G_SSQ, G_SSK, G_E) = range(20)
        gt = lambda i: gates[:, i]
        GB = [5, 6, 7]

        def tok_pe(pe):
            pe.wait_ge(N["tail_rows"], 3)
            for t in range(TT):
                last = nc.tensor.transpose(psum[7][:, 8 * t:8 * t + 8], baT[:, t * P:(t + 1) * P],
                                           ident[0:8, 0:8])
            last.then_inc(N["ba_tr"], 1)
            yield
            pe.wait_ge(N["conv_silu"], CONV_T)
            pe.wait_ge(N["ba_copied"], 1)
            for t in range(TT):
                for w in range(3):
                    n = 3 * t + w
                    if n >= 3:
                        pe.wait_ge(N["tok_copied"], n - 2)
                    for h in range(HEADS):
                        last = nc.tensor.transpose(psum[GB[w]][:, h * P:(h + 1) * P],
                                                   cT[:, 4 * w + h, t * P:(t + 1) * P], ident)
                    last.then_inc(N["tok_tr"], 1)
                yield
                yield

        def tok_dve(dve):
            dve.wait_ge(N["ba_tr"], 1)
            V.tensor_copy(ba[:], psum[7][:, 0:40].rearrange("p (t c) -> p t c", c=8))\
                .then_inc(N["ba_copied"], 1)
            yield
            for t in range(TT):
                for w in range(3):
                    dve.wait_ge(N["tok_tr"], 3 * t + w + 1)
                    V.tensor_copy(tok[:, t, 4 * w:4 * w + 4, :],
                                  psum[GB[w]].rearrange("p (h d) -> p h d", d=P))\
                        .then_inc(N["tok_copied"], 1)
                yield
                for w in range(2):
                    dve.wait_ge(N["tok_sq"], 2 * t + w + 1)
                    V.tensor_reduce(gates[:, G_SSQ + w, t, :], (kbg, kd)[w][:], AX.X, ALU.add)\
                        .then_inc(N["tok_sums"], 1)
                yield
            dve.wait_ge(N["tok_sums"], 2 * TT)

        def tok_act(act):
            yield
            act.wait_ge(N["x_spilled"], 32)
            for t in range(TT):
                yield
                for w in range(2):
                    act.wait_ge(N["tok_copied"], 3 * t + w + 1)
                    if t:
                        act.wait_ge(N["tok_sums"], 2 * t + w - 1)
                    nc.scalar.activation((kbg, kd)[w][:], tok[:, t, 4 * w:4 * w + 4, :],
                                         ACT.Square).then_inc(N["tok_sq"], 1)
                yield

        def gate_dve(dve):
            c = [0]

            def l(ins):
                c[0] += 1
                link(dve, "gate_chain", c[0], ins)

            beta_in, a_in = ba[:, :, 0:4], ba[:, :, 4:8]
            dt = over(head_par[:, 1, :], TT)
            l(V.tensor_tensor(gt(G_A), a_in, dt, ALU.add))
            l(V.tensor_scalar(gt(G_B), gt(G_A), -1.0, None, ALU.mult))
            l(V.tensor_tensor(gt(G_B), gt(G_A), gt(G_B), ALU.min))
            yield
            dve.wait_ge(N["gate_act"], 3)
            l(V.tensor_scalar(gt(G_C), gt(G_C), 1.0, None, ALU.add))
            l(V.reciprocal(gt(G_BETA), gt(G_C)))
            l(V.tensor_scalar(gt(G_A), gt(G_A), 0.0, None, ALU.max))
            l(V.tensor_tensor(gt(G_A), gt(G_A), gt(G_D), ALU.add))
            l(V.scalar_tensor_tensor(gt(G_G), gt(G_A), -1.0, over(head_par[:, 0, :], TT), ALU.mult,
                                     ALU.mult))
            yield
            dve.wait_ge(N["g_product"], 1)
            l(V.tensor_copy(gt(G_CUM), psum[6][:, 0:20].rearrange("p (t h) -> p t h", h=4)))
            l(V.tensor_copy(gt(G_TOT), psum[6][:, 32:52].rearrange("p (t h) -> p t h", h=4)))
            l(V.tensor_tensor(gt(G_E), gt(G_TOT), gt(G_CUM), ALU.subtract))
            ss = gates[:, G_SSQ:G_SSQ + 2]
            l(V.tensor_scalar(gates[:, G_A:G_A + 2], ss, EPS, None, ALU.add))
            l(V.reciprocal(gates[:, G_C:G_C + 2], gates[:, G_A:G_A + 2]))
            yield
            dve.wait_ge(N["gate_act"], 7)
            l(V.tensor_scalar(gt(G_RQ), gt(G_RQ), float(P) ** -0.5, None, ALU.mult))
            l(V.tensor_tensor(gt(G_KB), gt(G_RK), gt(G_BETA), ALU.mult))
            l(V.tensor_tensor(gt(G_KBG), gt(G_KB), gt(G_EC), ALU.mult))
            l(V.tensor_tensor(gt(G_KD), gt(G_RK), gt(G_ER), ALU.mult))
            V.tensor_tensor(gt(G_QD), gt(G_RQ), gt(G_EC), ALU.mult).then_inc(N["cs_ready"], 1)
            dve.wait_ge(N["cs_ready"], 1)
            V.memset(S_p[:], 0.0).then_inc(N["S_ready"], 1)
            yield

        def gate_act(act):
            act.wait_ge(N["gate_chain"], 3)
            nc.scalar.activation(gt(G_C), ba[:, :, 0:4], ACT.Exp, scale=-1.0)\
                .then_inc(N["gate_act"], 1)
            nc.scalar.activation(head_par[:, 0, :], head_par[:, 0, :], ACT.Exp)\
                .then_inc(N["gate_act"], 1)
            nc.scalar.activation(gt(G_D), gt(G_B), ACT.Exp).then_inc(N["rk_root"], 1)
            act.wait_ge(N["rk_root"], 1)
            nc.scalar.activation(gt(G_D), gt(G_D), ACT.Ln, bias=1.0).then_inc(N["gate_act"], 1)
            yield
            yield
            act.wait_ge(N["gate_chain"], 11)
            for dst, src in ((G_EC, G_CUM), (G_ER, G_E), (G_ET, G_TOT)):
                nc.scalar.activation(gt(dst), gt(src), ACT.Exp).then_inc(N["gate_act"], 1)
            act.wait_ge(N["gate_chain"], 13)
            nc.scalar.activation(gates[:, G_RQ:G_RQ + 2], gates[:, G_C:G_C + 2], ACT.Sqrt)\
                .then_inc(N["gate_act"], 1)
            yield
            yield

        def gate_pe(pe):
            yield
            pe.wait_ge(N["gate_chain"], 8)
            pe.wait_ge(N["tok_copied"], 3 * TT)
            g = gt(G_G)
            nc.tensor.matmul(psum[6][:, 0:16], const("cum_p"), g[:, 0:4, :], start=True, stop=True)
            nc.tensor.matmul(psum[6][:, 16:20], const("cum_s"), g[:, 4, :], start=True, stop=True)
            nc.tensor.matmul(psum[6][:, 32:48], const("ones"), g[:, 0:4, :], start=True, stop=True)
            nc.tensor.matmul(psum[6][:, 48:52], const("blk_s"), g[:, 4, :], start=True, stop=True)\
                .then_inc(N["g_product"], 1)
            yield
            yield
            yield

        LV = [7, 7, 7, 7, 4]
        CTB = [sum(LV[:t]) for t in range(TT + 1)]
        UPB = [sum(2 * (v - 1) - 1 for v in LV[:t]) for t in range(TT + 1)]
        XB = [sum(v - 1 for v in LV[:t]) for t in range(TT + 1)]
        b4 = lambda bank: psum[bank].rearrange("p (h d) -> p h d", d=P)
        hc = lambda h: slice(h * P, (h + 1) * P)

        def gdn_dve(dve, t):
            q4, k4 = tok[:, t, 0:4, :], tok[:, t, 4:8, :]
            f = lambda i: bc(gates[:, i, t, :], P)
            if t:
                dve.wait_ge(N["o_mm"], 2 * t)
            V.tensor_tensor(Xm[:], k4, f(G_RK), ALU.mult).then_inc(N["scaled"], 1)
            V.tensor_tensor(CT[1][:], k4, f(G_KB), ALU.mult).then_inc(N["scaled"], 1)
            V.tensor_tensor(CT[0][:], q4, f(G_RQ), ALU.mult).then_inc(N["scaled"], 1)
            V.tensor_tensor(qd[:], q4, f(G_QD), ALU.mult).then_inc(N["scaled"], 1)
            V.tensor_copy(gbc[:], f(G_G)).then_inc(N["scaled"], 1)
            dve.wait_ge(N["tr_scaled"], 5 * t + 2)
            V.tensor_copy(kbT[:], b4(6)).then_inc(N["kbT_ready"], 1)
            yield
            dve.wait_ge(N["tr_scaled"], 5 * t + 5)
            V.tensor_tensor(ET[:], b4(6), f(G_CUM), ALU.subtract).then_inc(N["diff"], 1)
            dve.wait_ge(N["diff"], 2 * t + 1)
            V.tensor_scalar(ET[:], ET[:], 0.0, None, ALU.min).then_inc(N["diff"], 1)
            yield
            dve.wait_ge(N["decay_exp"], t + 1)
            V.tensor_tensor(ET[:], ET[:], over(const("cum_s" if t == 4 else "cum_p"), HEADS),
                            ALU.mult).then_inc(N["decay"], 1)
            dve.wait_ge(N["decay"], t + 1)
            dve.wait_ge(N["kk"], 2 * t + 1)
            V.tensor_tensor(LT[:], b4(7), ET[:], ALU.mult).then_inc(N["masked"], 1)
            dve.wait_ge(N["kk"], 2 * t + 2)
            V.tensor_tensor(QKT[:], b4(5), ET[:], ALU.mult).then_inc(N["masked"], 1)
            yield
            dve.wait_ge(N["ct"], CTB[t] + 1)
            V.tensor_tensor(Rm[:], over(ident, HEADS), CT[0][:], ALU.subtract).then_inc(N["r0"], 1)
            yield
            yield
            n = LV[t] - 1
            for l in range(1, n + 1):
                yield
                dve.wait_ge(N["level_mm"], XB[t] + l)
                if l == 1:
                    dve.wait_ge(N["t0c"], t + 1)
                    dve.wait_ge(N["r0"], t + 1)
                else:
                    dve.wait_ge(N["level_upd"], UPB[t] + 2 * (l - 1))
                if l < n:
                    V.tensor_tensor(Tm[:], Tm[:], b4(5), ALU.subtract).then_inc(N["level_upd"], 1)
                V.tensor_tensor(Rm[:], Rm[:], b4(6), ALU.subtract).then_inc(N["level_upd"], 1)
                yield
            yield

        def gdn_state_dve(dve, t):
            dve.wait_ge(N["u_mm"], t + 1)
            V.tensor_copy(u_sb[:], b4(5)).then_inc(N["u_copied"], 1)
            yield
            dve.wait_ge(N["o_mm"], 2 * t + 2)
            dve.wait_ge(N["S_ready"], 4 * t + 1)
            for h in range(HEADS):
                V.scalar_tensor_tensor(S_p[:, h, :], S_p[:, h, :], gates[:, G_ET, t, h:h + 1],
                                       psum[7][:, hc(h)], ALU.mult, ALU.add)\
                    .then_inc(N["S_ready"], 1)
            yield

        def gdn_act(act, t):
            act.wait_ge(N["tr_scaled"], 5 * t + 1)
            nc.scalar.activation(knT[:], b4(5), ACT.Copy).then_inc(N["act_T"], 1)
            yield
            act.wait_ge(N["tr_scaled"], 5 * t + 3)
            nc.scalar.activation(qnT[:], b4(7), ACT.Copy).then_inc(N["act_T"], 1)
            act.wait_ge(N["tr_scaled"], 5 * t + 4)
            nc.scalar.activation(qdT[:], b4(5), ACT.Copy).then_inc(N["act_T"], 1)
            yield
            act.wait_ge(N["diff"], 2 * t + 2)
            if t == 4:
                nc.scalar.activation(gls[:], b4(6)[:, :, STEP - 1::STEP], ACT.Exp)\
                    .then_inc(N["gls"], 1)
            nc.scalar.activation(ET[:], ET[:], ACT.Exp).then_inc(N["decay_exp"], 1)
            yield
            yield
            act.wait_ge(N["t0"], t + 1)
            nc.scalar.activation(Tm[:], b4(6), ACT.Copy).then_inc(N["t0c"], 1)
            yield
            for l in range(1, LV[t]):
                act.wait_ge(N["x_mm"], XB[t] + l)
                nc.scalar.activation(Xm[:], b4(7), ACT.Copy).then_inc(N["x_copied"], 1)
                yield
                yield
            act.wait_ge(N["w_mm"], t + 1)
            nc.scalar.activation(nwT[:], b4(7), ACT.Copy, scale=-1.0).then_inc(N["nw"], 1)
            yield
            if t < 4:
                yield
                act.wait_ge(N["o_mm"], 2 * t + 1)
                nc.scalar.activation(tok[:, t, 0:4, :], b4(6), ACT.Copy).then_inc(N["o_copied"], 1)
                yield

        def gdn_pool(pool, t):
            k4, v4 = tok[:, t, 4:8, :], tok[:, t, 8:12, :]
            f = lambda i: bc(gates[:, i, t, :], P)
            if t == 0:
                pool.wait_ge(N["cs_ready"], 1)
            else:
                pool.wait_ge(N["o_mm"], 2 * t)
            nc.gpsimd.tensor_tensor(kbg[:], k4, f(G_KBG), ALU.mult).then_inc(N["pooled"], 1)
            nc.gpsimd.tensor_tensor(v4, v4, f(G_BETA), ALU.mult).then_inc(N["pooled"], 1)
            nc.gpsimd.tensor_tensor(kd[:], k4, f(G_KD), ALU.mult).then_inc(N["pooled"], 1)
            pool.wait_ge(N["masked"], 2 * t + 1)
            for i in range(LV[t]):
                if i == 2:
                    pool.wait_ge(N["r0"], t + 1)
                if i >= 3:
                    pool.wait_ge(N["x_mm"], XB[t] + i - 2)
                nc.gpsimd.tensor_tensor(CT[i % 2][:], LT[:], over(const(f"lvl{LEVELS[i]}"), HEADS),
                                        ALU.mult).then_inc(N["ct"], 1)

        def gdn_pe(pe, t):
            for i, (src, bank) in enumerate(((Xm, 5), (CT[1], 6), (CT[0], 7))):
                pe.wait_ge(N["scaled"], 5 * t + i + 1)
                if i == 1 and t:
                    pe.wait_ge(N["o_copied"], t)
                if i == 2 and t:
                    pe.wait_ge(N["S_ready"], 4 * t + 1)
                for h in range(HEADS):
                    last = nc.tensor.transpose(psum[bank][:, hc(h)], src[:, h, :], ident)
                last.then_inc(N["tr_scaled"], 1)
            yield
            pe.wait_ge(N["scaled"], 5 * t + 4)
            pe.wait_ge(N["act_T"], 3 * t + 1)
            for h in range(HEADS):
                last = nc.tensor.transpose(psum[5][:, hc(h)], qd[:, h, :], ident)
            last.then_inc(N["tr_scaled"], 1)
            pe.wait_ge(N["scaled"], 5 * t + 5)
            pe.wait_ge(N["kbT_ready"], t + 1)
            for h in range(HEADS):
                last = nc.tensor.matmul(psum[6][:, hc(h)], gbc[:, h, :],
                                        const("cum_s" if t == 4 else "cum_p"), start=True, stop=True)
            last.then_inc(N["tr_scaled"], 1)
            yield
            pe.wait_ge(N["act_T"], 3 * t + 2)
            for h in range(HEADS):
                last = nc.tensor.matmul(psum[7][:, hc(h)], knT[:, h, :], kbT[:, h, :], start=True,
                                        stop=True)
            last.then_inc(N["kk"], 1)
            pe.wait_ge(N["act_T"], 3 * t + 3)
            for h in range(HEADS):
                last = nc.tensor.matmul(psum[5][:, hc(h)], knT[:, h, :], qnT[:, h, :], start=True,
                                        stop=True)
            last.then_inc(N["kk"], 1)
            yield
            yield
            pe.wait_ge(N["r0"], t + 1)
            if t == 4:
                pe.wait_ge(N["gls"], 1)
            for h in range(HEADS):
                last = nc.tensor.transpose(psum[6][:, hc(h)], Rm[:, h, :], ident)
            last.then_inc(N["t0"], 1)
            yield
            n = LV[t] - 1
            for l in range(1, n + 1):
                pe.wait_ge(N["ct"], CTB[t] + l + 1)
                if l == 1:
                    pe.wait_ge(N["t0c"], t + 1)
                else:
                    pe.wait_ge(N["level_upd"], UPB[t] + 2 * (l - 1))
                for h in range(HEADS):
                    last = nc.tensor.matmul(psum[7][:, hc(h)], CT[l % 2][:, h, :], Tm[:, h, :],
                                            start=True, stop=True)
                last.then_inc(N["x_mm"], 1)
                yield
                pe.wait_ge(N["x_copied"], XB[t] + l)
                if l < n:
                    for h in range(HEADS):
                        nc.tensor.matmul(psum[5][:, hc(h)], Rm[:, h, :], Xm[:, h, :], start=True,
                                         stop=True)
                for h in range(HEADS):
                    last = nc.tensor.matmul(psum[6][:, hc(h)], Xm[:, h, :], Rm[:, h, :], start=True,
                                            stop=True)
                last.then_inc(N["level_mm"], 1)
                yield
            pe.wait_ge(N["level_upd"], UPB[t + 1])
            pe.wait_ge(N["pooled"], 3 * t + 1)
            for h in range(HEADS):
                last = nc.tensor.matmul(psum[7][:, hc(h)], kbg[:, h, :], Rm[:, h, :], start=True,
                                        stop=True)
            last.then_inc(N["w_mm"], 1)
            yield

        def gdn_state_pe(pe, t):
            pe.wait_ge(N["nw"], t + 1)
            pe.wait_ge(N["pooled"], 3 * t + 3)
            pe.wait_ge(N["S_ready"], 4 * t + 1)
            for h in range(HEADS):
                nc.tensor.matmul(psum[5][:, hc(h)], Rm[:, h, :], tok[:, t, 8 + h, :], start=True,
                                 stop=False)
                last = nc.tensor.matmul(psum[5][:, hc(h)], nwT[:, h, :], S_p[:, h, :], start=False,
                                        stop=True)
            last.then_inc(N["u_mm"], 1)
            yield
            pe.wait_ge(N["u_copied"], t + 1)
            for h in range(HEADS):
                nc.tensor.matmul(psum[6][:, hc(h)], qdT[:, h, :], S_p[:, h, :], start=True,
                                 stop=False)
                last = nc.tensor.matmul(psum[6][:, hc(h)], QKT[:, h, :], u_sb[:, h, :], start=False,
                                        stop=True)
            last.then_inc(N["o_mm"], 1)
            for h in range(HEADS):
                last = nc.tensor.matmul(psum[7][:, hc(h)], kd[:, h, :], u_sb[:, h, :], start=True,
                                        stop=True)
            last.then_inc(N["o_mm"], 1)
            yield

        def diag(t):
            flat = t[:].rearrange("p b c -> p (b c)")
            full = bass.AP(tensor=flat.tensor, offset=flat.offset,
                           ap=[flat.ap[0], [P + STEP, STREAMS], [1, STEP]])
            return full

        def streams_pool(pool):
            st = io["state_gdn"][0]

            def load(h):
                if h >= 2:
                    pool.wait_ge(s_ss_out[h % 2], 16 * (h // 2))
                pool.dma_start(S_s[h % 2][:], st[:, h].rearrange("b k v -> k b v"))\
                    .then_inc(s_ss_in[h % 2], 16)

            load(0)
            pool.wait_ge(N["kk"], 10)
            load(1)
            for h in range(HEADS):
                pool.wait_ge(N["ss_ready"], 3 * h + 3)
                pool.dma_start(io["gdn_sample"][0][:, h].rearrange("b k v -> k b v"),
                               S_s[h % 2][:]).then_inc(s_ss_out[h % 2], 16)
                if h + 2 < HEADS:
                    load(h + 2)

        def streams_pe(pe):
            t = 4
            yield
            for h in range(HEADS):
                s = h % 2
                pe.wait_ge(N["exp_ready"], 2 * h + 2)
                pe.wait_ge(s_ss_in[s], 16 * (h // 2 + 1))
                if h:
                    pe.wait_ge(N["oc4"], h)
                nc.tensor.matmul(psum[6][:, hc(h)], Rm[:, h, :], tok[:, t, 8 + h, :], start=True,
                                 stop=False)
                for b in range(STREAMS):
                    last = nc.tensor.matmul(psum[6][:, hc(h)], w_exp[s][:, b, :], S_s[s][:, b, :],
                                            start=False, stop=b == STREAMS - 1)
                last.then_inc(N["u4_mm"], 1)
                yield
                pe.wait_ge(N["ue_ready"], 2 * h + 2)
                if h:
                    pe.wait_ge(N["ss_ready"], 3 * h)
                for b in range(STREAMS):
                    nc.tensor.matmul(psum[6][:, hc(h)], qd_exp[s][:, b, :], S_s[s][:, b, :],
                                     start=b == 0, stop=False)
                nc.tensor.matmul(psum[6][:, hc(h)], QKT[:, h, :], u_sb[:, h, :], start=False,
                                 stop=True)
                for half in range(2):
                    last = nc.tensor.matmul(psum[7 - 2 * half], kd[:, h, :],
                                            u_exp[:, 4 * half:4 * half + 4, :], start=True, stop=True)
                last.then_inc(N["o4_mm"], 1)
                yield

        def streams_act(act):
            yield
            for h in range(HEADS):
                yield
                act.wait_ge(N["o4_mm"], h + 1)
                nc.scalar.activation(tok[:, 4, h, :], psum[6][:, hc(h)], ACT.Copy)\
                    .then_inc(N["oc4"], 1)
                yield

        def streams_dve(dve):
            dve.wait_ge(N["level_upd"], UPB[5])
            dve.wait_ge(N["w_mm"], 5)
            for s in range(2):
                V.memset(w_exp[s][:], 0.0).then_inc(N["zero_exp"], 1)
                V.memset(qd_exp[s][:], 0.0).then_inc(N["zero_exp"], 1)
            dve.wait_ge(N["nw"], 5)

            def expand(h):
                s = h % 2
                dve.wait_ge(N["zero_exp"], 2 * s + 2)
                if h >= 2:
                    dve.wait_ge(N["o4_mm"], h - 1)
                V.tensor_copy(diag(w_exp[s]), nwT[:, h, :].rearrange("p (b s) -> p b s", s=STEP))\
                    .then_inc(N["exp_ready"], 1)
                V.tensor_copy(diag(qd_exp[s]), qdT[:, h, :].rearrange("p (b s) -> p b s", s=STEP))\
                    .then_inc(N["exp_ready"], 1)

            expand(0)
            yield
            for h in range(HEADS):
                S = S_s[h % 2]
                if h + 1 < HEADS:
                    expand(h + 1)
                dve.wait_ge(N["u4_mm"], h + 1)
                V.tensor_copy(u_sb[:, h, :], psum[6][:, hc(h)]).then_inc(N["ue_ready"], 1)
                dve.wait_ge(N["ue_ready"], 2 * h + 1)
                V.tensor_tensor(u_exp[:], over(u_sb[:, h, :], STREAMS), bc(const("rowmask"), P),
                                ALU.mult).then_inc(N["ue_ready"], 1)
                yield
                dve.wait_ge(N["o4_mm"], h + 1)
                V.tensor_tensor(S[:], S[:], bc(gls[:, h, :], P), ALU.mult)\
                    .then_inc(N["ss_ready"], 1)
                dve.wait_ge(N["ss_ready"], 3 * h + 1)
                for half in range(2):
                    part = S[:, 4 * half:4 * half + 4, :]
                    V.tensor_tensor(part, part, b4(7 - 2 * half), ALU.add)\
                        .then_inc(N["ss_ready"], 1)
                yield

        def gdn_out_dve(dve):
            o4 = tok[:, :, 0:4, :]
            dve.wait_ge(N["og_act"], TT)
            ssum = gates[:, G_A].rearrange("p t h -> p (t h)")
            link(dve, "og_chain", 1, V.tensor_reduce(
                ssum, o_sq[:].rearrange("p t (h d) -> p (t h) d", d=P), AX.X, ALU.add))
            link(dve, "og_chain", 2, V.tensor_scalar(gt(G_B), gt(G_A), 1.0 / P, EPS, ALU.mult,
                                                     ALU.add))
            V.reciprocal(gt(G_C), gt(G_B)).then_inc(N["og_chain"], 1)
            dve.wait_ge(N["og_act"], TT + 1)
            for t in range(TT):
                n = 3 + 2 * t
                o = tok[:, t, 0:4, :]
                link(dve, "og_chain", n + 1, V.tensor_tensor(o, o, bc(gates[:, G_D, t, :], P),
                                                             ALU.mult))
                link(dve, "og_chain", n + 2, V.tensor_tensor(o, o, over(gdn_gain[:], HEADS),
                                                             ALU.mult))
                zt = z[:, t, :].rearrange("p (h d) -> p h d", d=P)
                V.tensor_tensor(zt, zt, o, ALU.mult).then_inc(N["og_done"], 1)

        def gdn_out_act(act):
            act.wait_ge(N["o_copied"], 4)
            act.wait_ge(N["ss_ready"], 12)
            act.wait_ge(N["oc4"], 4)
            for t in range(TT):
                nc.scalar.activation(o_sq[:, t, :].rearrange("p (h d) -> p h d", d=P),
                                     tok[:, t, 0:4, :], ACT.Square).then_inc(N["og_act"], 1)
            act.wait_ge(N["og_chain"], 3)
            nc.scalar.activation(gt(G_D), gt(G_C), ACT.Sqrt).then_inc(N["og_act"], 1)

        def qkT_pe(pe):
            pe.wait_ge(N["group_evac"], 4 * TT)
            pe.wait_ge(N["qk_done"], 4)
            for n in range(2 * TT):
                w, t = n // TT, n % TT
                if n >= 4:
                    pe.wait_ge(N["qkT_copied"], QKC[n - 3])
                for h in range(HEADS):
                    last = nc.tensor.transpose(psum[n % 4][:, hc(h)],
                                               (q_tok, k_tok)[w][:, t, hc(h)], ident)
                last.then_inc(N["qkT_mm"], 1)
                if n % 2:
                    yield

        QKC = [0, 1, 2, 3, 4, 6, 7, 8, 9, 10, 11]

        def qkT_dve(dve):
            dve.wait_ge(N["group_step"], 4 * KT)
            V.memset(q_bd[:], 0.0).then_inc(N["qbd_zero"], 1)
            for _ in range(TT):
                yield

        def qkT_act(act):
            act.wait_ge(N["qbd_zero"], 1)
            for n in range(2 * TT):
                w, t = n // TT, n % TT
                act.wait_ge(N["qkT_mm"], n + 1)
                if w == 0 and t == 4:
                    for m in range(MAPS):
                        rows = slice(DK * m, DK * m + DK)
                        nc.scalar.activation(
                            q_bd[rows, :, :, STEP * m:STEP * m + STEP].rearrange(
                                "p b h s -> p h b s"),
                            b4(n % 4)[rows].rearrange("p h (b s) -> p h b s", s=STEP), ACT.Copy)\
                            .then_inc(N["qkT_copied"], 1)
                else:
                    dst = (qT, kTn)[w][:, :, t * P:(t + 1) * P]
                    nc.scalar.activation(dst, b4(n % 4), ACT.Copy).then_inc(N["qkT_copied"], 1)
                if n % 2:
                    yield

        UNITS = [(qt, h) for qt in range(4) for h in range(HEADS)]

        def att_pe(pe):
            def scores(u):
                qt, h = UNITS[u]
                n = P * (qt + 1)
                if u:
                    pe.wait_ge(N["probs"], 2 * u)
                for m in range(MAPS):
                    rows = slice(DK * m, DK * m + DK)
                    nc.tensor.matmul(psum[m][:, 0:n], qT[rows, h, qt * P:(qt + 1) * P],
                                     kTn[rows, h, 0:n], start=True, stop=False,
                                     skip_group_check=True)
                    last = nc.tensor.matmul(psum[m][:, n - P:n], const("early_neg")[0:1, :],
                                            const("lvl64")[0:1, :], start=False, stop=True,
                                            skip_group_check=True)
                last.then_inc(N["sc_mm"], 1)

            def transposes(u):
                qt, h = UNITS[u]
                pe.wait_ge(N["pcomb"], u + 1)
                if u:
                    pe.wait_ge(N["p_copied"], u)
                for k in range(qt + 1):
                    last = nc.tensor.transpose(psum[2][:, hc(k)], pc[:, hc(k)], ident)
                last.then_inc(N["p_tr"], 1)

            def values(u):
                qt, h = UNITS[u]
                pe.wait_ge(N["p_copied"], u + 1)
                if u:
                    pe.wait_ge(N["pv_copied"], u)
                for k in range(qt + 1):
                    last = nc.tensor.matmul(psum[3][:, 0:P], pT[:, hc(k)], v_tok[:, k, hc(h)],
                                            start=k == 0, stop=k == qt)
                last.then_inc(N["pv_mm"], 1)

            pe.wait_ge(N["qkT_copied"], 11)
            for u in range(len(UNITS) + 1):
                if u < len(UNITS):
                    scores(u)
                if u:
                    transposes(u - 1)
                yield
                if u:
                    values(u - 1)
                yield

        def att_dve(dve):
            for u, (qt, h) in enumerate(UNITS):
                n = P * (qt + 1)
                dve.wait_ge(N["sc_mm"], u + 1)
                c = 4 * u
                both = psum_all[:, 0:2, 0:n]
                link(dve, "att_chain", c + 1, V.tensor_reduce(soft[:, 0:2], both, AX.X, ALU.max))
                V.tensor_scalar(soft[:, 2:4], soft[:, 0:2], -(DK ** -0.5), None, ALU.mult)\
                    .then_inc(N["nmax"], 1)
                yield
                dve.wait_ge(N["probs"], 2 * u + 2)
                link(dve, "att_chain", c + 2, V.reciprocal(soft[:, 6:8], soft[:, 4:6]))
                link(dve, "att_chain", c + 3, V.tensor_tensor(soft[:, 8:9], soft[:, 7:8],
                                                              lam[:, 7:8], ALU.mult))
                link(dve, "att_chain", c + 4, V.tensor_scalar(pr[:, 1, 0:n], pr[:, 1, 0:n],
                                                              soft[:, 8:9], None, ALU.mult))
                if u:
                    dve.wait_ge(N["p_tr"], u)
                V.scalar_tensor_tensor(pc[:, 0:n], pr[:, 0, 0:n], soft[:, 6:7], pr[:, 1, 0:n],
                                       ALU.mult, ALU.add).then_inc(N["pcomb"], 1)
                dve.wait_ge(N["pcomb"], u + 1)
                yield
            yield
            yield

        def att_act(act):
            for u in range(len(UNITS) + 1):
                if u:
                    qt, h = UNITS[u - 1]
                    n = P * (qt + 1)
                    act.wait_ge(N["p_tr"], u)
                    if u > 1:
                        act.wait_ge(N["pv_mm"], u - 1)
                    nc.scalar.activation(pT[:, 0:n], psum[2][:, 0:n], ACT.Copy)\
                        .then_inc(N["p_copied"], 1)
                yield
                if u < len(UNITS):
                    n = P * (UNITS[u][0] + 1)
                    act.wait_ge(N["nmax"], u + 1)
                    if u:
                        act.wait_ge(N["pcomb"], u)
                    for m in range(MAPS):
                        nc.scalar.activation(pr[:, m, 0:n], psum[m][:, 0:n], ACT.Exp,
                                             bias=soft[:, 2 + m:3 + m], scale=DK ** -0.5,
                                             accum_out=soft[:, 4 + m:5 + m])\
                            .then_inc(N["probs"], 1)
                if u:
                    act.wait_ge(N["pv_mm"], u)
                    nc.scalar.activation(q_tok[:, qt, hc(h)], psum[3][:, 0:P], ACT.Copy)\
                        .then_inc(N["pv_copied"], 1)
                yield

        def cache_sync(sp):
            ck = io["cache_k"][0].rearrange("b (k p) h m d -> b p k (h m d)", p=P)
            cv = io["cache_v"][0].rearrange("b (k p) h d -> b p k (h d)", p=P)
            sp.wait_ge(N["group_step"], 4 * KT)
            sp.wait_ge(N["qkT_mm"], 2 * TT)
            sp.wait_ge(N["kv_stored"], 64)
            for b in range(STREAMS):
                if b >= 2:
                    sp.wait_ge(N["kt_mm"], 4 * (b - 1))
                sp.dma_start(K_c[b % 2][:], ck[b]).then_inc(s_K[b % 2], 16)
                if b:
                    sp.wait_ge(N["spv_mm"], b)
                sp.dma_start(V_c[:], cv[b]).then_inc(s_V, 16)
                sp.dma_start(V_n[:], v_tok[STEP * b:STEP * b + STEP, 4, :]).then_inc(s_V, 16)

        def cache_pe(pe):
            def keys(b, heads):
                pe.wait_ge(s_K[b % 2], 16 * (b // 2 + 1))
                for h in heads:
                    n = 4 * b + h
                    if n >= 2:
                        pe.wait_ge(N["kt_copied"], n - 1)
                    for k in range(4):
                        last = nc.tensor.transpose(psum[2 + n % 2][:, hc(k)], K_c[b % 2][:, k, hc(h)],
                                                   ident)
                    last.then_inc(N["kt_mm"], 1)

            def scores(b):
                pe.wait_ge(N["kt_copied"], 4 * b + 4)
                if b:
                    pe.wait_ge(N["sp_copied"], 2 * b)
                for h in range(HEADS):
                    rows = slice(32 * h, 32 * h + 32)
                    nc.tensor.matmul(psum[0][rows, :], q_bd[:, b, h, :], KTc[:, h, :], start=True,
                                     stop=True, tile_position=(0, 32 * h))
                    last = nc.tensor.matmul(psum[1][rows, 0:STEP], q_bd[:, b, h, :],
                                            kTn[:, h, PROMPT + STEP * b:PROMPT + STEP * b + STEP],
                                            start=True, stop=True, tile_position=(0, 32 * h))
                last.then_inc(N["ssc_mm"], 1)

            def turn(b):
                pe.wait_ge(N["s_comb"], b + 1)
                for k in range(4):
                    nc.tensor.matmul(psum[0][:, hc(k)], ps[:, hc(k)], Cm[:], start=True, stop=True)
                nc.tensor.matmul(psum[1][0:STEP, 0:P], ps[:, PAST:PAST + STEP], Cm[:], start=True,
                                 stop=True).then_inc(N["sp_mm"], 1)

            def values(b, heads):
                pe.wait_ge(N["sp_copied"], 2 * b + 2)
                pe.wait_ge(s_V, 32 * (b + 1))
                rows = slice(32 * (b // 2), 32 * (b // 2) + 32)
                for h in heads:
                    out = psum[4][rows, hc(h)]
                    for k in range(4):
                        nc.tensor.matmul(out, pT[:, P * k + 32 * h:P * k + 32 * h + 32],
                                         V_c[:, k, hc(h)], start=b % 2 == 0 and h == 0 and k == 0,
                                         stop=False, skip_group_check=True,
                                         tile_position=(0, 32 * (b // 2)))
                    last = nc.tensor.matmul(out, pTn[:, 32 * h:32 * h + 32], V_n[:, hc(h)],
                                            start=False, stop=True, skip_group_check=True,
                                            tile_position=(0, 32 * (b // 2)))
                if h == HEADS - 1:
                    last.then_inc(N["spv_mm"], 1)

            pe.wait_ge(N["pv_copied"], 16)
            keys(0, (0, 1))
            yield
            keys(0, (2, 3))
            yield
            scores(0)
            yield
            yield
            for b in range(STREAMS):
                if b + 1 < STREAMS:
                    keys(b + 1, (0, 1))
                yield
                turn(b)
                yield
                if b + 1 < STREAMS:
                    keys(b + 1, (2, 3))
                yield
                values(b, (0, 1))
                yield
                if b + 1 < STREAMS:
                    scores(b + 1)
                yield
                values(b, (2, 3))
                yield

        def cache_act(act):
            def key(b, h):
                act.wait_ge(N["kt_mm"], 4 * b + h + 1)
                if h == 0 and b:
                    act.wait_ge(N["ssc_mm"], b)
                act.wait_ge(N["kt_copied"], 4 * b + h)
                nc.scalar.activation(KTc[:, h, :], psum[2 + h % 2], ACT.Copy)\
                    .then_inc(N["kt_copied"], 1)

            def probs(b):
                act.wait_ge(N["s_nmax"], b + 1)
                if b:
                    act.wait_ge(N["sp_mm"], b)
                nc.scalar.activation(ps[:], psum_flat[:, 0:PAST + STEP], ACT.Exp, bias=soft[:, 10:11],
                                     scale=DK ** -0.5, accum_out=soft[:, 11:12])\
                    .then_inc(N["s_probs"], 1)

            key(0, 0)
            yield
            key(0, 2)
            yield
            yield
            probs(0)
            yield
            for b in range(STREAMS):
                if b + 1 < STREAMS:
                    key(b + 1, 0)
                yield
                act.wait_ge(N["sp_mm"], b + 1)
                if b:
                    act.wait_ge(N["spv_mm"], b)
                nc.scalar.activation(pT[:], psum[0], ACT.Copy).then_inc(N["sp_copied"], 1)
                nc.scalar.activation(pTn[:], psum[1][0:STEP, 0:P], ACT.Copy)\
                    .then_inc(N["sp_copied"], 1)
                yield
                if b + 1 < STREAMS:
                    key(b + 1, 2)
                yield
                yield
                yield
                if b + 1 < STREAMS:
                    probs(b + 1)
                yield
            act.wait_ge(N["spv_mm"], STREAMS)
            nc.scalar.activation(q_tok[:, 4, :], psum[4], ACT.Copy).then_inc(N["pv_copied"], 1)

        def cache_dve(dve):
            def key(b, h):
                dve.wait_ge(N["kt_mm"], 4 * b + h + 1)
                if b:
                    dve.wait_ge(N["ssc_mm"], b)
                dve.wait_ge(N["kt_copied"], 4 * b + h)
                V.tensor_copy(KTc[:, h, :], psum[2 + h % 2]).then_inc(N["kt_copied"], 1)

            c = 4 * len(UNITS)

            def maximum(b):
                dve.wait_ge(N["ssc_mm"], b + 1)
                link(dve, "att_chain", c + 3 * b + 1,
                     V.tensor_reduce(soft[:, 9:10], psum_flat[:, 0:PAST + STEP], AX.X, ALU.max))
                V.tensor_scalar(soft[:, 10:11], soft[:, 9:10], -(DK ** -0.5), None, ALU.mult)\
                    .then_inc(N["s_nmax"], 1)

            def combine(b):
                dve.wait_ge(N["s_probs"], b + 1)
                link(dve, "att_chain", c + 3 * b + 2, V.reciprocal(soft[:, 12:13], soft[:, 11:12]))
                link(dve, "att_chain", c + 3 * b + 3,
                     V.tensor_tensor(soft[:, 13:14], soft[:, 12:13], lam[:, 6:7], ALU.mult))
                V.tensor_scalar(Cm[:], const(f"sel{b % 2}"), soft[:, 13:14], None, ALU.mult)\
                    .then_inc(N["s_comb"], 1)

            key(0, 1)
            yield
            key(0, 3)
            yield
            maximum(0)
            yield
            combine(0)
            yield
            for b in range(STREAMS):
                if b + 1 < STREAMS:
                    key(b + 1, 1)
                yield
                yield
                if b + 1 < STREAMS:
                    key(b + 1, 3)
                yield
                yield
                if b + 1 < STREAMS:
                    maximum(b + 1)
                yield
                if b + 1 < STREAMS:
                    combine(b + 1)
                yield

        def diff_out_act(act):
            act.wait_ge(N["pv_copied"], 17)
            act.wait_ge(N["spv_mm"], STREAMS)
            for t in range(TT):
                nc.scalar.activation(od_sq[:, t, :], q_tok[:, t, :], ACT.Square)\
                    .then_inc(N["od_act"], 1)
            act.wait_ge(N["od_chain"], 3)
            nc.scalar.activation(gt(G_SSQ), gt(G_SSK), ACT.Sqrt).then_inc(N["od_act"], 1)

        def diff_out_dve(dve):
            dve.wait_ge(N["od_act"], TT)
            link(dve, "od_chain", 1, V.tensor_reduce(
                gates[:, G_RQ].rearrange("p t h -> p (t h)"),
                od_sq[:].rearrange("p t (h d) -> p (t h) d", d=P), AX.X, ALU.add))
            link(dve, "od_chain", 2, V.tensor_scalar(gt(G_RK), gt(G_RQ), 1.0 / P, EPS, ALU.mult,
                                                     ALU.add))
            V.reciprocal(gt(G_SSK), gt(G_RK)).then_inc(N["od_chain"], 1)
            dve.wait_ge(N["od_act"], TT + 1)
            link(dve, "od_chain", 4, V.tensor_scalar(gt(G_E), gt(G_SSQ), 1.0 - LAM_INIT, None,
                                                     ALU.mult))
            for t in range(TT):
                o = q_tok[:, t, :].rearrange("p (h d) -> p h d", d=P)
                link(dve, "od_chain", 5 + t, V.tensor_tensor(o, o, bc(gates[:, G_E, t, :], P),
                                                             ALU.mult))
                V.tensor_tensor(o, o, over(diff_gain[:], HEADS), ALU.mult).then_inc(N["od_done"], 1)

        def wout_sync(sp):
            sp.wait_ge(N["og_done"], TT)
            sp.wait_ge(N["S_stored"], 16)
            for stored in s_ss_out:
                sp.wait_ge(stored, 32)
            for half, dst in enumerate((raw_o, raw_o1)):
                sp.dma_start(dst[:], w_out[:, :, half * BANK:(half + 1) * BANK])\
                    .then_inc(s_wo[half], 16)
            sp.dma_start(x_tok[:, 0:4, :], x_mid[0:PROMPT, :].rearrange("(t p) c -> p t c", p=P))\
                .then_inc(N["x_back"], 16)
            sp.dma_start(x_tok[:, 4, :], x_mid[PROMPT:TOK, :]).then_inc(N["x_back"], 16)
            sp.wait_ge(N["od_done"], TT)
            sp.dma_start(gain[:], io["ffn2_norm"].to_broadcast([P, D])).then_inc(s_gain[2], 16)

        def wout_act(act):
            for n in range(2 * KT):
                half, k = n // KT, n % KT
                act.wait_ge(s_wo[half], 16)
                if n >= 2:
                    act.wait_ge(N["wo_step"], n - 1)
                nc.scalar.activation(o_hi[:, n % 2], (raw_o, raw_o1)[half][:, k, :], ACT.Copy)\
                    .then_inc(N["wo_hi"], 1)

        def wout_dve(dve):
            for n in range(2 * KT):
                half, k = n // KT, n % KT
                dve.wait_ge(N["wo_hi"], n + 1)
                V.tensor_tensor(o_lo[:, n % 2], (raw_o, raw_o1)[half][:, k, :], raw(o_hi[:, n % 2]),
                                ALU.subtract).then_inc(N["wo_lo"], 1)
                if n == KT + 1:
                    dve.wait_ge(N["x_back"], 32)
                    for t in range(TT):
                        wout_residual(dve, 0, t)
            for t in range(TT):
                wout_residual(dve, 1, t)

        def wout_residual(dve, half, t):
            dve.wait_ge(N["wo_step"], (half + 1) * KT)
            cols = x_tok[:, t, half * BANK:(half + 1) * BANK]
            V.tensor_tensor(cols, psum[(half * TT + t) % 8], cols, ALU.add).then_inc(N["wo_res"], 1)

        def wout_pe(pe):
            pe.wait_ge(*on.lo(2 * TT))
            for n in range(2 * KT):
                half, k = n // KT, n % KT
                pe.wait_ge(N["wo_lo"], n + 1)
                for t in range(TT):
                    c = slice(t * P, (t + 1) * P)
                    if k == 0 and half == 1 and (TT + t) % 8 < TT:
                        pe.wait_ge(N["wo_res"], (TT + t) % 8 + 1)
                    last = three(psum[(half * TT + t) % 8], hT_hi[:, k, c], hT_lo[:, k, c],
                                 o_hi[:, n % 2], o_lo[:, n % 2], k == 0, k == KT - 1)
                last.then_inc(N["wo_step"], 1)

        s_wo = [sem(f"w_out_loaded{i}") for i in range(2)]
        psum_flat = psum_all[:].rearrange("p b c -> p (b c)")
        gls = small.put("stream_decay", [P, HEADS, STREAMS])

        def attention_steps(eng, groups, heads, prompt, cache):
            yield from groups(eng)
            yield from heads(eng)
            yield from prompt(eng)
            yield from cache(eng)

        def delta_steps(eng, tokens, gates, tile, state, streams):
            yield from tokens(eng)
            yield from gates(eng)
            for t in range(TT):
                yield from tile(eng, t)
                if t < 4 and state is not None:
                    yield from state(eng, t)
            yield from streams(eng)

        def by_turns(attention, delta):
            turn = 0
            attending = True
            while attending:
                attending = next(attention, "end") is None
                next(delta, None)
                turn += 1
            for _ in delta:
                pass

        block = ctx.enter_context(nc.Block())

        @block.sync
        def _(sp):
            sp.dma_start(x_tok[:, 0:4, :], io["x_prompt"][0].rearrange("(t p) c -> p t c", p=P))\
                .then_inc(s_x, 16)
            sp.dma_start(x_tok[:, 4, :], io["x_sample"].rearrange("b s c -> (b s) c"))\
                .then_inc(s_x, 16)
            sp.dma_start(consts[:], io["consts"]).then_inc(s_const, 16)
            sp.dma_start(gain[:], io["ffn1_norm"].to_broadcast([P, D])).then_inc(s_gain[0], 16)
            ffn_sync(sp, f1, io["ffn1_w_gu"][0], io["ffn1_w_down"][0])
            sp.wait_ge(*f1.dlo(4 + 0))
            sp.wait_ge(*f1.mm(2 * FT))
            sp.dma_start(gain[:], io["mix_norm"].to_broadcast([P, D])).then_inc(s_gain[1], 16)
            conv_sync(sp)
            cache_sync(sp)
            wout_sync(sp)
            ffn_sync(sp, f2, io["ffn2_w_gu"][0], io["ffn2_w_down"][0], N["wo_res"])
            sp.wait_ge(*f2.res(2 * TT))
            sp.dma_start(io["y_prompt"][0].rearrange("(t p) c -> p t c", p=P), x_tok[:, 0:4, :])\
                .then_inc(s_y, 16)
            sp.dma_start(io["y_sample"].rearrange("b s c -> (b s) c"), x_tok[:, 4, :])\
                .then_inc(s_y, 16)
            sp.wait_ge(s_y, 32)

        @block.gpsimd
        def _(pool):
            pool.wait_ge(N["tail_rows"], 3)
            pool.dma_start(io["conv_prompt"][0, 0], conv_out[0:3, :]).then_inc(N["tail_stored"], 16)
            pool.dma_start(io["conv_sample"][0].rearrange("b w c -> (b w) c"), conv_out[3:27, :])\
                .then_inc(N["tail_stored"], 16)
            pool.wait_ge(N["x_spilled"], 32)
            for t in range(TT):
                gdn_pool(pool, t)
                if t == 3:
                    pool.wait_ge(N["S_ready"], 17)
                    pool.dma_start(io["gdn_prompt"][0, 0].rearrange("h k v -> k h v"), S_p[:])\
                        .then_inc(N["S_stored"], 16)
            streams_pool(pool)
            pool.wait_ge(N["S_stored"], 16)
            for stored in s_ss_out:
                pool.wait_ge(stored, 32)

        @block.scalar
        def _(act):
            norm_act(act, f1.n, lambda e, t: e.wait_ge(s_x, 32) if t == 0 else None)
            ffn_act(act, f1)
            norm_act(act, mn, lambda e, t: e.wait_ge(*f1.res(6 + t)))
            conv_act(act)
            by_turns(attention_steps(act, group_act, qkT_act, att_act, cache_act),
                     delta_steps(act, tok_act, gate_act, gdn_act, None, streams_act))
            gdn_out_act(act)
            diff_out_act(act)
            split_act(act, on)
            wout_act(act)
            norm_act(act, f2.n, lambda e, t: e.wait_ge(N["wo_res"], 6 + t))
            ffn_act(act, f2)

        @block.vector
        def _(dve):
            dve.wait_ge(s_gain[0], 16)
            norm_dve(dve, f1.n)
            ffn_dve(dve, f1)
            dve.wait_ge(s_gain[1], 16)
            norm_dve(dve, mn)
            dve.wait_ge(*mn.lo(2 * TT))
            conv_dve(dve)
            by_turns(attention_steps(dve, group_dve, qkT_dve, att_dve, cache_dve),
                     delta_steps(dve, tok_dve, gate_dve, gdn_dve, gdn_state_dve, streams_dve))
            gdn_out_dve(dve)
            diff_out_dve(dve)
            for t in range(TT):
                split_dve(dve, on, t)
            wout_dve(dve)
            dve.wait_ge(s_gain[2], 16)
            norm_dve(dve, f2.n)
            ffn_dve(dve, f2)

        @block.tensor
        def _(pe):
            pe.wait_ge(s_const, 16)
            norm_pe(pe, f1.n)
            ffn_pe(pe, f1)
            norm_pe(pe, mn)
            conv_pe(pe)
            by_turns(attention_steps(pe, group_pe, qkT_pe, att_pe, cache_pe),
                     delta_steps(pe, tok_pe, gate_pe, gdn_pe, gdn_state_pe, streams_pe))
            norm_pe(pe, on, lambda t, c: (z if c < BANK else q_tok)[:, t, c % BANK:c % BANK + P],
                    lambda e, t, half: e.wait_ge(N["od_done" if half else "og_done"], t + 1))
            wout_pe(pe)
            norm_pe(pe, f2.n)
            ffn_pe(pe, f2)


INPUTS = """x_prompt x_sample cache_k cache_v state_gdn state_conv ffn1_norm ffn1_w_gu ffn1_w_down
    mix_norm w_in conv_w a_log dt_bias gdn_out_norm q_norm k_norm lambda_q lambda_k diff_out_norm
    w_out ffn2_norm ffn2_w_gu ffn2_w_down""".split()
OUTPUTS = {
    "y_prompt": (1, PROMPT, D), "y_sample": (STREAMS, STEP, D),
    "k_prompt": (1, 1, PROMPT, HEADS, MAPS, DK), "v_prompt": (1, 1, PROMPT, HEADS, P),
    "gdn_prompt": (1, 1, HEADS, P, P), "conv_prompt": (1, 1, 3, CONV_T * P),
    "k_sample": (1, STREAMS, STEP, HEADS, MAPS, DK), "v_sample": (1, STREAMS, STEP, HEADS, P),
    "gdn_sample": (1, STREAMS, HEADS, P, P), "conv_sample": (1, STREAMS, 3, CONV_T * P),
}


def kernel(**inputs):
    from concourse import bacc
    from concourse.bass_utils import run_bass_kernel_spmd

    nc = bacc.Bacc("TRN2", target_bir_lowering=False, num_devices=1)
    arrays, io = {}, {}
    consts, rotary = constants()
    for name, a in [(n, inputs[n]) for n in INPUTS] + [("consts", consts), ("rotary", rotary)]:
        a = np.ascontiguousarray(a)
        arrays[name] = a
        io[name] = nc.dram_tensor(name, a.shape, mybir.dt.from_np(a.dtype), kind="ExternalInput").ap()
    for name, shape in OUTPUTS.items():
        io[name] = nc.dram_tensor(name, shape, F32, kind="ExternalOutput").ap()
    build(nc, io)
    r = run_bass_kernel_spmd(nc, [arrays], core_ids=[0])
    return tuple(r.results[0][name] for name in OUTPUTS)
```

```python
import math
from contextlib import ExitStack

import numpy as np

import concourse.bass as bass
from concourse import mybir

F32 = mybir.dt.float32
F32R = mybir.dt.float32r
ALU = mybir.AluOpType
ACT = mybir.ActivationFunctionType
AX = mybir.AxisListType

P = 128
D = 1024
KT = D // P
PROMPT = 512
STREAMS, STEP = 8, 16
TOK = PROMPT + STREAMS * STEP
TT = TOK // P
FF = 2816
FT = FF // P
HALF = TOK // 2
EPS = 1e-6
BANK = 512

ARENA = 16640
ARENA_END = 229368


IN_COLS = 3592
HEADS = 4
DK = 64
MAPS = 2
CONV_T = 12
BA_COL, Z_COL = 1536, 1544
PAST = 512
LAM_INIT = 0.8 - 0.6 * math.exp(0.0)
NEG = -1e30
LEVELS = [1, 2, 4, 8, 16, 32, 64]


def const_layout():
    widths = [("ident", P), ("ones", P), ("cum_p", P), ("cum_s", P), ("blk_s", P)]
    widths += [(f"lvl{n}", P) for n in LEVELS]
    widths += [("sel0", P), ("sel1", P), ("rowmask", STREAMS), ("map0", 1), ("map1", 1), ("early_neg", P)]
    at, out = 0, {}
    for name, w in widths:
        out[name] = (at, w)
        at += w
    return out, at


CONST, CONST_COLS = const_layout()


def constants():
    c = np.zeros((P, CONST_COLS), np.float32)

    def put(name, a):
        at, w = CONST[name]
        c[:, at:at + w] = a

    i = np.arange(P)
    row, col = i[:, None], i[None, :]
    put("ident", row == col)
    put("ones", 1.0)
    same = row // STEP == col // STEP
    put("cum_p", row <= col)
    put("cum_s", (row <= col) & same)
    put("blk_s", same)
    for n in LEVELS:
        put(f"lvl{n}", (row // (2 * n) == col // (2 * n)) & (row // n % 2 == 0) & (col // n % 2 == 1))
    h, m, q = row // 32, row % 32 // STEP, row % STEP
    for par in range(2):
        put(f"sel{par}", col == 32 * h + STEP * par + q)
    put("rowmask", row // STEP == np.arange(STREAMS)[None, :])
    put("map0", m == 0)
    put("map1", -(m == 1).astype(np.float32))
    pos = np.concatenate([np.arange(PROMPT), PAST + np.arange(STREAMS * STEP) % STEP]).astype(np.float32)
    inv = np.float32(500000.0) ** (-np.arange(8, dtype=np.float32) * np.float32(2.0) / np.float32(16.0))
    ang = (pos[:, None] * inv[None, :]).astype(np.float32).reshape(TT, P, 8).transpose(1, 0, 2)
    put("early_neg", np.where(col < 64, NEG, 0.0))
    return c, np.concatenate([np.cos(ang).reshape(P, -1), np.sin(ang).reshape(P, -1)], 1)


class Region:

    def __init__(self, nc, start, end):
        self.nc, self.at, self.end = nc, start, end

    def put(self, name, shape, dtype=F32):
        size = 4 * int(np.prod(shape[1:]))
        size = (size + 31) // 32 * 32
        assert self.at + size <= self.end, (name, self.at + size - self.end)
        t = self.nc.alloc_sbuf_tensor_at(name, shape, dtype, offset=self.at)
        self.at += size
        return t


def raw(t):
    return t.bitcast(F32)


def build(nc, io):
    ctx = ExitStack()
    sem = lambda name: ctx.enter_context(nc.semaphore(name))
    with ctx:
        keep = Region(nc, ARENA, ARENA_END)
        x_tok = keep.put("x_tok", [P, TT, D])
        h_at = keep.at
        hT_hi = keep.put("hT_hi", [P, KT, TOK], F32R)
        hT_lo = keep.put("hT_lo", [P, KT, TOK], F32R)
        h_end = keep.at
        gain_at = keep.at
        gain = keep.put("gain", [P, D])
        x_norm = keep.put("x_norm", [P, 2, D])
        sq_junk = keep.put("sq_junk", [P, D])
        scratch_end = keep.at
        stats = keep.put("stats", [P, 4, TT])
        consts = keep.put("consts", [P, CONST_COLS])

        def const(name):
            at, w = CONST[name]
            return consts[:, at:at + w]

        ident = const("ident")
        F0 = keep.at

        ffn_mem = Region(nc, F0, ARENA_END)
        aT = ffn_mem.put("aT", [P, FT, TOK])
        ffn_mem.at = ring_at = ffn_mem.at + 1024
        raw_gu = ffn_mem.put("raw_gu", [P, 2, 2, KT, P])
        gu_hi = ffn_mem.put("gu_hi", [P, 2, 2, KT, P], F32R)
        gu_lo = ffn_mem.put("gu_lo", [P, 2, 2, KT, P], F32R)
        silu_gate = ffn_mem.put("silu_gate", [P, 2, TOK])
        ring_end = ffn_mem.at
        CH = [(0, 2), (2, 6), (6, 14), (14, 22)]
        wd = [[None] * 4, [None] * 4]
        wd[0][0] = ffn_mem.put("wd00", [P, 2, BANK])
        wd[0][1] = ffn_mem.put("wd01", [P, 4, BANK])
        over_h = Region(nc, h_at, h_end)
        wd[0][2] = over_h.put("wd02", [P, 8, BANK])
        wd[0][3] = over_h.put("wd03", [P, 8, BANK])
        wd[1][1] = over_h.put("wd11", [P, 4, BANK])
        over_ring = Region(nc, ring_at, ring_end)
        a_hi = over_ring.put("a_hi", [P, 2, TOK], F32R)
        a_lo = over_ring.put("a_lo", [P, 2, TOK], F32R)
        wd_hi = over_ring.put("wd_hi", [P, 2, BANK], F32R)
        wd_lo = over_ring.put("wd_lo", [P, 2, BANK], F32R)
        wd[1][2] = over_ring.put("wd12", [P, 8, BANK])
        wd[1][3] = over_ring.put("wd13", [P, 8, BANK])
        wd[1][0] = nc.alloc_sbuf_tensor_at("wd10", [P, 2, BANK], F32, offset=over_ring.at) \
            if over_ring.at + 4096 <= ring_end else x_norm[:, 0, :].rearrange("p (a b) -> p a b", a=2)

        psum_all = ctx.enter_context(nc.psum_tensor("psum_all", [P, 8, BANK], F32))
        psum = [psum_all[:, i, :] for i in range(8)]

        s_ident = sem("identity_loaded")
        s_const = sem("const_loaded")
        s_x = [sem(f"x_loaded{i}") for i in range(4)]
        s_gain = [sem(f"gain_loaded{i}") for i in range(3)]
        s_y = sem("y_stored")

        class Count:

            def __init__(self, of, base):
                self.sem, self.base = of, base

            def __call__(self, n):
                return self.sem, self.base + n

        norm_sems = {n: sem(f"norm_{w}") for n, w in dict(
            sq="mean_square",
            var="inverse",
            rstd="root",
            xn="scaled",
            tr="transposed",
            hi="hi",
            lo="lo").items()}
        NORM_STEPS = dict(sq=TT, var=2 * TT, rstd=TT, xn=TT, tr=2 * TT, hi=2 * TT, lo=2 * TT)

        class Norm:

            def __init__(self, r):
                rounds = r - (r == 3)
                self.sq, self.var, self.rstd, self.xn = (
                    Count(norm_sems[n], NORM_STEPS[n] * rounds) for n in ("sq", "var", "rstd", "xn"))
                self.tr, self.hi, self.lo = (
                    Count(norm_sems[n], NORM_STEPS[n] * r) for n in ("tr", "hi", "lo"))

        ffn_sems = {n: sem(f"ffn_{w}") for n, w in dict(
            hi="gate_up_hi", lo="gate_up_lo",
            mm="gate_up_product",
            silu="silu",
            a="hidden",
            dhi="down_hi", dlo="down_lo",
            dmm="down_step",
            out="down_product",
            res="residual").items()}
        FFN_STEPS = dict(hi=2 * FT, lo=2 * FT, mm=2 * FT, silu=2 * FT, a=2 * FT, dhi=4 * FT,
                         dlo=4 * FT, dmm=2 * (FT - 1), out=2 * TT, res=2 * TT)
        gu_loaded = [sem(f"ffn_gate_up_loaded{i}") for i in range(2)]
        down_loaded = [[sem(f"ffn_down_loaded{h}{c}") for c in range(4)] for h in range(2)]

        class Ffn:

            def __init__(self, r, norm):
                self.n = norm
                self.w = [Count(q, 16 * FT * r) for q in gu_loaded]
                self.wd = [[Count(q, 16 * r) for q in qs] for qs in down_loaded]
                (self.hi, self.lo, self.mm, self.silu, self.a, self.dhi, self.dlo, self.dmm,
                 self.out, self.res) = (Count(ffn_sems[n], FFN_STEPS[n] * r) for n in
                                        "hi lo mm silu a dhi dlo dmm out res".split())

        f1, f2 = Ffn(0, Norm(0)), Ffn(1, Norm(3))

        def norm_act(act, s, x_ready, ahead=lambda act: None):
            def square(t):
                x_ready(act, t)
                if t:
                    act.wait_ge(*s.sq(t))
                nc.scalar.activation(sq_junk[:], x_tok[:, t, :], ACT.Square,
                                     accum_out=stats[:, 0, t:t + 1]).then_inc(s.sq.sem, 1)

            def root(t):
                act.wait_ge(*s.var(2 * t + 2))
                nc.scalar.activation(stats[:, 2, t:t + 1], stats[:, 1, t:t + 1], ACT.Sqrt)\
                    .then_inc(s.rstd.sem, 1)

            square(0)
            square(1)
            root(0)
            square(2)
            root(1)
            root(2)
            split_act(act, s, 0, 4)
            ahead(act)
            split_act(act, s, 4, 6)
            square(3)
            square(4)
            root(3)
            root(4)
            split_act(act, s, 6, 2 * TT)

        def norm_bank(n):
            return 4 + n % 4

        def split_act(act, s, first, end):
            for n in range(first, end):
                t, half = n // 2, n % 2
                act.wait_ge(*s.tr(n + 1))
                nc.scalar.activation(
                    hT_hi[:, 4 * half:4 * half + 4, t * P:(t + 1) * P],
                    psum[norm_bank(n)].rearrange("p (k c) -> p k c", k=4), ACT.Copy).then_inc(s.hi.sem, 1)

        def norm_dve(dve, s, gain_ready, residual=lambda t: None, ahead=lambda dve: None):
            def inverse(t):
                dve.wait_ge(*s.sq(t + 1))
                nc.vector.tensor_scalar(stats[:, 3, t:t + 1], stats[:, 0, t:t + 1], 1.0 / D, EPS,
                                        ALU.mult, ALU.add).then_inc(s.var.sem, 1)
                dve.wait_ge(*s.var(2 * t + 1))
                nc.vector.reciprocal(stats[:, 1, t:t + 1], stats[:, 3, t:t + 1])\
                    .then_inc(s.var.sem, 1)

            def scale(t):
                dve.wait_ge(*s.rstd(t + 1))
                if t >= 2:
                    dve.wait_ge(*s.tr(2 * (t - 1)))
                nc.vector.scalar_tensor_tensor(x_norm[:, t % 2, :], x_tok[:, t, :],
                                               stats[:, 2, t:t + 1], gain[:], ALU.mult,
                                               ALU.mult).then_inc(s.xn.sem, 1)

            residual(0)
            residual(1)
            inverse(0)
            residual(2)
            inverse(1)
            dve.wait_ge(gain_ready, 16)
            scale(0)
            inverse(2)
            scale(1)
            split_dve(dve, s, 0)
            scale(2)
            split_dve(dve, s, 1)
            residual(3)
            ahead(dve)
            split_dve(dve, s, 2)
            residual(4)
            inverse(3)
            scale(3)
            inverse(4)
            scale(4)
            split_dve(dve, s, 3)
            split_dve(dve, s, 4)

        def split_dve(dve, s, t):
            for half in range(2):
                n = 2 * t + half
                dve.wait_ge(*s.hi(n + 1))
                cols = (slice(None), slice(4 * half, 4 * half + 4), slice(t * P, (t + 1) * P))
                nc.vector.tensor_tensor(
                    hT_lo[cols], psum[norm_bank(n)].rearrange("p (k c) -> p k c", k=4),
                    raw(hT_hi[cols]), ALU.subtract).then_inc(s.lo.sem, 1)

        def norm_pe(pe, s, tiles):
            for n in range(2 * tiles[0], 2 * tiles[-1] + 2):
                t, half = n // 2, n % 2
                if half == 0:
                    pe.wait_ge(*s.xn(t + 1))
                if n >= 4:
                    pe.wait_ge(*s.lo(n - 3))
                for k in range(4):
                    c = (4 * half + k) * P
                    last = nc.tensor.transpose(psum[norm_bank(n)][:, k * P:(k + 1) * P],
                                               x_norm[:, t % 2, c:c + P], ident)
                last.then_inc(s.tr.sem, 1)

        def bank_pair(which, slot):
            b = 4 * slot + 2 * which
            return psum[b], psum[b + 1]

        def ffn_sync(sp, s, w_gu, w_down, before=None, first=lambda: None):
            gu = w_gu.rearrange("(k p) c -> p k c", p=P)
            def load(j, slot):
                for which in range(2):
                    sp.dma_start(raw_gu[:, slot, which],
                                 gu[:, :, bass.ds(which * FF + j * P, P)]).then_inc(s.w[slot].sem, 16)

            load(0, 0)
            load(1, 1)
            first()
            dn = w_down.rearrange("(k p) c -> p k c", p=P)

            def load_down(half, c):
                a, b = CH[c]
                sp.dma_start(wd[half][c][:, :, :], dn[:, a:b, half * BANK:(half + 1) * BANK])\
                    .then_inc(s.wd[half][c].sem, 16)

            if before is not None:
                sp.wait_ge(before, 2 * TT)
            with sp.Fori(1, FT // 2) as pair:
                j = 2 * pair
                for slot in range(2):
                    sp.wait_ge(*s.lo(2 * (j + slot) - 2))
                    load(j + slot, slot)
            load_down(0, 0)
            load_down(0, 1)
            sp.wait_ge(*s.mm(2 * FT))
            load_down(0, 2)
            load_down(0, 3)
            load_down(1, 0)
            load_down(1, 1)
            sp.wait_ge(*s.a(2 * FT))
            load_down(1, 2)
            load_down(1, 3)

        def gu_split_act(act, s, j, slot):
            act.wait_ge(*s.w[slot](16 * (j - slot) + 32))
            for which in range(2):
                nc.scalar.activation(gu_hi[:, slot, which], raw_gu[:, slot, which],
                                     ACT.Copy).then_inc(s.hi.sem, 1)

        def gu_split_dve(dve, s, j, slot):
            for which in range(2):
                dve.wait_ge(*s.hi(2 * j + which + 1))
                nc.vector.tensor_tensor(gu_lo[:, slot, which], raw_gu[:, slot, which],
                                        raw(gu_hi[:, slot, which]), ALU.subtract)\
                    .then_inc(s.lo.sem, 1)

        def ffn_act(act, s):
            def silu(j, slot):
                g = bank_pair(0, slot)
                act.wait_ge(*s.mm(2 * j + 1))
                for part in range(2):
                    nc.scalar.activation(silu_gate[:, slot, part * HALF:(part + 1) * HALF],
                                         g[part][:, 0:HALF], ACT.Silu).then_inc(s.silu.sem, 1)

            def down_split(half, c, j, slot):
                a, _ = CH[c]
                nc.scalar.activation(a_hi[:, slot, :], aT[:, j, :], ACT.Copy).then_inc(s.dhi.sem, 1)
                nc.scalar.activation(wd_hi[:, slot, :], wd[half][c][:, j - a, :], ACT.Copy)\
                    .then_inc(s.dhi.sem, 1)

            gu_split_act(act, s, 1, 1)
            silu(0, 0)
            with act.Fori(1, FT // 2) as pair:
                j = 2 * pair
                act.wait_ge(*s.mm(2 * j - 2))
                gu_split_act(act, s, j, 0)
                act.wait_ge(*s.a(2 * j - 2))
                silu(j - 1, 1)
                act.wait_ge(*s.mm(2 * j))
                gu_split_act(act, s, j + 1, 1)
                act.wait_ge(*s.a(2 * j - 2))
                silu(j, 0)
            act.wait_ge(*s.lo(2 * FT))
            act.wait_ge(*s.mm(2 * FT - 2))
            act.wait_ge(*s.wd[0][0](16))
            down_split(0, 0, 0, 0)
            act.wait_ge(*s.a(2 * (FT - 2)))
            silu(FT - 1, 1)

            for half in range(2):
                for c, (a, b) in enumerate(CH):
                    act.wait_ge(*s.wd[half][c](16))
                    if c == 0:
                        for slot in range(2):
                            if half == 0:
                                if slot == 0:
                                    continue
                                act.wait_ge(*s.mm(2 * FT))
                                act.wait_ge(*s.a(2 * FT))
                            elif slot == 0:
                                act.wait_ge(*s.dmm(FT - 1))
                            else:
                                act.wait_ge(*s.out(TT))
                            down_split(half, 0, slot, slot)
                        continue
                    with act.Fori(a // 2, b // 2) as pair:
                        j = 2 * pair
                        for slot in range(2):
                            act.wait_ge(*s.dmm(half * (FT - 1) + j + slot - 1))
                            down_split(half, c, j + slot, slot)

        def ffn_dve(dve, s, finish=True):
            def hidden(j, slot):
                dve.wait_ge(*s.mm(2 * j + 2))
                u = bank_pair(1, slot)
                for part in range(2):
                    dve.wait_ge(*s.silu(2 * j + part + 1))
                    nc.vector.tensor_tensor(aT[:, j, part * HALF:(part + 1) * HALF],
                                            silu_gate[:, slot, part * HALF:(part + 1) * HALF],
                                            u[part][:, 0:HALF], ALU.mult).then_inc(s.a.sem, 1)

            gu_split_dve(dve, s, 1, 1)
            hidden(0, 0)
            with dve.Fori(1, FT // 2) as pair:
                j = 2 * pair
                gu_split_dve(dve, s, j, 0)
                hidden(j - 1, 1)
                gu_split_dve(dve, s, j + 1, 1)
                hidden(j, 0)

            def down_split(half, c, j, slot):
                a, _ = CH[c]
                n = 2 * (half * FT + j)
                dve.wait_ge(*s.dhi(n + 1))
                nc.vector.tensor_tensor(a_lo[:, slot, :], aT[:, j, :], raw(a_hi[:, slot, :]),
                                        ALU.subtract).then_inc(s.dlo.sem, 1)
                dve.wait_ge(*s.dhi(n + 2))
                nc.vector.tensor_tensor(wd_lo[:, slot, :], wd[half][c][:, j - a, :],
                                        raw(wd_hi[:, slot, :]), ALU.subtract).then_inc(s.dlo.sem, 1)

            down_split(0, 0, 0, 0)
            hidden(FT - 1, 1)
            down_split(0, 0, 1, 1)
            for half in range(2):
                for c, (a, b) in enumerate(CH):
                    if half == 0 and c == 0:
                        continue
                    with dve.Fori(a // 2, b // 2) as pair:
                        j = 2 * pair
                        for slot in range(2):
                            down_split(half, c, j + slot, slot)
                    if half == 1 and c == 0:
                        for t in range(TT):
                            residual(dve, s, 0, t)
            for t in range(TT if finish else 0):
                residual(dve, s, 1, t)

        def residual(dve, s, half, t):
            dve.wait_ge(*s.out(half * TT + t + 1))
            cols = x_tok[:, t, half * BANK:(half + 1) * BANK]
            nc.vector.scalar_tensor_tensor(cols, psum[(half * TT + t) % 8], 0.5, cols,
                                           ALU.mult, ALU.add).then_inc(s.res.sem, 1)

        def three(out, lhs_hi, lhs_lo, rhs_hi, rhs_lo, start, stop):
            nc.tensor.matmul(out, lhs_hi, rhs_hi, start=start, stop=False, skip_group_check=True)
            nc.tensor.matmul(out, lhs_hi, rhs_lo, start=False, stop=False, skip_group_check=True)
            return nc.tensor.matmul(out, lhs_lo, rhs_hi, start=False, stop=stop,
                                    skip_group_check=True)

        def ffn_pe(pe, s):
            def gate_up(j, slot):
                for which in range(2):
                    for k in range(KT):
                        for part in range(2):
                            tok = slice(part * HALF, (part + 1) * HALF)
                            last = three(bank_pair(which, slot)[part][:, 0:HALF],
                                         gu_hi[:, slot, which, k, :], gu_lo[:, slot, which, k, :],
                                         hT_hi[:, k, tok], hT_lo[:, k, tok], k == 0, k == KT - 1)
                    last.then_inc(s.mm.sem, 1)

            pe.wait_ge(*s.lo(2))
            for part in range(2):
                pe.wait_ge(*s.n.lo((6, 2 * TT)[part]))
                for which in range(2):
                    for k in range(KT):
                        tok = slice(part * HALF, (part + 1) * HALF)
                        last = three(bank_pair(which, 0)[part][:, 0:HALF],
                                     gu_hi[:, 0, which, k, :], gu_lo[:, 0, which, k, :],
                                     hT_hi[:, k, tok], hT_lo[:, k, tok], k == 0, k == KT - 1)
                    if part == 0:
                        norm_pe(pe, s.n, (3 + which,))
                    else:
                        last.then_inc(s.mm.sem, 1)
            pe.wait_ge(*s.lo(4))
            gate_up(1, 1)
            with pe.Fori(1, FT // 2) as pair:
                j = 2 * pair
                for slot in range(2):
                    pe.wait_ge(*s.lo(2 * (j + slot) + 2))
                    pe.wait_ge(*s.a(2 * (j + slot) - 2))
                    gate_up(j + slot, slot)

            def down(half, j, slot, start, stop):
                pe.wait_ge(*s.dlo(2 * (half * FT + j) + 2))
                for t in range(TT):
                    if start and half == 0 and t == 4:
                        pe.wait_ge(*s.silu(2 * FT))
                    if start and half == 1 and (TT + t) % 8 < TT:
                        pe.wait_ge(*s.res((TT + t) % 8 + 1))
                    tok = slice(t * P, (t + 1) * P)
                    last = three(psum[(half * TT + t) % 8], a_hi[:, slot, tok],
                                 a_lo[:, slot, tok], wd_hi[:, slot, :], wd_lo[:, slot, :],
                                 start, stop)
                    if stop:
                        last.then_inc(s.out.sem, 1)
                return last

            pe.wait_ge(*s.a(2 * FT - 2))
            for half in range(2):
                for slot in range(2):
                    down(half, slot, slot, slot == 0, False).then_inc(s.dmm.sem, 1)
                with pe.Fori(1, FT // 2 - 1) as pair:
                    j = 2 * pair
                    for slot in range(2):
                        down(half, j + slot, slot, False, False).then_inc(s.dmm.sem, 1)
                down(half, FT - 2, 0, False, False).then_inc(s.dmm.sem, 1)
                down(half, FT - 1, 1, False, True)

        small = Region(nc, gain_at, scratch_end)
        xp = small.put("xp", [P, 2, 668])
        sq_rows = [nc.alloc_sbuf_tensor_at(f"sq_rows{i}", [P, BANK], F32, offset=gain_at + 2048 * i)
                   for i in range(2)]
        rope_tmp = small.put("rope_tmp", [P, 4, TT * 64])
        rot = small.put("rot", [P, 2, TT, 8])
        gdn_gain = small.put("gdn_gain", [P, P])
        diff_gain = small.put("diff_gain", [P, P])
        qk_gain = small.put("qk_gain", [P, 2, DK])
        lam_in = small.put("lam_in", [P, 2, 2, DK])
        head_par = small.put("head_par", [P, 2, HEADS])
        gates = small.put("gates", [P, 20, TT, HEADS])
        ba = small.put("ba", [P, TT, 8])
        lam = small.put("lam", [P, 8])
        qk_ss = small.put("qk_ss", [P, 2, 3, TT * 8])
        soft = small.put("soft", [P, 16])

        mixm = Region(nc, F0, ARENA_END)
        z = mixm.put("z", [P, TT, BANK])
        q_tok = mixm.put("q_tok", [P, TT, BANK])
        k_at = mixm.at
        k_tok = mixm.put("k_tok", [P, TT, BANK])
        v_at = mixm.at
        v_tok = mixm.put("v_tok", [P, TT, BANK])
        tok_at = mixm.at
        tok = mixm.put("tok", [P, TT, CONV_T, P])
        c_at = mixm.at
        cT = mixm.put("cT", [P, CONV_T, TOK])
        c_end = d_at = mixm.at
        cv_hi = mixm.put("cv_hi", [P, 2, KT, P], F32R)
        cv_lo = mixm.put("cv_lo", [P, 2, KT, P], F32R)
        raw_cv = mixm.put("raw_cv", [P, 2, KT, P])
        d_end = mixm.at
        kb_mem = Region(nc, k_at, v_at)
        hist = kb_mem.put("hist", [P, CONV_T, 28])
        tail = kb_mem.put("tail", [P, CONV_T, 27])
        vb_mem = Region(nc, v_at, tok_at)
        conv_out = vb_mem.put("conv_out", [27, CONV_T * P])
        baT = vb_mem.put("baT", [8, TOK])
        conv_rows = Region(nc, tok_at, c_at).put("conv_rows", [28, CONV_T * P])
        dm = Region(nc, d_at, d_end)
        b_hi = dm.put("b_hi", [P, 2, BANK], F32R)
        b_lo = dm.put("b_lo", [P, 2, BANK], F32R)
        raw_b = [dm.put(f"raw_b{i}", [P, 4, BANK]) for i in (1, 0)][::-1]

        g1 = Region(nc, ARENA, h_at)
        H4 = [P, HEADS, P]
        qd, knT, kbT, qnT, kbg, kd, qdT, LT, QKT = (
            g1.put(n, H4) for n in "qd knT kbT qnT kbg kd qdT LT QKT".split())
        g2 = Region(nc, c_at, c_end)
        Rm, nwT, u_sb, S_p = (g2.put(n, H4) for n in "Rm nwT u_sb S_p".split())
        tx_at = g2.at
        Tm, Xm = g2.put("Tm", H4), g2.put("Xm", H4)
        ct_at = g2.at
        CT = [g2.put(f"CT{i}", H4) for i in range(2)]
        u_exp = nc.alloc_sbuf_tensor_at("u_exp", [P, STREAMS, P], F32, offset=ct_at)
        ge_at = g2.at
        gbc, ET = g2.put("gbc", H4), g2.put("ET", H4)
        rows_of = lambda name, at: nc.alloc_sbuf_tensor_at(name, [P, STREAMS, 2 * STEP], F32,
                                                           offset=at)
        qd_exp = [rows_of("qd_exp0", ge_at), rows_of("qd_exp1", tx_at)]
        S_s = [g2.put("S_s0", [P, STREAMS, P]),
               *(nc.alloc_sbuf_tensor_at(f"S_s{i + 1}", [P, STREAMS, P], F32,
                                         offset=ARENA + 4096 * i) for i in range(2))]
        w_exp = [rows_of("w_exp0", ge_at + 2048), rows_of("w_exp1", tx_at + 2048)]

        a1 = Region(nc, h_at, h_end)
        qT = a1.put("qT", [P, HEADS, PROMPT])
        kTn = a1.put("kTn", [P, HEADS, TOK])
        q_bd = a1.put("q_bd", [P, STREAMS, HEADS, 32])
        KTc = a1.put("KTc", [P, HEADS, PAST])
        pc = a1.put("pc", [P, BANK])
        a2 = Region(nc, d_at, d_end)
        K_c = [a2.put("K_c0", [P, 4, BANK]),
               nc.alloc_sbuf_tensor_at("K_c1", [P, 4, BANK], F32, offset=k_at)]
        V_c = a2.put("V_c", [P, 4, BANK])
        V_c = [V_c, nc.alloc_sbuf_tensor_at("V_c1", [P, 4, BANK], F32, offset=v_at)]
        V_n = [a2.put("V_n0", [STEP, BANK]), a1.put("V_n1", [STEP, BANK])]
        p_at = a2.at
        pr = a2.put("pr", [P, 2, BANK])
        ps = nc.alloc_sbuf_tensor_at("ps", [P, PAST + STEP], F32, offset=p_at)
        Cm = nc.alloc_sbuf_tensor_at("Cm", [P, P], F32, offset=p_at + 3072)
        pT = a1.put("pT", [P, BANK])
        pTn = a2.put("pTn", [STEP, P])
        od_sq = nc.alloc_sbuf_tensor_at("od_sq", [P, 4, BANK], F32, offset=h_at)
        od_sq4 = nc.alloc_sbuf_tensor_at("od_sq4", [P, 1, BANK], F32, offset=d_at)
        raw_o = [nc.alloc_sbuf_tensor_at(f"raw_o{i}", [P, KT, BANK], F32, offset=at)
                 for i, at in enumerate((tok_at, k_at))]
        wout = Region(nc, d_end - 8192, d_end)
        o_hi = wout.put("o_hi", [P, 2, BANK], F32R)
        o_lo = wout.put("o_lo", [P, 2, BANK], F32R)

        mn, on = Norm(1), Norm(2)
        N = {n: sem(n) for n in """
            x_spilled x_back params_loaded conv_rows_loaded hist_transposed hist_ready pad_zero
            conv_hi conv_lo conv_product conv_padded conv_sum conv_silu tail_transposed tail_rows
            tail_stored baT_copied ba_tr ba_copied
            group_hi group_lo group_step group_evac row_squares row_sums kv_stored
            lam_chain qk_chain act_qk qk_done
            tok_tr tok_copied tok_sq tok_sums gate_chain gate_act g_product cs_ready rk_root
            scaled pooled tr_scaled act_T kbT_ready diff decay_exp decay kk masked ct r0 t0 t0c x_mm
            x_copied level_mm level_upd w_mm nw u_mm u_copied o_mm o_copied S_ready S_stored
            exp_ready zero_exp u4_mm ue_ready o4_mm oc4 ss_ready gls
            z_gained og_chain og_act og_done
            qbd_zero qkT_mm qkT_copied sc_mm nmax probs pcomb p_tr p_copied pv_mm pv_copied att_chain
            kt_mm kt_copied ssc_mm s_nmax s_probs s_comb sp_mm sp_copied spv_mm 
            od_chain od_act od_done wo_hi wo_lo wo_step wo_out wo_res 
            """.split()}
        s_cvw = [sem(f"conv_loaded{i}") for i in range(2)]
        s_gw = [sem(f"group_loaded{i}") for i in range(2)]
        s_K = [sem(f"k_cache_loaded{i}") for i in range(2)]
        s_V = [sem(f"v_cache_loaded{i}") for i in range(2)]
        s_ss_in = [sem(f"stream_state_loaded{i}") for i in range(2)]
        s_ss_out = [sem(f"stream_state_stored{i}") for i in range(2)]

        x_mid = nc.dram_tensor("x_mid", [TOK, D], F32, kind="Internal").ap()
        w_in = io["w_in"][0].rearrange("(k p) c -> p k c", p=P)
        w_out = io["w_out"][0].rearrange("(k p) c -> p k c", p=P)
        V = nc.vector

        def link(eng, s, n, ins):
            ins.then_inc(N[s], 1)
            eng.wait_ge(N[s], n)

        def bc(ap, n):
            return ap.unsqueeze(2).broadcast_to([ap.shape[0], ap.shape[1], n])

        def over(ap, n):
            return ap.unsqueeze(1).broadcast_to([ap.shape[0], n, ap.shape[1]])

        def conv_sync(sp):
            rows = conv_rows[:]

            def load(j, slot):
                sp.dma_start(raw_cv[:, slot], w_in[:, :, bass.ds(j * P, P)]).then_inc(s_cvw[slot], 16)

            sp.wait_ge(*f1.out(TT))
            load(0, 0)
            load(1, 1)
            sp.wait_ge(*f1.out(2 * TT))
            sp.dma_start(rows[0:24, :], io["state_conv"][0].rearrange("b w c -> (b w) c"))\
                .then_inc(N["conv_rows_loaded"], 16)
            sp.dma_start(rows[24:28, :], io["conv_w"][0]).then_inc(N["conv_rows_loaded"], 16)

            for slot in range(2):
                sp.wait_ge(N["conv_lo"], slot + 1)
                load(2 + slot, slot)
            sp.wait_ge(*mn.lo(2 * TT))
            for dst, src in ((gdn_gain[:], io["gdn_out_norm"].to_broadcast([P, P])),
                             (diff_gain[:], io["diff_out_norm"].to_broadcast([P, P])),
                             (qk_gain[:, 0, :], io["q_norm"].to_broadcast([P, DK])),
                             (qk_gain[:, 1, :], io["k_norm"].to_broadcast([P, DK])),
                             (lam_in[:, 0], io["lambda_q"].to_broadcast([P, 2, DK])),
                             (lam_in[:, 1], io["lambda_k"].to_broadcast([P, 2, DK])),
                             (head_par[:, 0, :], io["a_log"].to_broadcast([P, HEADS])),
                             (head_par[:, 1, :], io["dt_bias"].to_broadcast([P, HEADS])),
                             (rot[:], io["rotary"].rearrange("p (a t f) -> p a t f", a=2, t=TT))):
                sp.dma_start(dst, src).then_inc(N["params_loaded"], 16)
            sp.dma_start(x_mid[0:PROMPT, :].rearrange("(t p) c -> p t c", p=P), x_tok[:, 0:4, :])\
                .then_inc(N["x_spilled"], 16)
            sp.dma_start(x_mid[PROMPT:TOK, :], x_tok[:, 4, :]).then_inc(N["x_spilled"], 16)
            with sp.Fori(2, CONV_T // 2) as pair:
                j = 2 * pair
                for slot in range(2):
                    sp.wait_ge(N["conv_lo"], j + slot - 1)
                    load(j + slot, slot)
            sp.wait_ge(N["conv_lo"], CONV_T - 1)
            load(CONV_T, 0)
            for hg in range(8):
                g, kh = GROUPS[hg // 2], hg % 2
                if hg == 0:
                    sp.wait_ge(N["conv_lo"], CONV_T + 1)
                elif hg == 1:
                    sp.wait_ge(N["conv_product"], CONV_T + 1)
                else:
                    sp.wait_ge(N["group_lo"], 4 * (hg - 1))
                sp.dma_start(raw_b[hg % 2][:],
                             w_in[:, 4 * kh:4 * kh + 4, Z_COL + BANK * g:Z_COL + BANK * (g + 1)])\
                    .then_inc(s_gw[hg % 2], 16)
            sp.wait_ge(N["qk_done"], 4)
            sp.wait_ge(N["group_evac"], 3 * TT)
            for name, dims, src in (("k", "(h m d)", k_tok), ("v", "(h d)", v_tok)):
                row = dims[1:-1]
                sp.dma_start(io[f"{name}_prompt"][0, 0].rearrange(f"(t p) {row} -> p t {dims}", p=P),
                             src[:, 0:4, :]).then_inc(N["kv_stored"], 16)
                sp.dma_start(io[f"{name}_sample"][0].rearrange(f"b s {row} -> (b s) {dims}"),
                             src[:, 4, :]).then_inc(N["kv_stored"], 16)

        def conv_split_act(act, j, slot):
            act.wait_ge(s_cvw[slot], 8 * (j - slot) + 16)
            nc.scalar.activation(cv_hi[:, slot], raw_cv[:, slot], ACT.Copy)\
                .then_inc(N["conv_hi"], 1)

        def conv_split_dve(dve, j, slot):
            dve.wait_ge(N["conv_hi"], j + 1)
            V.tensor_tensor(cv_lo[:, slot], raw_cv[:, slot], raw(cv_hi[:, slot]), ALU.subtract)\
                .then_inc(N["conv_lo"], 1)

        def conv_act(act):
            split = lambda j, slot: conv_split_act(act, j, slot)

            def pad(j, slot):
                act.wait_ge(N["conv_product"], j + 1)
                a, b = psum[2 * slot], psum[2 * slot + 1]
                x = xp[:, slot, :]
                for dst, src in ((x[:, 3:3 + HALF], a[:, 0:HALF]),
                                 (x[:, 3 + HALF:3 + PROMPT], b[:, 0:PROMPT - HALF]),
                                 (streams(x)[:, :, 3:19],
                                  b[:, PROMPT - HALF:HALF].rearrange("p (b s) -> p b s", s=STEP))):
                    nc.scalar.activation(dst, src, ACT.Copy).then_inc(N["conv_padded"], 1)

            def silu(j):
                act.wait_ge(N["conv_sum"], 11 * j + 11)
                nc.scalar.activation(cT[:, j, :], cT[:, j, :], ACT.Silu).then_inc(N["conv_silu"], 1)

            split(1, 1)
            act.wait_ge(N["pad_zero"], 1)
            pad(0, 0)
            with act.Fori(1, CONV_T // 2) as pair:
                j = 2 * pair
                act.wait_ge(N["conv_product"], j - 1)
                split(j, 0)
                act.wait_ge(N["conv_sum"], 11 * j - 21)
                pad(j - 1, 1)
                silu(j - 2)
                act.wait_ge(N["conv_product"], j)
                split(j + 1, 1)
                act.wait_ge(N["conv_sum"], 11 * j - 11)
                pad(j, 0)
                silu(j - 1)
            act.wait_ge(N["conv_product"], CONV_T - 1)
            split(CONV_T, 0)
            act.wait_ge(N["conv_sum"], 11 * (CONV_T - 2))
            pad(CONV_T - 1, 1)
            silu(CONV_T - 2)
            silu(CONV_T - 1)
            act.wait_ge(N["conv_product"], CONV_T + 1)
            for part in range(2):
                nc.scalar.activation(baT[:, part * HALF:(part + 1) * HALF], psum[part][0:8, 0:HALF],
                                     ACT.Copy).then_inc(N["baT_copied"], 1)

        def streams(x):
            return x[:, 515:667].rearrange("p (b s) -> p b s", s=19)

        def conv_dve(dve):
            conv_split_dve(dve, 1, 1)
            V.memset(xp[:, :, 0:3], 0.0).then_inc(N["pad_zero"], 1)
            dve.wait_ge(N["hist_transposed"], 1)
            V.tensor_copy(hist[:], psum[7][:, 0:336].rearrange("p (c w) -> p c w", w=28))\
                .then_inc(N["hist_ready"], 1)
            dve.wait_ge(N["hist_ready"], 1)

            split = lambda j, slot: conv_split_dve(dve, j, slot)

            def conv(j, slot):
                x, s, n = xp[:, slot, :], N["conv_sum"], 11 * j
                V.tensor_copy(streams(x)[:, :, 0:3],
                              hist[:, j, 0:24].rearrange("p (b w) -> p b w", w=3)).then_inc(s, 1)
                dve.wait_ge(N["conv_padded"], 3 * j + 3)
                V.tensor_copy(tail[:, j, 0:3], x[:, PROMPT:PROMPT + 3]).then_inc(s, 1)
                V.tensor_copy(tail[:, j, 3:27].rearrange("p (b w) -> p b w", w=3),
                              streams(x)[:, :, 16:19]).then_inc(s, 1)
                yp = cT[:, j, 0:PROMPT]
                yq = cT[:, j, PROMPT:TOK].rearrange("p (b s) -> p b s", s=STEP)
                for i in range(4):
                    w = hist[:, j, 24 + i:25 + i]
                    if i == 0:
                        dve.wait_ge(s, n + 1)
                        V.tensor_scalar(yp, x[:, 0:PROMPT], w, None, ALU.mult).then_inc(s, 1)
                        V.tensor_scalar(yq, streams(x)[:, :, 0:16], w, None, ALU.mult).then_inc(s, 1)
                    else:
                        dve.wait_ge(s, n + 2 + 2 * i)
                        V.scalar_tensor_tensor(yp, x[:, i:i + PROMPT], w, yp, ALU.mult,
                                               ALU.add).then_inc(s, 1)
                        dve.wait_ge(s, n + 3 + 2 * i)
                        V.scalar_tensor_tensor(yq, streams(x)[:, :, i:i + 16], w, yq, ALU.mult,
                                               ALU.add).then_inc(s, 1)

            conv(0, 0)
            with dve.Fori(1, CONV_T // 2) as pair:
                j = 2 * pair
                split(j, 0)
                dve.wait_ge(N["conv_sum"], 11 * j - 11)
                conv(j - 1, 1)
                split(j + 1, 1)
                dve.wait_ge(N["conv_sum"], 11 * j)
                conv(j, 0)
            split(CONV_T, 0)
            dve.wait_ge(N["conv_sum"], 11 * (CONV_T - 1))
            conv(CONV_T - 1, 1)
            for i in range(3):
                dve.wait_ge(N["tail_transposed"], i + 1)
                V.tensor_copy(conv_out[:, i * BANK:(i + 1) * BANK], psum[5 + i][0:27, :])\
                    .then_inc(N["tail_rows"], 1)

        def conv_pe(pe):
            def product(j, slot):
                for k in range(KT):
                    for part in range(2):
                        t = slice(part * HALF, (part + 1) * HALF)
                        last = three(psum[2 * slot + part][:, 0:HALF], cv_hi[:, slot, k, :],
                                     cv_lo[:, slot, k, :], hT_hi[:, k, t], hT_lo[:, k, t],
                                     k == 0, k == KT - 1)
                last.then_inc(N["conv_product"], 1)

            pe.wait_ge(N["conv_lo"], 1)
            for part in range(2):
                pe.wait_ge(*mn.lo((6, 2 * TT)[part]))
                t = slice(part * HALF, (part + 1) * HALF)
                for k in range(KT):
                    last = three(psum[part][:, 0:HALF], cv_hi[:, 0, k, :], cv_lo[:, 0, k, :],
                                 hT_hi[:, k, t], hT_lo[:, k, t], k == 0, k == KT - 1)
                if part == 0:
                    norm_pe(pe, mn, (3, 4))
            last.then_inc(N["conv_product"], 1)
            pe.wait_ge(N["conv_rows_loaded"], 32)
            for c in range(CONV_T):
                last = nc.tensor.transpose(psum[7][:, 28 * c:28 * c + 28],
                                           conv_rows[:, c * P:(c + 1) * P], ident[0:28, 0:28])
            last.then_inc(N["hist_transposed"], 1)
            pe.wait_ge(N["conv_lo"], 2)
            product(1, 1)
            with pe.Fori(1, CONV_T // 2) as pair:
                for slot in range(2):
                    j = 2 * pair + slot
                    pe.wait_ge(N["conv_lo"], j + 1)
                    pe.wait_ge(N["conv_padded"], 3 * j - 3)
                    product(j, slot)
            pe.wait_ge(N["conv_lo"], CONV_T + 1)
            pe.wait_ge(N["conv_padded"], 3 * (CONV_T - 1))
            product(CONV_T, 0)
            pe.wait_ge(N["conv_sum"], 11 * CONV_T)
            for i in range(3):
                for c in range(4):
                    last = nc.tensor.transpose(psum[5 + i][0:27, c * P:(c + 1) * P],
                                               tail[:, 4 * i + c, :], ident)
                last.then_inc(N["tail_transposed"], 1)

        GROUPS = (1, 2, 3, 0)

        def group_act(act):
            def split(n):
                act.wait_ge(s_gw[n // 4 % 2], 16 * (n // 8 + 1))
                if n >= 2:
                    act.wait_ge(N["group_step"], n - 1)
                else:
                    act.wait_ge(N["conv_product"], CONV_T + 1)
                nc.scalar.activation(b_hi[:, n % 2], raw_b[n // 4 % 2][:, n % 4], ACT.Copy)\
                    .then_inc(N["group_hi"], 1)

            def square(i, t):
                m = i * TT + t
                if m < 2:
                    act.wait_ge(N["conv_sum"], 11 * CONV_T)
                else:
                    act.wait_ge(N["row_sums"], m - 1)
                act.wait_ge(N["group_evac"], m + 1)
                nc.scalar.activation(sq_rows[m % 2][:], (q_tok, k_tok)[i][:, t, :], ACT.Square)\
                    .then_inc(N["row_squares"], 1)

            rope = qk_act(act)
            split(0)
            for n in range(4 * KT):
                i, k = n // KT, n % KT
                if i and k == 0:
                    for t in range(3):
                        evac(act, i - 1, t)
                if n + 1 < 4 * KT:
                    split(n + 1)
                yield
                if i and k == 0:
                    evac(act, i - 1, 3)
                    evac(act, i - 1, 4)
                if i in (1, 2) and 1 <= k <= TT:
                    square(i - 1, k - 1)
                if n >= ROPE_FROM:
                    next(rope, None)
                yield
            for t in range(TT):
                evac(act, 3, t)
            yield

        ROPE_FROM = KT + 6

        def evac(act, i, t):
            act.wait_ge(N["group_step"], (i + 1) * KT)
            if i == 1 and t == 0:
                act.wait_ge(N["tail_transposed"], 3)
            if i == 2 and t == 0:
                act.wait_ge(N["tail_stored"], 32)
            dst = (q_tok, k_tok, v_tok, z)[i][:, t, :]
            nc.scalar.activation(dst, psum[t], ACT.Silu if i == 3 else ACT.Copy)\
                .then_inc(N["group_evac"], 1)

        def group_dve(dve):
            def split(n):
                dve.wait_ge(N["group_hi"], n + 1)
                V.tensor_tensor(b_lo[:, n % 2], raw_b[n // 4 % 2][:, n % 4],
                                raw(b_hi[:, n % 2]), ALU.subtract).then_inc(N["group_lo"], 1)

            rope = qk_dve(dve)
            split(0)
            for n in range(4 * KT):
                i, k = n // KT, n % KT
                if n + 1 < 4 * KT:
                    split(n + 1)
                yield
                if i in (1, 2) and 1 <= k <= TT:
                    m = (i - 1) * TT + k - 1
                    dve.wait_ge(N["row_squares"], m + 1)
                    V.tensor_reduce(qk_ss[:, i - 1, 0, 8 * (k - 1):8 * k],
                                    sq_rows[m % 2][:].rearrange("p (c d) -> p c d", d=DK), AX.X,
                                    ALU.add).then_inc(N["row_sums"], 1)
                if n >= ROPE_FROM:
                    next(rope, None)
                yield
            yield

        def group_pe(pe):
            for n in range(4 * KT):
                i, k = n // KT, n % KT
                pe.wait_ge(N["group_lo"], n + 1)
                for t in range(TT):
                    if t == 3:
                        yield
                    if k == 0 and i:
                        pe.wait_ge(N["group_evac"], (i - 1) * TT + t + 1)
                    if n == 0 and t == 0:
                        pe.wait_ge(N["conv_padded"], 3 * CONV_T)
                        pe.wait_ge(N["baT_copied"], 2)
                    c = slice(t * P, (t + 1) * P)
                    last = three(psum[t], hT_hi[:, k, c], hT_lo[:, k, c], b_hi[:, n % 2],
                                 b_lo[:, n % 2], k == 0, k == KT - 1)
                last.then_inc(N["group_step"], 1)
                yield
            yield

        def qk_dve(dve):
            dve.wait_ge(N["params_loaded"], 16 * 9)
            prod = lam_in[:, 0]
            link(dve, "lam_chain", 1, V.tensor_tensor(prod, lam_in[:, 0], lam_in[:, 1], ALU.mult))
            V.tensor_reduce(lam[:, 0:2], prod, AX.X, ALU.add).then_inc(N["lam_chain"], 1)
            yield
            dve.wait_ge(N["act_qk"], 1)
            link(dve, "lam_chain", 3, V.tensor_tensor(lam[:, 4:5], lam[:, 2:3], lam[:, 3:4],
                                                      ALU.subtract))
            link(dve, "lam_chain", 4, V.tensor_scalar(lam[:, 5:6], lam[:, 4:5], LAM_INIT, None,
                                                      ALU.add))
            link(dve, "lam_chain", 5, V.scalar_tensor_tensor(
                lam[:, 6:7], const("map1"), lam[:, 5:6], const("map0"), ALU.mult, ALU.add))
            link(dve, "lam_chain", 6, V.tensor_scalar(lam[:, 7:8], lam[:, 5:6], -1.0, None, ALU.mult))
            yield
            for w, x in enumerate((q_tok, k_tok)):
                n = 10 * w
                dve.wait_ge(N["row_sums"], TT * (w + 1))
                dve.wait_ge(N["group_evac"], TT * (w + 1))
                link(dve, "qk_chain", n + 1, V.tensor_scalar(qk_ss[:, w, 1, :], qk_ss[:, w, 0, :],
                                                             1.0 / DK, EPS, ALU.mult, ALU.add))
                V.reciprocal(qk_ss[:, w, 2, :], qk_ss[:, w, 1, :]).then_inc(N["qk_chain"], 1)
                yield
                dve.wait_ge(N["act_qk"], w + 2)
                for p, (a, b) in enumerate(((0, 2), (2, TT))):
                    rows = x[:, a:b, :].rearrange("p t (c d) -> p (t c) d", d=DK)
                    link(dve, "qk_chain", n + 2 * p + 3, V.tensor_tensor(
                        rows, rows, bc(qk_ss[:, w, 0, 8 * a:8 * b], DK), ALU.mult))
                    yield
                    link(dve, "qk_chain", n + 2 * p + 4, V.tensor_tensor(
                        rows, rows, over(qk_gain[:, w, :], (b - a) * 8), ALU.mult))
                    yield
                v4 = x[:].rearrange("p t (c d) -> p t c d", d=DK)
                x1, x2 = v4[:, :, :, 0:8], v4[:, :, :, 8:16]
                tmp = [rope_tmp[:, i, :].rearrange("p (t c d) -> p t c d", c=8, d=8)
                       for i in range(4)]
                cos, sin = (rot[:, i].unsqueeze(2).broadcast_to([P, TT, 8, 8]) for i in range(2))
                for i, (a, f) in enumerate(((x1, cos), (x2, sin), (x2, cos), (x1, sin))):
                    V.tensor_tensor(tmp[i], a, f, ALU.mult).then_inc(N["qk_chain"], 1)
                yield
                dve.wait_ge(N["qk_chain"], n + 10)
                V.tensor_tensor(x1, tmp[0], tmp[1], ALU.subtract).then_inc(N["qk_done"], 1)
                V.tensor_tensor(x2, tmp[2], tmp[3], ALU.add).then_inc(N["qk_done"], 1)
                dve.wait_ge(N["qk_done"], 2 * w + 2)
                yield

        def qk_act(act):
            act.wait_ge(N["lam_chain"], 2)
            nc.scalar.activation(lam[:, 2:4], lam[:, 0:2], ACT.Exp).then_inc(N["act_qk"], 1)
            yield
            yield
            for w in range(2):
                act.wait_ge(N["qk_chain"], 10 * w + 2)
                nc.scalar.activation(qk_ss[:, w, 0, :], qk_ss[:, w, 2, :], ACT.Sqrt)\
                    .then_inc(N["act_qk"], 1)
                for _ in range(7):
                    yield

        (G_BETA, G_G, G_CUM, G_TOT, G_EC, G_ER, G_ET, G_RQ, G_RK, G_KB, G_KBG, G_KD, G_QD, G_A,
         G_B, G_C, G_D, G_SSQ, G_SSK, G_E) = range(20)
        gt = lambda i: gates[:, i]
        GB = [5, 6, 7]

        def tok_pe(pe):
            pe.wait_ge(N["tail_rows"], 3)
            for t in range(TT):
                last = nc.tensor.transpose(psum[7][:, 8 * t:8 * t + 8], baT[:, t * P:(t + 1) * P],
                                           ident[0:8, 0:8])
            last.then_inc(N["ba_tr"], 1)
            yield
            pe.wait_ge(N["conv_silu"], CONV_T)
            pe.wait_ge(N["ba_copied"], 1)
            for t in range(TT):
                for w in range(3):
                    n = 3 * t + w
                    if n >= 3:
                        pe.wait_ge(N["tok_copied"], n - 2)
                    for h in range(HEADS):
                        last = nc.tensor.transpose(psum[GB[w]][:, h * P:(h + 1) * P],
                                                   cT[:, 4 * w + h, t * P:(t + 1) * P], ident)
                    last.then_inc(N["tok_tr"], 1)
                yield
                yield

        def tok_dve(dve):
            dve.wait_ge(N["ba_tr"], 1)
            V.tensor_copy(ba[:], psum[7][:, 0:40].rearrange("p (t c) -> p t c", c=8))\
                .then_inc(N["ba_copied"], 1)
            yield
            for t in range(TT):
                for w in range(3):
                    dve.wait_ge(N["tok_tr"], 3 * t + w + 1)
                    V.tensor_copy(tok[:, t, 4 * w:4 * w + 4, :],
                                  psum[GB[w]].rearrange("p (h d) -> p h d", d=P))\
                        .then_inc(N["tok_copied"], 1)
                yield
                for w in range(2):
                    dve.wait_ge(N["tok_sq"], 2 * t + w + 1)
                    V.tensor_reduce(gates[:, G_SSQ + w, t, :], (kbg, kd)[w][:], AX.X, ALU.add)\
                        .then_inc(N["tok_sums"], 1)
                yield
            dve.wait_ge(N["tok_sums"], 2 * TT)

        def tok_act(act):
            yield
            act.wait_ge(N["x_spilled"], 32)
            for t in range(TT):
                yield
                for w in range(2):
                    act.wait_ge(N["tok_copied"], 3 * t + w + 1)
                    if t:
                        act.wait_ge(N["tok_sums"], 2 * t + w - 1)
                    nc.scalar.activation((kbg, kd)[w][:], tok[:, t, 4 * w:4 * w + 4, :],
                                         ACT.Square).then_inc(N["tok_sq"], 1)
                yield

        def gate_dve(dve):
            c = [0]

            def l(ins):
                c[0] += 1
                link(dve, "gate_chain", c[0], ins)

            beta_in, a_in = ba[:, :, 0:4], ba[:, :, 4:8]
            dt = over(head_par[:, 1, :], TT)
            l(V.tensor_tensor(gt(G_A), a_in, dt, ALU.add))
            l(V.tensor_scalar(gt(G_B), gt(G_A), -1.0, None, ALU.mult))
            l(V.tensor_tensor(gt(G_B), gt(G_A), gt(G_B), ALU.min))
            yield
            dve.wait_ge(N["gate_act"], 3)
            l(V.tensor_scalar(gt(G_C), gt(G_C), 1.0, None, ALU.add))
            l(V.reciprocal(gt(G_BETA), gt(G_C)))
            l(V.tensor_scalar(gt(G_A), gt(G_A), 0.0, None, ALU.max))
            l(V.tensor_tensor(gt(G_A), gt(G_A), gt(G_D), ALU.add))
            l(V.scalar_tensor_tensor(gt(G_G), gt(G_A), -1.0, over(head_par[:, 0, :], TT), ALU.mult,
                                     ALU.mult))
            yield
            dve.wait_ge(N["g_product"], 1)
            l(V.tensor_copy(gt(G_CUM), psum[6][:, 0:20].rearrange("p (t h) -> p t h", h=4)))
            l(V.tensor_copy(gt(G_TOT), psum[6][:, 32:52].rearrange("p (t h) -> p t h", h=4)))
            l(V.tensor_tensor(gt(G_E), gt(G_TOT), gt(G_CUM), ALU.subtract))
            ss = gates[:, G_SSQ:G_SSQ + 2]
            l(V.tensor_scalar(gates[:, G_A:G_A + 2], ss, EPS, None, ALU.add))
            l(V.reciprocal(gates[:, G_C:G_C + 2], gates[:, G_A:G_A + 2]))
            yield
            dve.wait_ge(N["gate_act"], 7)
            l(V.tensor_scalar(gt(G_RQ), gt(G_RQ), float(P) ** -0.5, None, ALU.mult))
            l(V.tensor_tensor(gt(G_KB), gt(G_RK), gt(G_BETA), ALU.mult))
            l(V.tensor_tensor(gt(G_KBG), gt(G_KB), gt(G_EC), ALU.mult))
            l(V.tensor_tensor(gt(G_KD), gt(G_RK), gt(G_ER), ALU.mult))
            V.tensor_tensor(gt(G_QD), gt(G_RQ), gt(G_EC), ALU.mult).then_inc(N["cs_ready"], 1)
            dve.wait_ge(N["cs_ready"], 1)
            V.memset(S_p[:], 0.0).then_inc(N["S_ready"], 1)
            yield

        def gate_act(act):
            act.wait_ge(N["gate_chain"], 3)
            nc.scalar.activation(gt(G_C), ba[:, :, 0:4], ACT.Exp, scale=-1.0)\
                .then_inc(N["gate_act"], 1)
            nc.scalar.activation(head_par[:, 0, :], head_par[:, 0, :], ACT.Exp)\
                .then_inc(N["gate_act"], 1)
            nc.scalar.activation(gt(G_D), gt(G_B), ACT.Exp).then_inc(N["rk_root"], 1)
            act.wait_ge(N["rk_root"], 1)
            nc.scalar.activation(gt(G_D), gt(G_D), ACT.Ln, bias=1.0).then_inc(N["gate_act"], 1)
            yield
            yield
            act.wait_ge(N["gate_chain"], 11)
            for dst, src in ((G_EC, G_CUM), (G_ER, G_E), (G_ET, G_TOT)):
                nc.scalar.activation(gt(dst), gt(src), ACT.Exp).then_inc(N["gate_act"], 1)
            act.wait_ge(N["gate_chain"], 13)
            nc.scalar.activation(gates[:, G_RQ:G_RQ + 2], gates[:, G_C:G_C + 2], ACT.Sqrt)\
                .then_inc(N["gate_act"], 1)
            yield
            yield

        def gate_pe(pe):
            yield
            pe.wait_ge(N["gate_chain"], 8)
            pe.wait_ge(N["tok_copied"], 3 * TT)
            g = gt(G_G)
            nc.tensor.matmul(psum[6][:, 0:16], const("cum_p"), g[:, 0:4, :], start=True, stop=True)
            nc.tensor.matmul(psum[6][:, 16:20], const("cum_s"), g[:, 4, :], start=True, stop=True)
            nc.tensor.matmul(psum[6][:, 32:48], const("ones"), g[:, 0:4, :], start=True, stop=True)
            nc.tensor.matmul(psum[6][:, 48:52], const("blk_s"), g[:, 4, :], start=True, stop=True)\
                .then_inc(N["g_product"], 1)
            yield
            yield
            yield

        LV = [7, 7, 7, 7, 4]
        CTB = [sum(LV[:t]) for t in range(TT + 1)]
        UPB = [sum(2 * (v - 1) - 1 for v in LV[:t]) for t in range(TT + 1)]
        XB = [sum(v - 1 for v in LV[:t]) for t in range(TT + 1)]
        b4 = lambda bank: psum[bank].rearrange("p (h d) -> p h d", d=P)
        hc = lambda h: slice(h * P, (h + 1) * P)

        def gdn_dve(dve, t):
            q4, k4 = tok[:, t, 0:4, :], tok[:, t, 4:8, :]
            f = lambda i: bc(gates[:, i, t, :], P)
            if t:
                dve.wait_ge(N["o_mm"], 2 * t)
                out_sums(dve, t - 1)
            V.tensor_tensor(Xm[:], k4, f(G_RK), ALU.mult).then_inc(N["scaled"], 1)
            V.tensor_tensor(CT[1][:], k4, f(G_KB), ALU.mult).then_inc(N["scaled"], 1)
            V.tensor_tensor(CT[0][:], q4, f(G_RQ), ALU.mult).then_inc(N["scaled"], 1)
            V.tensor_tensor(qd[:], q4, f(G_QD), ALU.mult).then_inc(N["scaled"], 1)
            V.tensor_copy(gbc[:], f(G_G)).then_inc(N["scaled"], 1)
            yield
            dve.wait_ge(N["tr_scaled"], 5 * t + 2)
            V.tensor_copy(kbT[:], b4(6)).then_inc(N["kbT_ready"], 1)
            yield
            dve.wait_ge(N["tr_scaled"], 5 * t + 5)
            V.tensor_tensor(ET[:], b4(6), f(G_CUM), ALU.subtract).then_inc(N["diff"], 1)
            dve.wait_ge(N["diff"], 2 * t + 1)
            V.tensor_scalar(ET[:], ET[:], 0.0, None, ALU.min).then_inc(N["diff"], 1)
            yield
            dve.wait_ge(N["decay_exp"], t + 1)
            V.tensor_tensor(ET[:], ET[:], over(const("cum_s" if t == 4 else "cum_p"), HEADS),
                            ALU.mult).then_inc(N["decay"], 1)
            dve.wait_ge(N["decay"], t + 1)
            dve.wait_ge(N["kk"], 2 * t + 1)
            V.tensor_tensor(LT[:], b4(7), ET[:], ALU.mult).then_inc(N["masked"], 1)
            dve.wait_ge(N["kk"], 2 * t + 2)
            V.tensor_tensor(QKT[:], b4(5), ET[:], ALU.mult).then_inc(N["masked"], 1)
            yield
            dve.wait_ge(N["ct"], CTB[t] + 1)
            V.tensor_tensor(Rm[:], over(ident, HEADS), CT[0][:], ALU.subtract).then_inc(N["r0"], 1)
            yield
            yield
            n = LV[t] - 1
            for l in range(1, n + 1):
                u = UPB[t] + 2 * (l - 1)
                if l > 1:
                    dve.wait_ge(N["t0"], XB[t] + l)
                    V.tensor_copy(Rm[:], b4(6)).then_inc(N["level_upd"], 1)
                yield
                dve.wait_ge(N["level_mm"], XB[t] + l)
                if l == 1:
                    dve.wait_ge(N["t0c"], t + 1)
                else:
                    dve.wait_ge(N["level_upd"], u)
                if l < n:
                    V.tensor_tensor(Tm[:], Tm[:], b4(5), ALU.subtract).then_inc(N["level_upd"], 1)
                else:
                    V.tensor_tensor(Rm[:], Rm[:], b4(6), ALU.subtract).then_inc(N["level_upd"], 1)
                yield
            yield

        def gdn_state_dve(dve, t):
            dve.wait_ge(N["u_mm"], t + 1)
            V.tensor_copy(u_sb[:], b4(5)).then_inc(N["u_copied"], 1)
            yield
            dve.wait_ge(N["o_mm"], 2 * t + 2)
            dve.wait_ge(N["S_ready"], 4 * t + 1)
            for h in range(HEADS):
                V.scalar_tensor_tensor(S_p[:, h, :], S_p[:, h, :], gates[:, G_ET, t, h:h + 1],
                                       psum[7][:, hc(h)], ALU.mult, ALU.add)\
                    .then_inc(N["S_ready"], 1)
            yield

        def gdn_act(act, t):
            yield
            act.wait_ge(N["tr_scaled"], 5 * t + 1)
            nc.scalar.activation(knT[:], b4(5), ACT.Copy).then_inc(N["act_T"], 1)
            yield
            act.wait_ge(N["tr_scaled"], 5 * t + 3)
            nc.scalar.activation(qnT[:], b4(7), ACT.Copy).then_inc(N["act_T"], 1)
            act.wait_ge(N["tr_scaled"], 5 * t + 4)
            nc.scalar.activation(qdT[:], b4(5), ACT.Copy).then_inc(N["act_T"], 1)
            yield
            act.wait_ge(N["diff"], 2 * t + 2)
            if t == 4:
                nc.scalar.activation(gls[:], b4(6)[:, :, STEP - 1::STEP], ACT.Exp)\
                    .then_inc(N["gls"], 1)
            nc.scalar.activation(ET[:], ET[:], ACT.Exp).then_inc(N["decay_exp"], 1)
            yield
            yield
            act.wait_ge(N["t0"], XB[t] + 1)
            nc.scalar.activation(Tm[:], b4(6), ACT.Copy).then_inc(N["t0c"], 1)
            yield
            for l in range(1, LV[t]):
                act.wait_ge(N["x_mm"], XB[t] + l)
                nc.scalar.activation(Xm[:], b4(7), ACT.Copy).then_inc(N["x_copied"], 1)
                yield
                yield
            act.wait_ge(N["w_mm"], t + 1)
            nc.scalar.activation(nwT[:], b4(7), ACT.Copy, scale=-1.0).then_inc(N["nw"], 1)
            yield
            if t < 4:
                yield
                act.wait_ge(N["o_mm"], 2 * t + 1)
                nc.scalar.activation(tok[:, t, 0:4, :], b4(6), ACT.Copy).then_inc(N["o_copied"], 1)
                act.wait_ge(N["o_copied"], t + 1)
                out_squares(t)
                yield

        def out_squares(t):
            nc.scalar.activation(LT[:], tok[:, t, 0:4, :], ACT.Square).then_inc(N["og_act"], 1)

        def out_sums(dve, t):
            dve.wait_ge(N["og_act"], t + 1)
            V.tensor_reduce(gates[:, G_A, t, :], LT[:], AX.X, ALU.add).then_inc(N["og_chain"], 1)

        def gdn_pool(pool, t):
            k4, v4 = tok[:, t, 4:8, :], tok[:, t, 8:12, :]
            f = lambda i: bc(gates[:, i, t, :], P)
            if t == 0:
                pool.wait_ge(N["cs_ready"], 1)
            else:
                pool.wait_ge(N["o_mm"], 2 * t)
            nc.gpsimd.tensor_tensor(kbg[:], k4, f(G_KBG), ALU.mult).then_inc(N["pooled"], 1)
            nc.gpsimd.tensor_tensor(v4, v4, f(G_BETA), ALU.mult).then_inc(N["pooled"], 1)
            nc.gpsimd.tensor_tensor(kd[:], k4, f(G_KD), ALU.mult).then_inc(N["pooled"], 1)
            pool.wait_ge(N["masked"], 2 * t + 1)
            for i in range(LV[t]):
                if i == 2:
                    pool.wait_ge(N["r0"], t + 1)
                if i >= 3:
                    pool.wait_ge(N["x_mm"], XB[t] + i - 2)
                nc.gpsimd.tensor_tensor(CT[i % 2][:], LT[:], over(const(f"lvl{LEVELS[i]}"), HEADS),
                                        ALU.mult).then_inc(N["ct"], 1)

        def gdn_pe(pe, t):
            yield
            for i, (src, bank) in enumerate(((Xm, 5), (CT[1], 6), (CT[0], 7))):
                pe.wait_ge(N["scaled"], 5 * t + i + 1)
                if i == 1 and t:
                    pe.wait_ge(N["o_copied"], t)
                if i == 2 and t:
                    pe.wait_ge(N["S_ready"], 4 * t + 1)
                for h in range(HEADS):
                    last = nc.tensor.transpose(psum[bank][:, hc(h)], src[:, h, :], ident)
                last.then_inc(N["tr_scaled"], 1)
            yield
            pe.wait_ge(N["scaled"], 5 * t + 4)
            pe.wait_ge(N["act_T"], 3 * t + 1)
            for h in range(HEADS):
                last = nc.tensor.transpose(psum[5][:, hc(h)], qd[:, h, :], ident)
            last.then_inc(N["tr_scaled"], 1)
            pe.wait_ge(N["scaled"], 5 * t + 5)
            pe.wait_ge(N["kbT_ready"], t + 1)
            for h in range(HEADS):
                last = nc.tensor.matmul(psum[6][:, hc(h)], gbc[:, h, :],
                                        const("cum_s" if t == 4 else "cum_p"), start=True, stop=True)
            last.then_inc(N["tr_scaled"], 1)
            yield
            pe.wait_ge(N["act_T"], 3 * t + 2)
            for h in range(HEADS):
                last = nc.tensor.matmul(psum[7][:, hc(h)], knT[:, h, :], kbT[:, h, :], start=True,
                                        stop=True)
            last.then_inc(N["kk"], 1)
            pe.wait_ge(N["act_T"], 3 * t + 3)
            for h in range(HEADS):
                last = nc.tensor.matmul(psum[5][:, hc(h)], knT[:, h, :], qnT[:, h, :], start=True,
                                        stop=True)
            last.then_inc(N["kk"], 1)
            yield
            yield
            pe.wait_ge(N["r0"], t + 1)
            if t == 4:
                pe.wait_ge(N["gls"], 1)
            for h in range(HEADS):
                last = nc.tensor.transpose(psum[6][:, hc(h)], Rm[:, h, :], ident)
            last.then_inc(N["t0"], 1)
            yield
            n = LV[t] - 1
            for l in range(1, n + 1):
                pe.wait_ge(N["ct"], CTB[t] + l + 1)
                if l == 1:
                    pe.wait_ge(N["t0c"], t + 1)
                else:
                    pe.wait_ge(N["level_upd"], UPB[t] + 2 * (l - 1) - 1)
                for h in range(HEADS):
                    last = nc.tensor.matmul(psum[7][:, hc(h)], CT[l % 2][:, h, :], Tm[:, h, :],
                                            start=True, stop=True)
                last.then_inc(N["x_mm"], 1)
                if l > 1:
                    for h in range(HEADS):
                        last = nc.tensor.transpose(psum[6][:, hc(h)], Tm[:, h, :], ident)
                    last.then_inc(N["t0"], 1)
                yield
                pe.wait_ge(N["x_copied"], XB[t] + l)
                if l > 1:
                    pe.wait_ge(N["level_upd"], UPB[t] + 2 * (l - 1))
                for h in range(HEADS):
                    if l < n:
                        last = nc.tensor.matmul(psum[5][:, hc(h)], Rm[:, h, :], Xm[:, h, :],
                                                start=True, stop=True)
                    else:
                        last = nc.tensor.matmul(psum[6][:, hc(h)], Xm[:, h, :], Rm[:, h, :],
                                                start=True, stop=True)
                last.then_inc(N["level_mm"], 1)
                yield
            pe.wait_ge(N["level_upd"], UPB[t + 1])
            pe.wait_ge(N["pooled"], 3 * t + 1)
            for h in range(HEADS):
                last = nc.tensor.matmul(psum[7][:, hc(h)], kbg[:, h, :], Rm[:, h, :], start=True,
                                        stop=True)
            last.then_inc(N["w_mm"], 1)
            yield

        def gdn_state_pe(pe, t):
            pe.wait_ge(N["nw"], t + 1)
            pe.wait_ge(N["pooled"], 3 * t + 3)
            pe.wait_ge(N["S_ready"], 4 * t + 1)
            for h in range(HEADS):
                nc.tensor.matmul(psum[5][:, hc(h)], Rm[:, h, :], tok[:, t, 8 + h, :], start=True,
                                 stop=False)
                last = nc.tensor.matmul(psum[5][:, hc(h)], nwT[:, h, :], S_p[:, h, :], start=False,
                                        stop=True)
            last.then_inc(N["u_mm"], 1)
            yield
            pe.wait_ge(N["u_copied"], t + 1)
            for h in range(HEADS):
                nc.tensor.matmul(psum[6][:, hc(h)], qdT[:, h, :], S_p[:, h, :], start=True,
                                 stop=False)
                last = nc.tensor.matmul(psum[6][:, hc(h)], QKT[:, h, :], u_sb[:, h, :], start=False,
                                        stop=True)
            last.then_inc(N["o_mm"], 1)
            for h in range(HEADS):
                last = nc.tensor.matmul(psum[7][:, hc(h)], kd[:, h, :], u_sb[:, h, :], start=True,
                                        stop=True)
            last.then_inc(N["o_mm"], 1)
            yield

        def diag(t):
            flat = t[:].rearrange("p b c -> p (b c)")
            return bass.AP(tensor=flat.tensor, offset=flat.offset,
                           ap=[flat.ap[0], [64, STREAMS // 2], [32 + STEP, 2], [1, STEP]])

        SS = (0, 1, 1, 0)
        SS_COUNT = (16, 16, 32, 32)

        def streams_pool(pool):
            st = io["state_gdn"][0]

            def load(h):
                pool.dma_start(S_s[h % 3][:], st[:, h].rearrange("b k v -> k b v"))\
                    .then_inc(s_ss_in[SS[h]], 16)

            load(0)
            pool.wait_ge(N["w_mm"], 5)
            for s in range(2):
                nc.gpsimd.memset(w_exp[s][:], 0.0).then_inc(N["zero_exp"], 1)
                nc.gpsimd.memset(qd_exp[s][:], 0.0).then_inc(N["zero_exp"], 1)
            load(1)
            pool.wait_ge(s_ss_in[1], 16)
            load(2)
            for h in range(HEADS):
                pool.wait_ge(N["ss_ready"], 3 * h + 3)
                pool.dma_start(io["gdn_sample"][0][:, h].rearrange("b k v -> k b v"),
                               S_s[h % 3][:]).then_inc(s_ss_out[SS[h]], 16)
                if h == 0:
                    pool.wait_ge(s_ss_out[0], 16)
                    load(3)

        def by_stream(rows, S, h):
            for b in (0, 2, 4, 6, 1, 3, 5, 7):
                pair = 32 * (b // 2)
                last = nc.tensor.matmul(psum[6][pair:pair + 32, hc(h)], rows[:, b, :], S[:, b, :],
                                        start=False, stop=b % 2 == 1, skip_group_check=True,
                                        tile_position=(0, pair))
            return last

        def streams_pe(pe):
            t = 4
            yield
            for h in range(HEADS):
                s = h % 2
                pe.wait_ge(N["exp_ready"], 2 * h + 2)
                pe.wait_ge(s_ss_in[SS[h]], SS_COUNT[h])
                if h:
                    pe.wait_ge(N["oc4"], h)
                nc.tensor.matmul(psum[6][:, hc(h)], Rm[:, h, :], tok[:, t, 8 + h, :], start=True,
                                 stop=False, skip_group_check=True)
                by_stream(w_exp[s], S_s[h % 3], h).then_inc(N["u4_mm"], 1)
                yield
                pe.wait_ge(N["ue_ready"], 2 * h + 2)
                if h:
                    pe.wait_ge(N["ss_ready"], 3 * h)
                nc.tensor.matmul(psum[6][:, hc(h)], QKT[:, h, :], u_sb[:, h, :], start=True,
                                 stop=False, skip_group_check=True)
                by_stream(qd_exp[s], S_s[h % 3], h)
                for half in range(2):
                    last = nc.tensor.matmul(psum[7 - 2 * half], kd[:, h, :],
                                            u_exp[:, 4 * half:4 * half + 4, :], start=True, stop=True)
                last.then_inc(N["o4_mm"], 1)
                yield

        def streams_act(act):
            yield
            for h in range(HEADS):
                yield
                act.wait_ge(N["o4_mm"], h + 1)
                nc.scalar.activation(tok[:, 4, h, :], psum[6][:, hc(h)], ACT.Copy)\
                    .then_inc(N["oc4"], 1)
                yield

        def streams_dve(dve):
            dve.wait_ge(N["nw"], 5)

            def expand(h):
                s = h % 2
                dve.wait_ge(N["zero_exp"], 2 * s + 2)
                if h >= 2:
                    dve.wait_ge(N["o4_mm"], h - 1)
                V.tensor_copy(diag(w_exp[s]), nwT[:, h, :].rearrange("p (g r s) -> p g r s", r=2, s=STEP))\
                    .then_inc(N["exp_ready"], 1)
                V.tensor_copy(diag(qd_exp[s]), qdT[:, h, :].rearrange("p (g r s) -> p g r s", r=2, s=STEP))\
                    .then_inc(N["exp_ready"], 1)

            expand(0)
            yield
            for h in range(HEADS):
                S = S_s[h % 3]
                if h + 1 < HEADS:
                    expand(h + 1)
                dve.wait_ge(N["u4_mm"], h + 1)
                V.tensor_copy(u_sb[:, h, :], psum[6][:, hc(h)]).then_inc(N["ue_ready"], 1)
                dve.wait_ge(N["ue_ready"], 2 * h + 1)
                V.tensor_tensor(u_exp[:], over(u_sb[:, h, :], STREAMS), bc(const("rowmask"), P),
                                ALU.mult).then_inc(N["ue_ready"], 1)
                yield
                dve.wait_ge(N["o4_mm"], h + 1)
                V.tensor_tensor(S[:], S[:], bc(gls[:, h, :], P), ALU.mult)\
                    .then_inc(N["ss_ready"], 1)
                dve.wait_ge(N["ss_ready"], 3 * h + 1)
                for half in range(2):
                    part = S[:, 4 * half:4 * half + 4, :]
                    V.tensor_tensor(part, part, b4(7 - 2 * half), ALU.add)\
                        .then_inc(N["ss_ready"], 1)
                yield

        def gdn_out_dve(dve):
            out_sums(dve, 4)
            dve.wait_ge(N["og_chain"], TT)
            link(dve, "og_chain", TT + 1, V.tensor_scalar(gt(G_B), gt(G_A), 1.0 / P, EPS, ALU.mult,
                                                          ALU.add))
            V.reciprocal(gt(G_C), gt(G_B)).then_inc(N["og_chain"], 1)
            yield
            dve.wait_ge(N["og_act"], TT + 1)
            dve.wait_ge(N["z_gained"], TT)
            for t in range(TT):
                for h in range(HEADS):
                    last = V.scalar_tensor_tensor(z[:, t, hc(h)], tok[:, t, h, :],
                                                  gates[:, G_D, t, h:h + 1], z[:, t, hc(h)],
                                                  ALU.mult, ALU.mult)
                    last.then_inc(N["og_done"], 1)
                yield

        def gdn_out_act(act):
            act.wait_ge(N["oc4"], 4)
            act.wait_ge(N["og_chain"], 4)
            out_squares(4)
            yield
            act.wait_ge(N["og_chain"], TT + 2)
            nc.scalar.activation(gt(G_D), gt(G_C), ACT.Sqrt).then_inc(N["og_act"], 1)
            for t in range(TT):
                yield

        def qkT_pe(pe):
            pe.wait_ge(N["group_evac"], 4 * TT)
            pe.wait_ge(N["qk_done"], 4)
            for n in range(2 * TT):
                w, t = n // TT, n % TT
                if n >= 4:
                    pe.wait_ge(N["qkT_copied"], QKC[n - 3])
                for h in range(HEADS):
                    last = nc.tensor.transpose(psum[n % 4][:, hc(h)],
                                               (q_tok, k_tok)[w][:, t, hc(h)], ident)
                last.then_inc(N["qkT_mm"], 1)
                if n % 2:
                    yield

        QKC = [0, 1, 2, 3, 4, 6, 7, 8, 9, 10, 11]

        def qkT_dve(dve):
            dve.wait_ge(N["group_step"], 4 * KT)
            V.memset(q_bd[:], 0.0).then_inc(N["qbd_zero"], 1)
            for _ in range(TT):
                yield

        def qkT_act(act):
            act.wait_ge(N["qbd_zero"], 1)
            for n in range(2 * TT):
                w, t = n // TT, n % TT
                act.wait_ge(N["qkT_mm"], n + 1)
                if w == 0 and t == 4:
                    for m in range(MAPS):
                        rows = slice(DK * m, DK * m + DK)
                        nc.scalar.activation(
                            q_bd[rows, :, :, STEP * m:STEP * m + STEP].rearrange(
                                "p b h s -> p h b s"),
                            b4(n % 4)[rows].rearrange("p h (b s) -> p h b s", s=STEP), ACT.Copy)\
                            .then_inc(N["qkT_copied"], 1)
                else:
                    dst = (qT, kTn)[w][:, :, t * P:(t + 1) * P]
                    nc.scalar.activation(dst, b4(n % 4), ACT.Copy).then_inc(N["qkT_copied"], 1)
                if n % 2:
                    yield

        UNITS = [(qt, h) for qt in range(4) for h in range(HEADS)]

        def att_pe(pe):
            def scores(u):
                qt, h = UNITS[u]
                n = P * (qt + 1)
                if u:
                    pe.wait_ge(N["probs"], 2 * u)
                for m in range(MAPS):
                    rows = slice(DK * m, DK * m + DK)
                    nc.tensor.matmul(psum[m][:, 0:n], qT[rows, h, qt * P:(qt + 1) * P],
                                     kTn[rows, h, 0:n], start=True, stop=False,
                                     skip_group_check=True)
                    last = nc.tensor.matmul(psum[m][:, n - 64:n], const("early_neg")[0:1, :],
                                            const("lvl64")[0:1, 64:P], start=False, stop=True,
                                            skip_group_check=True)
                last.then_inc(N["sc_mm"], 1)

            def transposes(u):
                qt, h = UNITS[u]
                pe.wait_ge(N["pcomb"], u + 1)
                if u:
                    pe.wait_ge(N["p_copied"], u)
                for k in range(qt + 1):
                    last = nc.tensor.transpose(psum[2][:, hc(k)], pc[:, hc(k)], ident)
                last.then_inc(N["p_tr"], 1)

            def values(u):
                qt, h = UNITS[u]
                pe.wait_ge(N["p_copied"], u + 1)
                if u:
                    pe.wait_ge(N["pv_copied"], u)
                for k in range(qt + 1):
                    last = nc.tensor.matmul(psum[3][:, 0:P], pT[:, hc(k)], v_tok[:, k, hc(h)],
                                            start=k == 0, stop=k == qt)
                last.then_inc(N["pv_mm"], 1)

            pe.wait_ge(N["qkT_copied"], 11)
            for u in range(len(UNITS) + 1):
                if u < len(UNITS):
                    scores(u)
                if u:
                    transposes(u - 1)
                yield
                if u:
                    values(u - 1)
                yield

        def att_dve(dve):
            for u, (qt, h) in enumerate(UNITS):
                n = P * (qt + 1)
                dve.wait_ge(N["sc_mm"], u + 1)
                c = 4 * u
                both = psum_all[:, 0:2, 0:n]
                link(dve, "att_chain", c + 1, V.tensor_reduce(soft[:, 0:2], both, AX.X, ALU.max))
                V.tensor_scalar(soft[:, 2:4], soft[:, 0:2], -(DK ** -0.5), None, ALU.mult)\
                    .then_inc(N["nmax"], 1)
                yield
                dve.wait_ge(N["probs"], 2 * u + 2)
                link(dve, "att_chain", c + 2, V.reciprocal(soft[:, 6:8], soft[:, 4:6]))
                link(dve, "att_chain", c + 3, V.tensor_tensor(soft[:, 8:9], soft[:, 7:8],
                                                              lam[:, 7:8], ALU.mult))
                link(dve, "att_chain", c + 4, V.tensor_scalar(pr[:, 1, 0:n], pr[:, 1, 0:n],
                                                              soft[:, 8:9], None, ALU.mult))
                if u:
                    dve.wait_ge(N["p_tr"], u)
                V.scalar_tensor_tensor(pc[:, 0:n], pr[:, 0, 0:n], soft[:, 6:7], pr[:, 1, 0:n],
                                       ALU.mult, ALU.add).then_inc(N["pcomb"], 1)
                dve.wait_ge(N["pcomb"], u + 1)
                yield
            yield
            yield

        def att_act(act):
            for u in range(len(UNITS) + 1):
                if u:
                    qt, h = UNITS[u - 1]
                    n = P * (qt + 1)
                    act.wait_ge(N["p_tr"], u)
                    if u > 1:
                        act.wait_ge(N["pv_mm"], u - 1)
                    nc.scalar.activation(pT[:, 0:n], psum[2][:, 0:n], ACT.Copy)\
                        .then_inc(N["p_copied"], 1)
                yield
                if u < len(UNITS):
                    n = P * (UNITS[u][0] + 1)
                    act.wait_ge(N["nmax"], u + 1)
                    if u:
                        act.wait_ge(N["pcomb"], u)
                    for m in range(MAPS):
                        nc.scalar.activation(pr[:, m, 0:n], psum[m][:, 0:n], ACT.Exp,
                                             bias=soft[:, 2 + m:3 + m], scale=DK ** -0.5,
                                             accum_out=soft[:, 4 + m:5 + m])\
                            .then_inc(N["probs"], 1)
                if u:
                    act.wait_ge(N["pv_mm"], u)
                    nc.scalar.activation(q_tok[:, qt, hc(h)], psum[3][:, 0:P], ACT.Copy)\
                        .then_inc(N["pv_copied"], 1)
                yield

        def cache_sync(sp):
            ck = io["cache_k"][0].rearrange("b (k p) h m d -> b p k (h m d)", p=P)
            cv = io["cache_v"][0].rearrange("b (k p) h d -> b p k (h d)", p=P)
            sp.wait_ge(N["group_step"], 4 * KT)
            sp.wait_ge(N["qkT_mm"], 2 * TT)
            sp.wait_ge(N["kv_stored"], 64)
            for b in range(STREAMS):
                if b >= 2:
                    sp.wait_ge(N["kt_mm"], 4 * (b - 1))
                sp.dma_start(K_c[b % 2][:], ck[b]).then_inc(s_K[b % 2], 16)
                if b >= 2:
                    sp.wait_ge(N["spv_mm"], b - 1)
                elif b == 1:
                    sp.wait_ge(N["pv_mm"], len(UNITS))
                sp.dma_start(V_c[b % 2][:], cv[b]).then_inc(s_V[b % 2], 16)
                sp.dma_start(V_n[b % 2][:], v_tok[STEP * b:STEP * b + STEP, 4, :])\
                    .then_inc(s_V[b % 2], 16)

        def cache_pe(pe):
            def keys(b, heads):
                pe.wait_ge(s_K[b % 2], 16 * (b // 2 + 1))
                for h in heads:
                    n = 4 * b + h
                    if n >= 2:
                        pe.wait_ge(N["kt_copied"], n - 1)
                    for k in range(4):
                        last = nc.tensor.transpose(psum[2 + n % 2][:, hc(k)], K_c[b % 2][:, k, hc(h)],
                                                   ident)
                    last.then_inc(N["kt_mm"], 1)

            def scores(b):
                pe.wait_ge(N["kt_copied"], 4 * b + 4)
                if b:
                    pe.wait_ge(N["sp_copied"], 2 * b)
                for h in range(HEADS):
                    rows = slice(32 * h, 32 * h + 32)
                    nc.tensor.matmul(psum[0][rows, :], q_bd[:, b, h, :], KTc[:, h, :], start=True,
                                     stop=True, tile_position=(0, 32 * h))
                    last = nc.tensor.matmul(psum[1][rows, 0:STEP], q_bd[:, b, h, :],
                                            kTn[:, h, PROMPT + STEP * b:PROMPT + STEP * b + STEP],
                                            start=True, stop=True, tile_position=(0, 32 * h))
                last.then_inc(N["ssc_mm"], 1)

            def turn(b):
                pe.wait_ge(N["s_comb"], b + 1)
                for k in range(4):
                    nc.tensor.matmul(psum[0][:, hc(k)], ps[:, hc(k)], Cm[:], start=True, stop=True)
                nc.tensor.matmul(psum[1][0:STEP, 0:P], ps[:, PAST:PAST + STEP], Cm[:], start=True,
                                 stop=True).then_inc(N["sp_mm"], 1)

            def values(b):
                pe.wait_ge(N["sp_copied"], 2 * b + 2)
                pe.wait_ge(s_V[b % 2], 32 * (b // 2 + 1))
                for k in range(5):
                    for h in range(HEADS):
                        out = psum[4][32 * h:32 * h + 32, hc(b // 2)]
                        if k < 4:
                            nc.tensor.matmul(out, pT[:, P * k + 32 * h:P * k + 32 * h + 32],
                                             V_c[b % 2][:, k, hc(h)], start=b == 0 and k == 0,
                                             stop=False, skip_group_check=True,
                                             tile_position=(0, 32 * h))
                        else:
                            last = nc.tensor.matmul(out, pTn[:, 32 * h:32 * h + 32],
                                                    V_n[b % 2][:, hc(h)], start=False, stop=True,
                                                    skip_group_check=True,
                                                    tile_position=(0, 32 * h))
                last.then_inc(N["spv_mm"], 1)

            pe.wait_ge(N["pv_copied"], 16)
            keys(0, (0, 1))
            yield
            keys(0, (2, 3))
            yield
            scores(0)
            yield
            yield
            for b in range(STREAMS):
                if b + 1 < STREAMS:
                    keys(b + 1, (0, 1))
                yield
                turn(b)
                yield
                if b + 1 < STREAMS:
                    keys(b + 1, (2, 3))
                yield
                if b + 1 < STREAMS:
                    scores(b + 1)
                yield
                values(b)
                yield

        def cache_act(act):
            def key(b, h):
                act.wait_ge(N["kt_mm"], 4 * b + h + 1)
                if h == 0 and b:
                    act.wait_ge(N["ssc_mm"], b)
                act.wait_ge(N["kt_copied"], 4 * b + h)
                nc.scalar.activation(KTc[:, h, :], psum[2 + h % 2], ACT.Copy)\
                    .then_inc(N["kt_copied"], 1)

            def probs(b):
                act.wait_ge(N["s_nmax"], b + 1)
                if b:
                    act.wait_ge(N["sp_mm"], b)
                nc.scalar.activation(ps[:], psum_flat[:, 0:PAST + STEP], ACT.Exp, bias=soft[:, 10:11],
                                     scale=DK ** -0.5, accum_out=soft[:, 11:12])\
                    .then_inc(N["s_probs"], 1)

            key(0, 0)
            yield
            key(0, 2)
            yield
            yield
            probs(0)
            yield
            for b in range(STREAMS):
                if b + 1 < STREAMS:
                    key(b + 1, 0)
                yield
                act.wait_ge(N["sp_mm"], b + 1)
                if b:
                    act.wait_ge(N["spv_mm"], b)
                nc.scalar.activation(pT[:], psum[0], ACT.Copy).then_inc(N["sp_copied"], 1)
                nc.scalar.activation(pTn[:], psum[1][0:STEP, 0:P], ACT.Copy)\
                    .then_inc(N["sp_copied"], 1)
                yield
                if b + 1 < STREAMS:
                    key(b + 1, 2)
                yield
                yield
                if b + 1 < STREAMS:
                    probs(b + 1)
                yield
            act.wait_ge(N["spv_mm"], STREAMS)
            nc.scalar.activation(q_tok[:, 4, :], psum[4], ACT.Copy).then_inc(N["pv_copied"], 1)

        def cache_dve(dve):
            def key(b, h):
                dve.wait_ge(N["kt_mm"], 4 * b + h + 1)
                if b:
                    dve.wait_ge(N["ssc_mm"], b)
                dve.wait_ge(N["kt_copied"], 4 * b + h)
                V.tensor_copy(KTc[:, h, :], psum[2 + h % 2]).then_inc(N["kt_copied"], 1)

            c = 4 * len(UNITS)

            def maximum(b):
                dve.wait_ge(N["ssc_mm"], b + 1)
                link(dve, "att_chain", c + 3 * b + 1,
                     V.tensor_reduce(soft[:, 9:10], psum_flat[:, 0:PAST + STEP], AX.X, ALU.max))
                V.tensor_scalar(soft[:, 10:11], soft[:, 9:10], -(DK ** -0.5), None, ALU.mult)\
                    .then_inc(N["s_nmax"], 1)

            def combine(b):
                dve.wait_ge(N["s_probs"], b + 1)
                link(dve, "att_chain", c + 3 * b + 2, V.reciprocal(soft[:, 12:13], soft[:, 11:12]))
                link(dve, "att_chain", c + 3 * b + 3,
                     V.tensor_tensor(soft[:, 13:14], soft[:, 12:13], lam[:, 6:7], ALU.mult))
                V.tensor_scalar(Cm[:], const(f"sel{b % 2}"), soft[:, 13:14], None, ALU.mult)\
                    .then_inc(N["s_comb"], 1)

            key(0, 1)
            yield
            key(0, 3)
            yield
            maximum(0)
            yield
            combine(0)
            yield
            for b in range(STREAMS):
                if b + 1 < STREAMS:
                    key(b + 1, 1)
                yield
                yield
                if b + 1 < STREAMS:
                    key(b + 1, 3)
                yield
                if b + 1 < STREAMS:
                    maximum(b + 1)
                yield
                if b + 1 < STREAMS:
                    combine(b + 1)
                yield

        OUT_TILES = [range(0, 4), range(4, 5)]

        def diff_out_act(act, part):
            tiles = OUT_TILES[part]
            a, b = tiles[0], tiles[-1] + 1
            act.wait_ge(N["pv_copied"], (16, 17)[part])
            for t in tiles:
                nc.scalar.activation((od_sq, od_sq4)[part][:, t - a, :], q_tok[:, t, :],
                                     ACT.Square)\
                    .then_inc(N["od_act"], 1)
            yield
            act.wait_ge(N["od_chain"], (3, 4 + 3)[part])
            nc.scalar.activation(gates[:, G_SSQ, a:b], gates[:, G_SSK, a:b], ACT.Sqrt)\
                .then_inc(N["od_act"], 1)
            for t in tiles:
                yield

        def diff_out_dve(dve, part):
            tiles = OUT_TILES[part]
            a, b = tiles[0], tiles[-1] + 1
            n = (0, 4)[part]
            g = lambda i: gates[:, i, a:b]
            dve.wait_ge(N["od_act"], (4, 6)[part])
            link(dve, "od_chain", n + 1, V.tensor_reduce(
                g(G_RQ).rearrange("p t h -> p (t h)"),
                (od_sq, od_sq4)[part][:].rearrange("p t (h d) -> p (t h) d", d=P), AX.X, ALU.add))
            link(dve, "od_chain", n + 2, V.tensor_scalar(g(G_RK), g(G_RQ), 1.0 / P, EPS, ALU.mult,
                                                         ALU.add))
            V.reciprocal(g(G_SSK), g(G_RK)).then_inc(N["od_chain"], 1)
            yield
            dve.wait_ge(N["od_act"], (5, 7)[part])
            link(dve, "od_chain", n + 4, V.tensor_scalar(g(G_E), g(G_SSQ), 1.0 - LAM_INIT, None,
                                                         ALU.mult))
            for t in tiles:
                for h in range(HEADS):
                    V.scalar_tensor_tensor(q_tok[:, t, hc(h)], q_tok[:, t, hc(h)],
                                           gates[:, G_E, t, h:h + 1], diff_gain[:], ALU.mult,
                                           ALU.mult).then_inc(N["od_done"], 1)
                yield

        def wout_pool(pool):
            pool.wait_ge(N["og_done"], TT * HEADS)
            pool.wait_ge(N["spv_mm"], STREAMS - 2)
            pool.wait_ge(N["S_stored"], 16)
            for stored in s_ss_out:
                pool.wait_ge(stored, 32)
            pool.dma_start(raw_o[0][:], w_out[:, :, 0:BANK]).then_inc(s_wo[0], 16)
            pool.wait_ge(s_wo[0], 16)
            pool.dma_start(x_tok[:, 0:4, :], x_mid[0:PROMPT, :].rearrange("(t p) c -> p t c", p=P))\
                .then_inc(N["x_back"], 16)
            pool.dma_start(x_tok[:, 4, :], x_mid[PROMPT:TOK, :]).then_inc(N["x_back"], 16)

        def wout_sync(sp):
            sp.wait_ge(N["kt_mm"], 4 * STREAMS)
            sp.wait_ge(N["spv_mm"], STREAMS)
            sp.dma_start(raw_o[1][:], w_out[:, :, BANK:D]).then_inc(s_wo[1], 16)
            sp.wait_ge(N["od_done"], TT * HEADS)
            sp.wait_ge(N["og_done"], TT * HEADS)
            sp.dma_start(gain[:], io["ffn2_norm"].to_broadcast([P, D])).then_inc(s_gain[2], 16)

        BEHIND = {0: range(TT, TT + 3), 1: range(TT + 3, 2 * TT)}

        def out_bank(n):
            return n if n < TT else TT + (n - TT) % 3

        def out_hT(which, n):
            half, t = n // TT, n % TT
            part = which[:, 4 * half:4 * half + 4, t * P:(t + 1) * P]
            return part if n < 2 * TT - 1 else part.rearrange("p h (b c) -> p h b c", c=32)

        def out_psum(n):
            if n < 2 * TT - 1:
                return b4(out_bank(n))
            return psum[out_bank(n)].rearrange("p (b h c) -> p h b c", h=HEADS, c=32)

        def out_pe(pe, n):
            half, t = n // TT, n % TT
            pe.wait_ge(N["od_done" if half else "og_done"], HEADS * (t + 1))
            if n == TT - 1:
                pe.wait_ge(N["pv_copied"], 17)
            if n >= TT + 3:
                pe.wait_ge(*on.lo(n - 2))
            for k in range(4):
                last = nc.tensor.transpose(psum[out_bank(n)][:, hc(k)],
                                           (z, q_tok)[half][:, t, hc(k)], ident)
            last.then_inc(on.tr.sem, 1)

        def out_act(act, n):
            act.wait_ge(*on.tr(n + 1))
            nc.scalar.activation(out_hT(hT_hi, n), out_psum(n), ACT.Copy).then_inc(on.hi.sem, 1)

        def out_dve(dve, n):
            dve.wait_ge(*on.hi(n + 1))
            V.tensor_tensor(out_hT(hT_lo, n), out_psum(n), out_hT(raw(hT_hi), n),
                            ALU.subtract).then_inc(on.lo.sem, 1)

        def wout_act(act):
            for n in range(TT):
                out_act(act, n)
            for n in range(2 * KT):
                half, k = n // KT, n % KT
                if n == 2:
                    finish(diff_out_act(act, 1))
                for m in BEHIND.get(n - 2, ()):
                    out_act(act, m)
                act.wait_ge(s_wo[half], 16)
                if n >= 2:
                    act.wait_ge(N["wo_step"], n - 1)
                nc.scalar.activation(o_hi[:, n % 2], raw_o[half][:, k, :], ACT.Copy)\
                    .then_inc(N["wo_hi"], 1)

        def wout_dve(dve):
            for n in range(TT):
                out_dve(dve, n)
            for n in range(2 * KT):
                half, k = n // KT, n % KT
                if n == 2:
                    finish(diff_out_dve(dve, 1))
                for m in BEHIND.get(n - 2, ()):
                    out_dve(dve, m)
                dve.wait_ge(N["wo_hi"], n + 1)
                V.tensor_tensor(o_lo[:, n % 2], raw_o[half][:, k, :], raw(o_hi[:, n % 2]),
                                ALU.subtract).then_inc(N["wo_lo"], 1)
                if n == KT + 1:
                    dve.wait_ge(N["x_back"], 32)
                    for t in range(TT):
                        wout_residual(dve, 0, t)

        def wout_residual(dve, half, t):
            if half == 0:
                dve.wait_ge(N["wo_step"], KT)
            else:
                dve.wait_ge(N["wo_out"], t + 1)
            cols = x_tok[:, t, half * BANK:(half + 1) * BANK]
            V.tensor_tensor(cols, psum[(half * TT + t) % 8], cols, ALU.add).then_inc(N["wo_res"], 1)

        def wout_pe(pe):
            for n in range(TT):
                out_pe(pe, n)
            for n in range(2 * KT):
                half, k = n // KT, n % KT
                if n == 0:
                    pe.wait_ge(*on.lo(TT))
                elif n == KT // 2:
                    pe.wait_ge(*on.lo(2 * TT))
                pe.wait_ge(N["wo_lo"], n + 1)
                for t in range(TT):
                    c = slice(t * P, (t + 1) * P)
                    if k == 0 and half == 1 and (TT + t) % 8 < TT:
                        pe.wait_ge(N["wo_res"], (TT + t) % 8 + 1)
                    last = three(psum[(half * TT + t) % 8], hT_hi[:, k, c], hT_lo[:, k, c],
                                 o_hi[:, n % 2], o_lo[:, n % 2], k == 0, k == KT - 1)
                    if n == 2 * KT - 1:
                        last.then_inc(N["wo_out"], 1)
                if n < 2 * KT - 1:
                    last.then_inc(N["wo_step"], 1)
                for m in BEHIND.get(n, ()):
                    out_pe(pe, m)

        s_wo = [sem(f"w_out_loaded{i}") for i in range(2)]
        psum_flat = psum_all[:].rearrange("p b c -> p (b c)")
        gls = small.put("stream_decay", [P, HEADS, STREAMS])

        def nothing(eng, part=0):
            return iter(())

        def attention_steps(eng, groups, heads, prompt, cache):
            yield from groups(eng)
            yield from heads(eng)
            yield from prompt(eng)
            yield from cache(eng)

        def delta_steps(eng, tokens, gates, tile, state, streams, out, diff_out):
            yield from tokens(eng)
            yield from gates(eng)
            for t in range(TT):
                yield from tile(eng, t)
                if t < 4:
                    yield from state(eng, t)
            yield from streams(eng)
            yield from out(eng)
            yield from diff_out(eng, 0)

        def by_turns(attention, delta):
            for _ in attention:
                next(delta, None)
            next(delta, None)
            finish(delta)

        def finish(steps):
            while next(steps, "end") is None:
                continue

        block = ctx.enter_context(nc.Block())

        @block.sync
        def _(sp):
            x_in = io["x_prompt"][0].rearrange("(t p) c -> p t c", p=P)
            rest = slice(P, CONST_COLS)
            sp.dma_start(x_tok[:, 0, :], x_in[:, 0, :]).then_inc(s_x[0], 16)
            sp.dma_start(ident, io["consts"][:, 0:P]).then_inc(s_ident, 16)
            sp.dma_start(x_tok[:, 1:3, :], x_in[:, 1:3, :]).then_inc(s_x[1], 16)
            sp.dma_start(gain[:], io["ffn1_norm"].to_broadcast([P, D])).then_inc(s_gain[0], 16)
            sp.dma_start(x_tok[:, 3, :], x_in[:, 3, :]).then_inc(s_x[2], 16)
            sp.dma_start(x_tok[:, 4, :], io["x_sample"].rearrange("b s c -> (b s) c"))\
                .then_inc(s_x[3], 16)
            ffn_sync(sp, f1, io["ffn1_w_gu"][0], io["ffn1_w_down"][0],
                     first=lambda: sp.dma_start(consts[:, rest], io["consts"][:, rest])
                     .then_inc(s_const, 16))
            sp.wait_ge(*f1.mm(2 * FT))
            sp.dma_start(gain[:], io["mix_norm"].to_broadcast([P, D])).then_inc(s_gain[1], 16)
            conv_sync(sp)
            cache_sync(sp)
            wout_sync(sp)
            ffn_sync(sp, f2, io["ffn2_w_gu"][0], io["ffn2_w_down"][0], N["wo_res"])
            for half in range(2):
                cols = slice(half * BANK, (half + 1) * BANK)
                for t in range(TT):
                    sp.wait_ge(*f2.res(half * TT + t + 1))
                    y = io["y_prompt"][0][t * P:(t + 1) * P, cols] if t < 4 else \
                        io["y_sample"].rearrange("b s c -> (b s) c")[:, cols]
                    sp.dma_start(y, x_tok[:, t, cols]).then_inc(s_y, 16)
            sp.wait_ge(s_y, 16 * 2 * TT)

        @block.gpsimd
        def _(pool):
            pool.wait_ge(s_const, 16)
            pool.wait_ge(N["tail_rows"], 3)
            pool.dma_start(io["conv_prompt"][0, 0], conv_out[0:3, :]).then_inc(N["tail_stored"], 16)
            pool.dma_start(io["conv_sample"][0].rearrange("b w c -> (b w) c"), conv_out[3:27, :])\
                .then_inc(N["tail_stored"], 16)
            pool.wait_ge(N["x_spilled"], 32)
            for t in range(TT):
                gdn_pool(pool, t)
                if t == 3:
                    pool.wait_ge(N["group_evac"], 4 * TT)
                    for i in range(TT):
                        zt = z[:, i, :].rearrange("p (h d) -> p h d", d=P)
                        nc.gpsimd.tensor_tensor(zt, zt, over(gdn_gain[:], HEADS), ALU.mult)\
                            .then_inc(N["z_gained"], 1)
                if t == 3:
                    pool.wait_ge(N["S_ready"], 17)
                    pool.dma_start(io["gdn_prompt"][0, 0].rearrange("h k v -> k h v"), S_p[:])\
                        .then_inc(N["S_stored"], 16)
            streams_pool(pool)
            wout_pool(pool)
            pool.wait_ge(N["tail_stored"], 32)

        @block.scalar
        def _(act):
            norm_act(act, f1.n, lambda e, t: e.wait_ge(s_x[(0, 1, 1, 2, 3)[t]], 16),
                     lambda e: gu_split_act(e, f1, 0, 0))
            ffn_act(act, f1)
            norm_act(act, mn, lambda e, t: e.wait_ge(*f1.res(6 + t)),
                     lambda e: conv_split_act(e, 0, 0))
            conv_act(act)
            by_turns(attention_steps(act, group_act, qkT_act, att_act, cache_act),
                     delta_steps(act, tok_act, gate_act, gdn_act, nothing, streams_act,
                                 gdn_out_act, diff_out_act))
            wout_act(act)
            gu_split_act(act, f2, 0, 0)
            norm_act(act, f2.n, lambda e, t: e.wait_ge(N["wo_res"], 6 + t))
            ffn_act(act, f2)

        @block.vector
        def _(dve):
            norm_dve(dve, f1.n, s_gain[0], ahead=lambda e: gu_split_dve(e, f1, 0, 0))
            ffn_dve(dve, f1, finish=False)
            dve.wait_ge(s_const, 16)
            norm_dve(dve, mn, s_gain[1], lambda t: residual(dve, f1, 1, t),
                     lambda e: conv_split_dve(e, 0, 0))
            dve.wait_ge(*mn.lo(2 * TT))
            conv_dve(dve)
            by_turns(attention_steps(dve, group_dve, qkT_dve, att_dve, cache_dve),
                     delta_steps(dve, tok_dve, gate_dve, gdn_dve, gdn_state_dve, streams_dve,
                                 gdn_out_dve, diff_out_dve))
            wout_dve(dve)
            gu_split_dve(dve, f2, 0, 0)
            norm_dve(dve, f2.n, s_gain[2], lambda t: wout_residual(dve, 1, t))
            ffn_dve(dve, f2)

        @block.tensor
        def _(pe):
            pe.wait_ge(s_ident, 16)
            norm_pe(pe, f1.n, range(3))
            ffn_pe(pe, f1)
            pe.wait_ge(s_const, 16)
            norm_pe(pe, mn, range(3))
            conv_pe(pe)
            by_turns(attention_steps(pe, group_pe, qkT_pe, att_pe, cache_pe),
                     delta_steps(pe, tok_pe, gate_pe, gdn_pe, gdn_state_pe, streams_pe,
                                 nothing, nothing))
            wout_pe(pe)
            norm_pe(pe, f2.n, range(3))
            ffn_pe(pe, f2)


INPUTS = """x_prompt x_sample cache_k cache_v state_gdn state_conv ffn1_norm ffn1_w_gu ffn1_w_down
    mix_norm w_in conv_w a_log dt_bias gdn_out_norm q_norm k_norm lambda_q lambda_k diff_out_norm
    w_out ffn2_norm ffn2_w_gu ffn2_w_down""".split()
OUTPUTS = {
    "y_prompt": (1, PROMPT, D), "y_sample": (STREAMS, STEP, D),
    "k_prompt": (1, 1, PROMPT, HEADS, MAPS, DK), "v_prompt": (1, 1, PROMPT, HEADS, P),
    "gdn_prompt": (1, 1, HEADS, P, P), "conv_prompt": (1, 1, 3, CONV_T * P),
    "k_sample": (1, STREAMS, STEP, HEADS, MAPS, DK), "v_sample": (1, STREAMS, STEP, HEADS, P),
    "gdn_sample": (1, STREAMS, HEADS, P, P), "conv_sample": (1, STREAMS, 3, CONV_T * P),
}


def kernel(**inputs):
    from concourse import bacc
    from concourse.bass_utils import run_bass_kernel_spmd

    nc = bacc.Bacc("TRN2", target_bir_lowering=False, num_devices=1)
    arrays, io = {}, {}
    consts, rotary = constants()
    for name, a in [(n, inputs[n]) for n in INPUTS] + [("consts", consts), ("rotary", rotary)]:
        a = np.ascontiguousarray(a)
        arrays[name] = a
        io[name] = nc.dram_tensor(name, a.shape, mybir.dt.from_np(a.dtype), kind="ExternalInput").ap()
    for name, shape in OUTPUTS.items():
        io[name] = nc.dram_tensor(name, shape, F32, kind="ExternalOutput").ap()
    build(nc, io)
    r = run_bass_kernel_spmd(nc, [arrays], core_ids=[0])
    return tuple(r.results[0][name] for name in OUTPUTS)
```
